# Optimizing a Trainium2 kernel written in Bass

```python
import math
import jax
import jax.numpy as jnp
from jax import lax
import numpy as np

D_MODEL = 2048
BATCH = 1
SEQ = 512
DEPTH = 1

HEAD_DIM = 128
DN_HEADS = 6
DIL_HEADS = 4
NSA_HEADS = 6
DN_WIDTH = DN_HEADS * HEAD_DIM
DIL_WIDTH = DIL_HEADS * HEAD_DIM
NSA_WIDTH = NSA_HEADS * HEAD_DIM
MIX_WIDTH = DN_WIDTH + DIL_WIDTH + NSA_WIDTH
DN_CONV = 4
DN_CHUNK = 64
DT_MIN = 1e-3
DT_MAX = 1e-1
DIL_PATTERNS = ((128, 1), (512, 4), (2048, 16))
NSA_KV_GROUPS = 2
NSA_Q_PER_KV = NSA_HEADS // NSA_KV_GROUPS
CMP_LEN = 32
CMP_STRIDE = 16
CMP_HIDDEN = 256
SLC_BLOCK = 64
SLC_TOPK = 16
SLC_LOCAL = 2
SLC_Q_BLOCK = 32
WIN = 512
NSA_KV_COLS = 3 * 2 * NSA_KV_GROUPS * HEAD_DIM
NSA_GATE_COLS = 3 * NSA_HEADS
IN_COLS = 3 * DN_WIDTH + DN_WIDTH + 2 * DN_HEADS + 3 * DIL_WIDTH + NSA_WIDTH + NSA_KV_COLS + NSA_GATE_COLS
REL_BUCKETS = 32
REL_MAX_DIST = 2048
N_BIAS_HEADS = DIL_HEADS + NSA_HEADS
D_FF = 5632
FFN_CONV = 3
Q_BLOCK = 128
EPS = 1e-6
NEG = -1e30

kernel_name = 'hybrid_deltanet_dilated_nsa_convffn'

def rmsnorm(x, g):
    xf = x.astype(jnp.float32)
    y = xf * lax.rsqrt(jnp.mean(xf * xf, axis=-1, keepdims=True) + EPS)
    return (y * g.astype(jnp.float32)).astype(x.dtype)

def l2norm(x):
    return x * lax.rsqrt(jnp.sum(x * x, axis=-1, keepdims=True) + EPS)

def causal_dwconv(x, w):
    k_w, c = w.shape
    return lax.conv_general_dilated(x, w[:, None, :].astype(x.dtype), window_strides=(1,),
                                    padding=[(k_w - 1, 0)], dimension_numbers=('NWC', 'WIO', 'NWC'),
                                    feature_group_count=c)

def rel_bucket(dist):
    max_exact = REL_BUCKETS // 2
    n = jnp.maximum(dist, 0)
    nf = jnp.maximum(n, 1).astype(jnp.float32)
    large = max_exact + (jnp.log(nf / max_exact) / math.log(REL_MAX_DIST / max_exact)
                         * (REL_BUCKETS - max_exact)).astype(jnp.int32)
    large = jnp.minimum(large, REL_BUCKETS - 1)
    return jnp.where(n < max_exact, n, large)

def masked_softmax(logits, mask):
    logits = jnp.where(mask, logits.astype(jnp.float32), NEG)
    m = jnp.max(logits, axis=-1, keepdims=True)
    p = jnp.exp(logits - m) * mask
    return p / jnp.maximum(jnp.sum(p, axis=-1, keepdims=True), 1e-30)

def split_cols(proj):
    sizes = (3 * DN_WIDTH, DN_WIDTH, DN_HEADS, DN_HEADS, 3 * DIL_WIDTH, NSA_WIDTH, NSA_KV_COLS, NSA_GATE_COLS)
    points = []
    acc = 0
    for s in sizes[:-1]:
        acc += s
        points.append(acc)
    return jnp.split(proj, points, axis=-1)

def chunk_gated_delta_rule(q, k, v, beta, g):
    B, H, S, dk = q.shape
    dv = v.shape[-1]
    C = DN_CHUNK
    N = S // C

    def to_chunks(t):
        return t.reshape((B, H, N, C) + t.shape[3:])

    q, k, v, beta, g = (to_chunks(t) for t in (q, k, v, beta, g))
    g = jnp.cumsum(g, axis=-1)
    k_beta = k * beta[..., None]
    v_beta = v * beta[..., None]
    causal = jnp.tril(jnp.ones((C, C), dtype=bool))
    decay = jnp.exp(jnp.where(causal, g[..., :, None] - g[..., None, :], -jnp.inf))
    eye = jnp.eye(C, dtype=q.dtype)
    a_mat = jnp.einsum('bhnid,bhnjd->bhnij', k_beta, k) * decay * (1.0 - eye)
    t_mat = lax.linalg.triangular_solve(eye + a_mat, jnp.broadcast_to(eye, a_mat.shape),
                                        left_side=True, lower=True, unit_diagonal=True)
    u = jnp.einsum('bhnij,bhnjd->bhnid', t_mat, v_beta)
    w = jnp.einsum('bhnij,bhnjd->bhnid', t_mat, k_beta * jnp.exp(g)[..., None])
    attn = jnp.einsum('bhnid,bhnjd->bhnij', q, k) * decay

    def step(state, xs):
        q_c, k_c, u_c, w_c, g_c, attn_c = xs
        v_new = u_c - jnp.einsum('bhck,bhkv->bhcv', w_c, state)
        o_c = (jnp.einsum('bhck,bhkv->bhcv', q_c * jnp.exp(g_c)[..., None], state)
               + jnp.einsum('bhij,bhjv->bhiv', attn_c, v_new))
        g_last = g_c[..., -1:]
        state = (state * jnp.exp(g_last)[..., None]
                 + jnp.einsum('bhck,bhcv->bhkv', k_c * jnp.exp(g_last - g_c)[..., None], v_new))
        return state, o_c

    xs = tuple(jnp.moveaxis(t, 2, 0) for t in (q, k, u, w, g, attn))
    state0 = jnp.zeros((B, H, dk, dv), q.dtype)
    _, o = lax.scan(step, state0, xs)
    return jnp.moveaxis(o, 0, 2).reshape(B, H, S, dv)

def gated_deltanet(qkv, z, b, a, conv_w, a_log, dt_bias, norm_g):
    B, S, _ = qkv.shape
    H, hd = DN_HEADS, HEAD_DIM
    f32 = jnp.float32
    qkv = jax.nn.silu(causal_dwconv(qkv, conv_w)).astype(f32)
    qkv = qkv.reshape(B, S, 3, H, hd).transpose(2, 0, 3, 1, 4)
    q = l2norm(qkv[0]) * hd ** -0.5
    k = l2norm(qkv[1])
    v = qkv[2]
    beta = jax.nn.sigmoid(b.astype(f32)).transpose(0, 2, 1)
    g = (-jnp.exp(a_log.astype(f32)) * jax.nn.softplus(a.astype(f32) + dt_bias.astype(f32))).transpose(0, 2, 1)
    o = chunk_gated_delta_rule(q, k, v, beta, g).transpose(0, 2, 1, 3)
    o = rmsnorm(o, norm_g) * jax.nn.silu(z.astype(f32).reshape(B, S, H, hd))
    return o.reshape(B, S, H * hd)

def dilated_attention(qkv, bias_tab):
    B, S, _ = qkv.shape
    H, hd = DIL_HEADS, HEAD_DIM
    f32 = jnp.float32
    qkv = qkv.astype(f32).reshape(B, S, 3, H, hd).transpose(2, 0, 3, 1, 4)
    q, k, v = qkv[0] * hd ** -0.5, qkv[1], qkv[2]
    tab = bias_tab.astype(f32)

    def block(bi):
        t = bi * Q_BLOCK + jnp.arange(Q_BLOCK)
        qb = lax.dynamic_slice_in_dim(q, bi * Q_BLOCK, Q_BLOCK, axis=2)
        outs, maxs, dens = [], [], []
        for window, dil in DIL_PATTERNS:
            j = jnp.arange(window // dil + 1)
            idx = t[:, None] - dil * j[None, :]
            valid = idx >= 0
            idx = jnp.maximum(idx, 0)
            kg = jnp.take(k, idx, axis=2)
            vg = jnp.take(v, idx, axis=2)
            logits = (jnp.einsum('bhqd,bhqjd->bhqj', qb, kg)
                      + tab[:, rel_bucket(dil * j)][None, :, None, :])
            logits = jnp.where(valid, logits, NEG)
            m = jnp.max(logits, axis=-1, keepdims=True)
            p = jnp.exp(logits - m) * valid
            den = jnp.sum(p, axis=-1, keepdims=True)
            outs.append(jnp.einsum('bhqj,bhqjd->bhqd', p, vg) / den)
            maxs.append(m)
            dens.append(den)
        m_all = maxs[0]
        for m_ in maxs[1:]:
            m_all = jnp.maximum(m_all, m_)
        wts = [d_ * jnp.exp(m_ - m_all) for d_, m_ in zip(dens, maxs)]
        num = wts[0] * outs[0]
        den_all = wts[0]
        for w_, o_ in zip(wts[1:], outs[1:]):
            num = num + w_ * o_
            den_all = den_all + w_
        return num / den_all

    o = lax.map(block, jnp.arange(S // Q_BLOCK))
    return o.transpose(1, 0, 3, 2, 4).reshape(B, S, H * hd)

def nsa_attention(q, kv, gate_logits, bias_tab, cmp_pos, cmp_w1, cmp_w2):
    B, S, _ = q.shape
    G, R, hd = NSA_KV_GROUPS, NSA_Q_PER_KV, HEAD_DIM
    f32 = jnp.float32
    qg = q.astype(f32).reshape(B, S, G, R, hd).transpose(0, 2, 3, 1, 4) * hd ** -0.5
    kv = kv.astype(f32).reshape(B, S, 3, 2, G, hd).transpose(2, 3, 0, 4, 1, 5)
    t = jnp.arange(S)
    tab = bias_tab.astype(f32)
    head_bias = tab.reshape(G, R, REL_BUCKETS)

    n_cmp = (S - CMP_LEN) // CMP_STRIDE + 1
    c_start = CMP_STRIDE * jnp.arange(n_cmp)
    blk_idx = c_start[:, None] + jnp.arange(CMP_LEN)[None, :]

    def compress(xs, i):
        blocks = jnp.take(xs, blk_idx, axis=2) + cmp_pos[i].astype(f32)
        hmid = jax.nn.gelu(jnp.einsum('bgcf,fh->bgch', blocks.reshape(B, G, n_cmp, CMP_LEN * hd),
                                      cmp_w1[i].astype(f32)))
        return jnp.einsum('bgch,hd->bgcd', hmid, cmp_w2[i].astype(f32))

    k_cmp = compress(kv[0, 0], 0)
    v_cmp = compress(kv[0, 1], 1)
    c_end = c_start + CMP_LEN - 1
    c_mask = c_end[None, :] <= t[:, None]
    c_bias = head_bias[:, :, rel_bucket(t[:, None] - c_end[None, :])]
    c_logits = jnp.einsum('bgrsd,bgcd->bgrsc', qg, k_cmp) + c_bias
    p_cmp = masked_softmax(c_logits, c_mask)
    o_cmp = jnp.einsum('bgrsc,bgcd->bgrsd', p_cmp, v_cmp)

    n_slc = S // SLC_BLOCK
    s_start = SLC_BLOCK * jnp.arange(n_slc)
    overlap = jnp.clip(jnp.minimum(c_start[:, None] + CMP_LEN, s_start[None, :] + SLC_BLOCK)
                       - jnp.maximum(c_start[:, None], s_start[None, :]), 0).astype(f32) / CMP_STRIDE
    imp = jnp.einsum('bgrsc,cj->bgsj', p_cmp, overlap)
    cur = t // SLC_BLOCK
    jb = jnp.arange(n_slc)
    forced = (jb[None, :] == 0) | ((jb[None, :] <= cur[:, None]) & (jb[None, :] > cur[:, None] - SLC_LOCAL))
    allowed = jb[None, :] <= cur[:, None]
    imp = jnp.where(forced, jnp.inf, jnp.where(allowed, imp, -jnp.inf))
    n_top = min(SLC_TOPK, n_slc)
    _, sel = lax.top_k(imp, n_top)
    sel_ok = sel <= cur[None, None, :, None]

    k_slc = kv[1, 0].reshape(B, G, n_slc, SLC_BLOCK, hd)
    v_slc = kv[1, 1].reshape(B, G, n_slc, SLC_BLOCK, hd)
    b_ix = jnp.arange(B)[:, None, None, None]
    g_ix = jnp.arange(G)[None, :, None, None]
    flat_bias = tab.reshape(-1)
    head_off = (jnp.arange(G)[:, None] * R + jnp.arange(R)[None, :])[None, :, :, None, None] * REL_BUCKETS
    in_blk = jnp.arange(SLC_BLOCK)

    def slc_step(bi):
        t0 = bi * SLC_Q_BLOCK
        tq = t0 + jnp.arange(SLC_Q_BLOCK)
        qb = lax.dynamic_slice_in_dim(qg, t0, SLC_Q_BLOCK, axis=3)
        sb = lax.dynamic_slice_in_dim(sel, t0, SLC_Q_BLOCK, axis=2)
        ok = lax.dynamic_slice_in_dim(sel_ok, t0, SLC_Q_BLOCK, axis=2)
        kg = k_slc[b_ix, g_ix, sb].reshape(B, G, SLC_Q_BLOCK, n_top * SLC_BLOCK, hd)
        vg = v_slc[b_ix, g_ix, sb].reshape(B, G, SLC_Q_BLOCK, n_top * SLC_BLOCK, hd)
        pos5 = sb[..., None] * SLC_BLOCK + in_blk
        mask5 = ok[..., None] & (pos5 <= tq[None, None, :, None, None])
        pos = pos5.reshape(B, G, SLC_Q_BLOCK, n_top * SLC_BLOCK)
        mask = mask5.reshape(B, G, SLC_Q_BLOCK, n_top * SLC_BLOCK)
        bias = flat_bias[head_off + rel_bucket(tq[None, None, :, None] - pos)[:, :, None]]
        logits = jnp.einsum('bgrqd,bgqkd->bgrqk', qb, kg) + bias
        p = masked_softmax(logits, mask[:, :, None])
        return jnp.einsum('bgrqk,bgqkd->bgrqd', p, vg)

    o_slc = lax.map(slc_step, jnp.arange(S // SLC_Q_BLOCK))
    o_slc = o_slc.transpose(1, 2, 3, 0, 4, 5).reshape(B, G, R, S, hd)

    k_win = jnp.pad(kv[2, 0], ((0, 0), (0, 0), (WIN, 0), (0, 0)))
    v_win = jnp.pad(kv[2, 1], ((0, 0), (0, 0), (WIN, 0), (0, 0)))
    span = Q_BLOCK + WIN
    rel = jnp.arange(Q_BLOCK)[:, None] + WIN - jnp.arange(span)[None, :]
    band = (rel >= 0) & (rel < WIN)
    w_bias = head_bias[:, :, rel_bucket(rel)]

    def win_step(bi):
        t0 = bi * Q_BLOCK
        qb = lax.dynamic_slice_in_dim(qg, t0, Q_BLOCK, axis=3)
        kb = lax.dynamic_slice_in_dim(k_win, t0, span, axis=2)
        vb = lax.dynamic_slice_in_dim(v_win, t0, span, axis=2)
        mask = band & ((t0 - WIN + jnp.arange(span)) >= 0)[None, :]
        logits = jnp.einsum('bgrqd,bgkd->bgrqk', qb, kb) + w_bias
        p = masked_softmax(logits, mask)
        return jnp.einsum('bgrqk,bgkd->bgrqd', p, vb)

    o_win = lax.map(win_step, jnp.arange(S // Q_BLOCK))
    o_win = o_win.transpose(1, 2, 3, 0, 4, 5).reshape(B, G, R, S, hd)

    gates = jax.nn.sigmoid(gate_logits.astype(f32)).reshape(B, S, G, R, 3).transpose(4, 0, 2, 3, 1)[..., None]
    o = gates[0] * o_cmp + gates[1] * o_slc + gates[2] * o_win
    return o.transpose(0, 3, 1, 2, 4).reshape(B, S, NSA_WIDTH)

def setup_inputs(seed: int = 0) -> dict:
    key = jax.random.key(seed)
    ks = jax.random.split(key, 17)
    f32 = jnp.float32
    L = DEPTH

    def nrm(k, shape, scale):
        return jax.random.normal(k, shape, f32) * scale

    dt = jnp.exp(jax.random.uniform(ks[5], (L, DN_HEADS), f32, minval=math.log(DT_MIN), maxval=math.log(DT_MAX)))
    return {
        'x': nrm(ks[0], (BATCH, SEQ, D_MODEL), 1.0),
        'norm1_g': 1.0 + nrm(ks[1], (L, D_MODEL), 0.02),
        'w_in': nrm(ks[2], (L, D_MODEL, IN_COLS), D_MODEL ** -0.5),
        'dn_conv': nrm(ks[3], (L, DN_CONV, 3 * DN_WIDTH), DN_CONV ** -0.5),
        'dn_a_log': jnp.log(jax.random.uniform(ks[4], (L, DN_HEADS), f32, minval=1.0, maxval=16.0)),
        'dn_dt_bias': dt + jnp.log(-jnp.expm1(-dt)),
        'dn_norm_g': 1.0 + nrm(ks[6], (L, HEAD_DIM), 0.02),
        'cmp_pos': nrm(ks[7], (L, 2, CMP_LEN, HEAD_DIM), 0.02),
        'cmp_w1': nrm(ks[8], (L, 2, CMP_LEN * HEAD_DIM, CMP_HIDDEN), (CMP_LEN * HEAD_DIM) ** -0.5),
        'cmp_w2': nrm(ks[9], (L, 2, CMP_HIDDEN, HEAD_DIM), CMP_HIDDEN ** -0.5),
        'w_out': nrm(ks[10], (L, MIX_WIDTH, D_MODEL), MIX_WIDTH ** -0.5),
        'norm2_g': 1.0 + nrm(ks[11], (L, D_MODEL), 0.02),
        'ffn_up': nrm(ks[12], (L, D_MODEL, 2 * D_FF), D_MODEL ** -0.5),
        'ffn_conv': nrm(ks[13], (L, FFN_CONV, 2 * D_FF), FFN_CONV ** -0.5),
        'ffn_down': nrm(ks[14], (L, D_FF, D_MODEL), D_FF ** -0.5),
        'rel_bias': nrm(ks[15], (N_BIAS_HEADS, REL_BUCKETS), 0.2),
        'final_g': 1.0 + nrm(ks[16], (D_MODEL,), 0.02),
    }

def reference(x, norm1_g, w_in, dn_conv, dn_a_log, dn_dt_bias, dn_norm_g, cmp_pos, cmp_w1, cmp_w2,
              w_out, norm2_g, ffn_up, ffn_conv, ffn_down, rel_bias, final_g):
    dil_bias = rel_bias[:DIL_HEADS]
    nsa_bias = rel_bias[DIL_HEADS:]
    for l in range(DEPTH):
        h = rmsnorm(x, norm1_g[l])
        proj = jnp.einsum('bsd,dp->bsp', h, w_in[l])
        dn_qkv, dn_z, dn_b, dn_a, dil_qkv, nsa_q, nsa_kv, nsa_g = split_cols(proj)
        o_dn = gated_deltanet(dn_qkv, dn_z, dn_b, dn_a, dn_conv[l], dn_a_log[l], dn_dt_bias[l], dn_norm_g[l])
        o_dil = dilated_attention(dil_qkv, dil_bias)
        o_nsa = nsa_attention(nsa_q, nsa_kv, nsa_g, nsa_bias, cmp_pos[l], cmp_w1[l], cmp_w2[l])
        mix = jnp.concatenate([o_dn, o_dil, o_nsa], axis=-1).astype(x.dtype)
        x = x + jnp.einsum('bsm,md->bsd', mix, w_out[l])
        h = rmsnorm(x, norm2_g[l])
        u = causal_dwconv(jnp.einsum('bsd,df->bsf', h, ffn_up[l]), ffn_conv[l])
        u_gate, u_val = jnp.split(u, 2, axis=-1)
        x = x + jnp.einsum('bsf,fd->bsd', jax.nn.silu(u_gate) * u_val, ffn_down[l])
    return rmsnorm(x, final_g)


_drawn_inputs = setup_inputs


def setup_inputs(seed=0):
    import zlib

    import numpy as np

    out = dict(_drawn_inputs(seed))
    spreads = {}
    factors = {'norm1_g': 4.112,
     'dn_norm_g': 7.334,
     'cmp_pos': 64.0,
     'norm2_g': 12.345,
     'final_g': 8.441,
     'rel_bias': 4.345}
    for name, (base, spread) in spreads.items():
        noise = np.random.default_rng([zlib.crc32(name.encode()), seed]).standard_normal(out[name].shape)
        drawn = base * np.exp(spread * noise) if base else spread * noise
        out[name] = jnp.asarray(drawn.astype(out[name].dtype))
    for name, factor in factors.items():
        out[name] = (out[name] * factor).astype(out[name].dtype)
    return out
```

```python
import math
from contextlib import ExitStack, contextmanager

import numpy as np
import concourse.bass as bass
from concourse import mybir

F32 = mybir.dt.float32
F32R = mybir.dt.float32r
ALU = mybir.AluOpType
ACT = mybir.ActivationFunctionType
AX = mybir.AxisListType

P = 128
SEQ = 512
D_MODEL = 2048
HD = 128
TB = SEQ // P
KT = D_MODEL // P
DN_H, DIL_H, NSA_H, NSA_G = 6, 4, 6, 2
NSA_R = NSA_H // NSA_G
CHUNK = 64
N_CHUNK = SEQ // CHUNK
D_FF = 5632
FT = D_FF // P
GT = 4
N_GROUP = FT // GT
CMP_LEN, CMP_STRIDE, CMP_HID = 32, 16, 256
N_CMP = (SEQ - CMP_LEN) // CMP_STRIDE + 1
BUCKETS, REL_MAX = 32, 2048
EPS = 1e-6
SCALE = HD ** -0.5
BIG = 1e30
QW = 512
RING = 8
AHEAD = 6
TW_DIL, TW_NSA = 512, 896
YLEN = 1024
C_G, C_BETA, C_GC, C_BG, C_KD = range(5)
LEVELS = (2, 4, 8, 16, 32)
(K_ID, K_ONE, K_TRI, K_BLK, K_ML, K_MU, K_M1, K_M1T, K_REV) = range(9)
K_LV = 9
N_CST = K_LV + len(LEVELS)
N_SMALL = 2 * DN_H + 3 * NSA_H
TICKS = {"dn_dve": 25, "dn_act": 6, "dil_dve": 16, "nsa_dve": 50, "dil_act": 10, "nsa_act": 6,
         "ffn_dve": 26, "ffn_act": 24}


class Count:

    def __init__(self):
        self.n, self.reg, self.per = 0, None, 0

    def at(self, k=0, div=1, scale=1):
        v = scale * ((self.n + k) // div)
        return v if self.reg is None else self.reg * (scale * self.per // div) + v

    def enter(self, reg, per):
        self.reg, self.per, self.first = reg, per, self.n

    def leave(self, times, what):
        assert self.n - self.first == self.per, (what, self.n - self.first, self.per)
        self.n, self.reg = self.first + self.per * times, None


@contextmanager
def repeat(engine, times, *counts):
    with engine.Fori(0, times) as i:
        for c, per, _ in counts:
            c.enter(i, per)
        yield i
    for c, per, name in counts:
        c.leave(times, name)


def bc(ap, n):
    return ap[:, :, None].to_broadcast([ap.shape[0], ap.shape[1], n])


def program(nc, t):
    with ExitStack() as ctx:
        def sem(name):
            return ctx.enter_context(nc.semaphore(name))

        def sb(c, name, shape, dt=F32):
            return c.enter_context(nc.sbuf_tensor(name, shape, dt))

        h_hi = sb(ctx, "h_hi", [P, KT, SEQ], F32R)
        h_lo = sb(ctx, "h_lo", [P, KT, SEQ], F32R)
        w_raw = sb(ctx, "w_raw", [P, 2, 4 * QW])
        w_hi = sb(ctx, "w_hi", [P, RING, QW], F32R)
        w_lo = sb(ctx, "w_lo", [P, RING, QW], F32R)
        cst = sb(ctx, "cst", [P, N_CST, P])
        eps_t = sb(ctx, "eps_t", [P, 1])
        one_t = sb(ctx, "one_t", [P, 1])
        bank = [ctx.enter_context(nc.psum_tensor(f"bank{i}", [P, QW], F32)) for i in range(8)]
        PB, W = bank[:4], bank[4:]
        ident, ones = cst[:, K_ID, :], cst[:, K_ONE, :]
        mix_d = nc.dram_tensor("mix_scratch", (KT, P, SEQ), F32).ap()
        rev_d = nc.dram_tensor("bias_scratch", (DIL_H + NSA_H, YLEN), F32)

        raw_in = [sem("raw_in_even"), sem("raw_in_odd")]
        hi_done = sem("hi_done")
        lo_done = sem("lo_done")
        q_used = sem("q_used")
        pe_q, act_q, dve_q, sp_u = Count(), Count(), Count(), Count()

        def load_unit(sp):
            if sp_u.n >= 2:
                sp.wait_ge(lo_done, sp_u.at(-1, scale=4))
            u = sp_u.at()
            s = sp_u.n % 2
            src = t["weights"][u, :, :] if sp_u.reg is None else t["weights"][bass.ds(u, 1), :, :]
            if sp_u.reg is not None:
                src = src.rearrange("u p n -> p (u n)")
            sp.dma_start(w_raw[:, s, :], src).then_inc(raw_in[s], 16)
            sp_u.n += 1

        def load_units(sp, last):
            if sp_u.n < 2:
                load_unit(sp)
                load_unit(sp)
            if sp_u.n % 2 and sp_u.n < last:
                load_unit(sp)
            pairs = (last - sp_u.n) // 2
            if pairs > 0:
                with repeat(sp, pairs, (sp_u, 2, "units")):
                    load_unit(sp)
                    load_unit(sp)
            if sp_u.n < last:
                load_unit(sp)

        def raw_quarter(c):
            return w_raw[:, (c.n // 4) % 2, (c.n % 4) * QW:(c.n % 4 + 1) * QW]

        def split_hi(act, n=1):
            for _ in range(n):
                act.wait_ge(raw_in[(act_q.n // 4) % 2], act_q.at(8, div=8, scale=16))
                if act_q.n >= RING:
                    act.wait_ge(q_used, act_q.at(1 - RING))
                nc.scalar.activation(w_hi[:, act_q.n % RING, :], raw_quarter(act_q), ACT.Copy)\
                    .then_inc(hi_done, 1)
                act_q.n += 1

        def split_lo(dve, n=1):
            for _ in range(n):
                dve.wait_ge(hi_done, dve_q.at(1))
                s = dve_q.n % RING
                nc.vector.tensor_tensor(w_lo[:, s, :], raw_quarter(dve_q), w_hi[:, s, :].bitcast(F32),
                                        ALU.subtract).then_inc(lo_done, 1)
                dve_q.n += 1

        dve_chain, act_chain = sem("dve_chain"), sem("act_chain")
        dve_c, act_c = Count(), Count()

        def step(ins):
            ins.then_inc(dve_chain, 1)
            dve_c.n += 1

        def settle(dve):
            dve.wait_ge(dve_chain, dve_c.at())

        def link(dve, ins):
            step(ins)
            settle(dve)

        def astep(ins):
            ins.then_inc(act_chain, 1)
            act_c.n += 1

        def asettle(act):
            act.wait_ge(act_chain, act_c.at())

        def alink(act, ins):
            astep(ins)
            asettle(act)

        def project_half(pe, pb, j):
            q, s = j // 2, pe_q.n % RING
            if j % 2 == 0:
                pe.wait_ge(lo_done, pe_q.at(1))
            for k in range(2 * (j % 2), 2 * (j % 2) + 2):
                kt = 4 * q + k
                for n, (a, b) in enumerate(((w_hi, h_hi), (w_lo, h_hi), (w_hi, h_lo))):
                    m = nc.tensor.matmul(PB[pb][:], a[:, s, k * P:(k + 1) * P], b[:, kt, :],
                                         start=(kt == 0 and n == 0), stop=(kt == KT - 1 and n == 2))
            if j % 2:
                m.then_inc(q_used, 1)
                pe_q.n += 1

        tok = sb(ctx, "tok", [P, DN_H, 5, TB])
        gate = sb(ctx, "gate", [P, 3 * NSA_H, TB])
        small_w = t["w_small"]
        in_x, in_small = sem("in_x"), sem("in_small")
        const_in, table_in = sem("const_in"), sem("table_in")
        stored = sem("stored")

        def normalize(name, x_ready_waits, g_dram, xs, c1):
            sq, y = sb(c1, f"{name}_sq", [P, D_MODEL]), sb(c1, f"{name}_y", [P, 2, D_MODEL])
            ss, rs = sb(c1, f"{name}_ss", [P, TB]), sb(c1, f"{name}_rs", [P, TB])
            gk = sb(c1, f"{name}_g", [P, KT])
            hf = sb(c1, f"{name}_hf", [P, 2, TB, P])
            s = {k: sem(f"{name}_{k}") for k in
                 ("g_in", "sum", "root", "y", "turned", "scaled", "hi", "lo")}
            act_ready, dve_ready = x_ready_waits

            def sp_part(sp):
                sp.dma_start(gk[:], g_dram).then_inc(s["g_in"], 16)

            def act_part(act):
                for b in range(TB):
                    act_ready(act, b)
                    if b:
                        act.wait_ge(s["sum"], b)
                    nc.scalar.activation(sq[:], xs[:, b, :], ACT.Square, accum_out=ss[:, b:b + 1])\
                        .then_inc(s["sum"], 1)
                act.wait_ge(s["sum"], TB)
                nc.scalar.activation(rs[:], ss[:], ACT.Sqrt, bias=eps_t[:], scale=1.0 / D_MODEL)\
                    .then_inc(s["root"], 1)
                for i in range(16):
                    b, kg = i // 4, i % 4
                    act.wait_ge(s["scaled"], i + 1)
                    nc.scalar.activation(h_hi[:, 4 * kg:4 * kg + 4, b * P:(b + 1) * P], hf[:, i % 2],
                                         ACT.Copy).then_inc(s["hi"], 1)

            def dve_part(dve):
                dve.wait_ge(s["root"], 1)
                link(dve, nc.vector.reciprocal(rs[:], rs[:]))
                dve.wait_ge(s["g_in"], 16)
                for i in range(16):
                    b, kg = i // 4, i % 4
                    if kg == 0:
                        if b >= 2:
                            dve.wait_ge(s["turned"], 4 * (b - 1))
                        nc.vector.tensor_scalar(y[:, b % 2, :], xs[:, b, :], rs[:, b:b + 1], None,
                                                ALU.mult).then_inc(s["y"], 1)
                    dve.wait_ge(s["turned"], i + 1)
                    if i >= 2:
                        dve.wait_ge(s["lo"], i - 1)
                    nc.vector.tensor_tensor(hf[:, i % 2], bank[i % 8][:].rearrange("p (k n) -> p k n", k=4),
                                            bc(gk[:, 4 * kg:4 * kg + 4], P), ALU.mult)\
                        .then_inc(s["scaled"], 1)
                    dve.wait_ge(s["hi"], i + 1)
                    nc.vector.tensor_tensor(h_lo[:, 4 * kg:4 * kg + 4, b * P:(b + 1) * P], hf[:, i % 2],
                                            h_hi[:, 4 * kg:4 * kg + 4, b * P:(b + 1) * P].bitcast(F32),
                                            ALU.subtract).then_inc(s["lo"], 1)

            def pe_part(pe):
                for i in range(16):
                    b, kg = i // 4, i % 4
                    pe.wait_ge(s["y"], b + 1)
                    if i >= 8:
                        pe.wait_ge(s["scaled"], i - 7)
                    for k in range(4):
                        kt = 4 * kg + k
                        m = nc.tensor.transpose(bank[i % 8][:, k * P:(k + 1) * P],
                                                y[:, b % 2, kt * P:(kt + 1) * P], ident)
                    m.then_inc(s["turned"], 1)

            return sp_part, act_part, dve_part, pe_part, s["lo"]

        with ExitStack() as c1, nc.Block() as block:
            xs = sb(c1, "xs1", [P, TB, D_MODEL])
            sw = sb(c1, "small_raw", [P, KT, N_SMALL])
            sw_hi = sb(c1, "small_hi", [P, KT, N_SMALL], F32R)
            sw_lo = sb(c1, "small_lo", [P, KT, N_SMALL], F32R)
            st = sb(c1, "small_t", [N_SMALL, SEQ])
            sk = sb(c1, "small_tok", [P, TB, N_SMALL])
            ab = sb(c1, "a_log_bc", [P, 2, DN_H])
            bl, oh = sb(c1, "bias_lhs", [BUCKETS + 2, DIL_H + NSA_H]), sb(c1, "onehot", [BUCKETS + 2, YLEN])
            rev = sb(c1, "bias_rows", [DIL_H + NSA_H, YLEN])
            xa, ax = sb(c1, "xa", [P, DN_H, TB]), sb(c1, "ax", [P, DN_H, TB])
            gr, gt = sb(c1, "g_raw", [P, DN_H, TB]), sb(c1, "g_tot", [P, DN_H, TB])
            eb = sb(c1, "eb", [P, DN_H, TB])
            x_in = [sem(f"x_in{b}") for b in range(TB)]
            const_ready, ps_small, sm_hi, sm_lo = sem("const_ready"), sem("ps_small"), sem("sm_hi"), sem("sm_lo")
            sm_t, sm_tp, sm_tok, rev_ps, rev_sb = (sem(n) for n in ("sm_t", "sm_tp", "sm_tok", "rev_ps", "rev_sb"))
            g_e, g_a, g_cum, g_ok = sem("g_exp"), sem("g_act"), sem("g_cum"), sem("g_ok")
            n1_sp, n1_act, n1_dve, n1_pe, n1_lo = normalize(
                "n1", (lambda e, b: e.wait_ge(x_in[b], 16), None), t["g1"], xs, c1)

            @block.sync
            def _(sp):
                for b in range(TB):
                    sp.dma_start(xs[:, b, :], t["x"][b * P:(b + 1) * P, :]).then_inc(x_in[b], 16)
                sp.dma_start(cst[:], t["cst"]).then_inc(const_in, 16)
                n1_sp(sp)
                sp.dma_start(sw[:], small_w).then_inc(in_small, 16)
                sp.dma_start(ab[:], t["ab"]).then_inc(in_small, 16)
                sp.dma_start(bl[:], t["bias_lhs"]).then_inc(in_small, 16)
                sp.dma_start(oh[:], t["onehot"]).then_inc(in_small, 16)
                load_units(sp, 2)
                sp.wait_ge(rev_sb, 1)
                sp.dma_start(rev_d.ap()[:, :], rev[:]).then_inc(stored, 16)
                sp.wait_ge(stored, 16)

            @block.gpsimd
            def _(pool):
                nc.gpsimd.memset(eps_t[:], EPS).then_inc(const_ready, 1)
                nc.gpsimd.memset(one_t[:], 1.0).then_inc(const_ready, 1)

            @block.scalar
            def _(act):
                act.wait_ge(const_ready, 2)
                n1_act(act)
                act.wait_ge(in_small, 64)
                nc.scalar.activation(sw_hi[:], sw[:], ACT.Copy).then_inc(sm_hi, 1)
                act.wait_ge(ps_small, 1)
                nc.scalar.activation(st[:], bank[0][0:N_SMALL, :], ACT.Copy).then_inc(sm_t, 1)
                act.wait_ge(sm_tok, 2)
                astep(nc.scalar.activation(eb[:], sk[:, :, 0:DN_H].rearrange("p b h -> p h b"), ACT.Exp,
                                           scale=-1.0))
                astep(nc.scalar.activation(gate[:], sk[:, :, 2 * DN_H:].rearrange("p b c -> p c b"), ACT.Exp,
                                           scale=-1.0))
                astep(nc.scalar.activation(ab[:, 0, :], ab[:, 0, :], ACT.Exp))
                alink(act, nc.scalar.activation(ax[:], xa[:], ACT.Abs))
                alink(act, nc.scalar.activation(ax[:], ax[:], ACT.Exp, scale=-1.0))
                nc.scalar.activation(ax[:], ax[:], ACT.Ln, bias=one_t[:]).then_inc(g_a, 1)
                act.wait_ge(g_ok, 2)
                nc.scalar.activation(tok[:, :, C_BG, :], tok[:, :, C_GC, :], ACT.Exp).then_inc(g_e, 1)
                nc.scalar.activation(tok[:, :, C_KD, :], gt[:], ACT.Exp).then_inc(g_e, 1)
                split_hi(act, AHEAD)

            @block.vector
            def _(dve):
                n1_dve(dve)
                dve.wait_ge(sm_hi, 1)
                nc.vector.tensor_tensor(sw_lo[:], sw[:], sw_hi[:].bitcast(F32), ALU.subtract).then_inc(sm_lo, 1)
                dve.wait_ge(rev_ps, 1)
                step(nc.vector.tensor_copy(rev[:, 0:512], bank[1][0:DIL_H + NSA_H, :]))
                nc.vector.tensor_copy(rev[:, 512:1024], bank[2][0:DIL_H + NSA_H, :]).then_inc(rev_sb, 1)
                dve.wait_ge(sm_tp, 1)
                nc.vector.tensor_copy(sk[:], bank[3][:, 0:TB * 32].rearrange("p (b c) -> p b c", b=TB)[:, :, 0:N_SMALL])\
                    .then_inc(sm_tok, 1)
                dve.wait_ge(sm_tok, 1)
                nc.vector.tensor_tensor(xa[:], sk[:, :, DN_H:2 * DN_H].rearrange("p b h -> p h b"),
                                        bc(ab[:, 1, :], TB), ALU.add).then_inc(sm_tok, 1)
                dve.wait_ge(g_a, 1)
                link(dve, nc.vector.tensor_scalar(eb[:], eb[:], 1.0, None, ALU.add))
                step(nc.vector.reciprocal(tok[:, :, C_BETA, :], eb[:]))
                link(dve, nc.vector.tensor_scalar(gate[:], gate[:], 1.0, None, ALU.add))
                step(nc.vector.reciprocal(gate[:], gate[:]))
                link(dve, nc.vector.scalar_tensor_tensor(gr[:], xa[:], 0.0, ax[:], ALU.max, ALU.add))
                link(dve, nc.vector.scalar_tensor_tensor(gr[:], gr[:], -1.0, bc(ab[:, 0, :], TB), ALU.mult, ALU.mult))
                nc.vector.tensor_copy(tok[:, :, C_G, :], gr[:]).then_inc(g_ok, 1)
                dve.wait_ge(g_cum, 1)
                link(dve, nc.vector.tensor_copy(tok[:, :, C_GC, :], bank[4][:, 0:DN_H * TB].rearrange("p (h b) -> p h b", h=DN_H)))
                nc.vector.tensor_tensor(gt[:], bank[5][:, 0:DN_H * TB].rearrange("p (h b) -> p h b", h=DN_H),
                                        tok[:, :, C_GC, :], ALU.subtract).then_inc(g_ok, 1)
                dve.wait_ge(g_e, 2)
                link(dve, nc.vector.tensor_tensor(tok[:, :, C_BG, :], tok[:, :, C_BG, :], tok[:, :, C_BETA, :], ALU.mult))
                split_lo(dve, AHEAD)

            @block.tensor
            def _(pe):
                pe.wait_ge(const_in, 16)
                n1_pe(pe)
                pe.wait_ge(n1_lo, 16)
                pe.wait_ge(sm_lo, 1)
                for kt in range(KT):
                    for n, (a, b) in enumerate(((sw_hi, h_hi), (sw_lo, h_hi), (sw_hi, h_lo))):
                        m = nc.tensor.matmul(bank[0][0:N_SMALL, :], a[:, kt, :], b[:, kt, :],
                                             start=(kt == 0 and n == 0), stop=(kt == KT - 1 and n == 2))
                m.then_inc(ps_small, 1)
                for i in range(2):
                    m = nc.tensor.matmul(bank[1 + i][0:DIL_H + NSA_H, :], bl[:], oh[:, i * 512:(i + 1) * 512],
                                         start=True, stop=True)
                m.then_inc(rev_ps, 1)
                pe.wait_ge(sm_t, 1)
                for b in range(TB):
                    m = nc.tensor.transpose(bank[3][:, b * 32:b * 32 + N_SMALL], st[:, b * P:(b + 1) * P],
                                            cst[0:N_SMALL, K_ID, 0:N_SMALL])
                m.then_inc(sm_tp, 1)
                pe.wait_ge(g_ok, 1)
                nc.tensor.matmul(bank[4][:, 0:DN_H * TB], cst[:, K_TRI, :], gr[:].rearrange("p h b -> p (h b)"),
                                 start=True, stop=True)
                nc.tensor.matmul(bank[5][:, 0:DN_H * TB], cst[:, K_BLK, :], gr[:].rearrange("p h b -> p (h b)"),
                                 start=True, stop=True).then_inc(g_cum, 1)

        with ExitStack() as c2, nc.Block() as block:
            names = ("gb qp kp vp zs qT kT kbg kdec vb m1 D DT EG qg A AT T U Y attnT u wT ob").split()
            B = {n: sb(c2, f"dn_{n}", [P, SEQ]) for n in names}
            LT = sb(c2, "dn_LT", [P, len(LEVELS), SEQ])
            S = sb(c2, "dn_S", [P, P])
            hp, cw = sb(c2, "dn_hp", [P, 5, TB]), sb(c2, "dn_cw", [P, 3, 4])
            cwa = sb(c2, "dn_cwa", [P, DN_H, 3, 4])
            ng = sb(c2, "dn_ng", [P, 1])
            ssq, rms = sb(c2, "dn_ssq", [P, TB]), sb(c2, "dn_rms", [P, TB])
            trash = sb(c2, "dn_trash", [P, P])

            def v3(ap):
                return ap.rearrange("p (b n) -> p b n", b=TB)

            par_in = sem("dn_par_in")
            (g_rep, grow_ps, conv_v, z_free, silu_a, sqr_a, norm_ps, root_a, qk_n, tr_ps, tr_used, masks_v, decay_a,
             kk_ps, qk_ps, a_v, at_v2, at_ps, at_a, lt_g, t_v, y_ps, y_a, d_ps, uw_ps, uw_a, ready_v, v_ps, vn_v,
             s_ps, s_v, o_a, osc_v, o_ps, o_v) = (
                sem(f"dn_{n}") for n in (
                    "g_rep grow_ps conv_v z_free silu_a sqr_a norm_ps root_a qk_n tr_ps tr_used masks_v decay_a "
                    "kk_ps qk_ps a_v at_v at_ps at_a lt_g t_v y_ps y_a d_ps uw_ps uw_a ready_v v_ps vn_v "
                    "s_ps s_v o_a osc_v o_ps o_v").split())
            NL = len(LEVELS)

            def dn_pe(pe, h, next_units):
                halves = iter([(u, j) for u in range(next_units) for j in range(8)])

                def fill(n):
                    for _ in range(n):
                        u_j = next(halves, None)
                        if u_j is None:
                            return
                        u, j = u_j
                        if j == 0:
                            if u < 3:
                                pe.wait_ge(conv_v, 3 * h + u + 1)
                            else:
                                pe.wait_ge(z_free, h + 1)
                        project_half(pe, u, j)

                pe.wait_ge(g_rep, h + 1)
                for b in range(TB):
                    m = nc.tensor.matmul(W[0][:, b * P:(b + 1) * P], B["gb"][:, b * P:(b + 1) * P],
                                         cst[:, K_TRI, :], start=True, stop=True)
                m.then_inc(grow_ps, 1)
                fill(3)
                pe.wait_ge(sqr_a, 2 * h + 2)
                nc.tensor.matmul(W[1][:], ones, B["Y"][:], start=True, stop=True).then_inc(norm_ps, 1)
                nc.tensor.matmul(W[2][:], ones, B["u"][:], start=True, stop=True).then_inc(norm_ps, 1)
                fill(4)
                pe.wait_ge(qk_n, 2 * h + 2)
                for b in range(TB):
                    m = nc.tensor.transpose(W[3][:, b * P:(b + 1) * P], B["kT"][:, b * P:(b + 1) * P], ident)
                m.then_inc(tr_ps, 1)
                for b in range(TB):
                    m = nc.tensor.matmul(W[2][:, b * P:(b + 1) * P], B["kT"][:, b * P:(b + 1) * P],
                                         B["kT"][:, b * P:(b + 1) * P], start=True, stop=True)
                m.then_inc(kk_ps, 1)
                pe.wait_ge(silu_a, 3 * h + 3)
                for b in range(TB):
                    m = nc.tensor.transpose(W[1][:, b * P:(b + 1) * P], B["vp"][:, b * P:(b + 1) * P], ident)
                m.then_inc(tr_ps, 1)
                fill(3)
                pe.wait_ge(a_v, h + 1)
                pe.wait_ge(decay_a, h + 1)
                for b in range(TB):
                    m = nc.tensor.transpose(W[0][:, b * P:(b + 1) * P], B["A"][:, b * P:(b + 1) * P], ident)
                m.then_inc(at_ps, 1)
                pe.wait_ge(tr_used, 2 * h + 1)
                for b in range(TB):
                    m = nc.tensor.matmul(W[3][:, b * P:(b + 1) * P], B["kT"][:, b * P:(b + 1) * P],
                                         B["qT"][:, b * P:(b + 1) * P], start=True, stop=True)
                m.then_inc(qk_ps, 1)
                fill(2)
                for lv in range(NL):
                    pe.wait_ge(t_v, (NL + 1) * h + lv + 1)
                    pe.wait_ge(lt_g, NL * h + lv + 1)
                    if lv == 0:
                        pe.wait_ge(tr_used, 2 * h + 2)
                    for b in range(TB):
                        c = slice(b * P, (b + 1) * P)
                        m = nc.tensor.matmul(W[1][:, c], LT[:, lv, c], B["T"][:, c], start=True, stop=True)
                    m.then_inc(y_ps, 1)
                    fill(1)
                    pe.wait_ge(y_a, NL * h + lv + 1)
                    if lv == 0:
                        pe.wait_ge(ready_v, 2 * h + 1)
                    for b in range(TB):
                        c = slice(b * P, (b + 1) * P)
                        m = nc.tensor.matmul(W[3][:, c], B["Y"][:, c], B["U"][:, c], start=True, stop=True)
                        if lv < NL - 1:
                            m = nc.tensor.matmul(W[2][:, c], B["U"][:, c], B["Y"][:, c], start=True, stop=True)
                    m.then_inc(d_ps, 1)
                    fill(1)
                pe.wait_ge(t_v, (NL + 1) * h + NL + 1)
                for b in range(TB):
                    c = slice(b * P, (b + 1) * P)
                    nc.tensor.matmul(W[1][:, c], B["U"][:, c], B["vb"][:, c], start=True, stop=True)
                    m = nc.tensor.matmul(W[2][:, c], B["kbg"][:, c], B["U"][:, c], start=True, stop=True)
                m.then_inc(uw_ps, 1)
                fill(2)
                for c in range(N_CHUNK):
                    b, o = c // 2, CHUNK * (c % 2)
                    rows, cc = slice(o, o + CHUNK), slice(c * CHUNK, (c + 1) * CHUNK)
                    cb = slice(b * P, (b + 1) * P)
                    pe.wait_ge(s_v, (N_CHUNK + 1) * h + c + 1)
                    if c == 0:
                        pe.wait_ge(uw_a, 2 * h + 2)
                        pe.wait_ge(ready_v, 2 * h + 2)
                    nc.tensor.matmul(W[1][rows, cb], B["wT"][:, cc], S[:], start=True, stop=True)\
                        .then_inc(v_ps, 1)
                    nc.tensor.matmul(W[3][rows, cb], B["qg"][:, cc], S[:], start=True, stop=False)
                    fill(1)
                    pe.wait_ge(vn_v, N_CHUNK * h + c + 1)
                    nc.tensor.matmul(W[2][:, 0:P], B["kdec"][rows, cb], B["qp"][rows, cb],
                                     start=True, stop=True).then_inc(s_ps, 1)
                    nc.tensor.matmul(W[3][rows, cb], B["attnT"][rows, cc.start:cc.stop],
                                     B["qp"][rows, cb], start=False, stop=True).then_inc(s_ps, 1)
                fill(32)
                pe.wait_ge(osc_v, h + 1)
                for b in range(TB):
                    m = nc.tensor.transpose(W[1][:, b * P:(b + 1) * P], B["gb"][:, b * P:(b + 1) * P], ident)
                m.then_inc(o_ps, 1)

            def dn_act(act, h, splits):
                left = [splits]

                def sp_hi(n):
                    n = min(n, left[0])
                    left[0] -= n
                    split_hi(act, n)

                for i, n in enumerate(("qp", "kp", "vp")):
                    act.wait_ge(conv_v, 3 * h + i + 1)
                    nc.scalar.activation(B[n][:], B[n][:], ACT.Silu).then_inc(silu_a, 1)
                act.wait_ge(q_used, 16 * h + 16)
                nc.scalar.activation(B["zs"][:], PB[3][:], ACT.Silu).then_inc(z_free, 1)
                act.wait_ge(z_free, h + 1)
                for i, (src, dst) in enumerate((("qp", "Y"), ("kp", "u"))):
                    nc.scalar.activation(B[dst][:], B[src][:], ACT.Square).then_inc(sqr_a, 1)
                sp_hi(2)
                for i, n in enumerate(("A", "AT")):
                    act.wait_ge(norm_ps, 2 * h + i + 1)
                    nc.scalar.activation(B[n][:], W[1 + i][:], ACT.Sqrt, bias=eps_t[:]).then_inc(root_a, 1)
                sp_hi(1)
                act.wait_ge(masks_v, h + 1)
                astep(nc.scalar.activation(B["D"][:], B["D"][:], ACT.Exp, scale=-1.0))
                astep(nc.scalar.activation(B["DT"][:], B["DT"][:], ACT.Exp))
                nc.scalar.activation(B["EG"][:], W[0][:], ACT.Exp).then_inc(decay_a, 1)
                sp_hi(2)
                act.wait_ge(at_ps, h + 1)
                nc.scalar.activation(B["AT"][:], W[0][:], ACT.Copy).then_inc(at_a, 1)
                sp_hi(1)
                for lv in range(NL):
                    act.wait_ge(y_ps, NL * h + lv + 1)
                    nc.scalar.activation(B["Y"][:], W[1][:], ACT.Copy).then_inc(y_a, 1)
                    sp_hi(1)
                act.wait_ge(uw_ps, h + 1)
                nc.scalar.activation(B["u"][:], W[1][:], ACT.Copy).then_inc(uw_a, 1)
                nc.scalar.activation(B["wT"][:], W[2][:], ACT.Copy).then_inc(uw_a, 1)
                sp_hi(16)
                act.wait_ge(s_ps, 2 * N_CHUNK * (h + 1))
                for b in range(TB):
                    alink(act, nc.scalar.activation(trash[:], W[3][:, b * P:(b + 1) * P], ACT.Square,
                                                    accum_out=ssq[:, b:b + 1]))
                nc.scalar.activation(rms[:], ssq[:], ACT.Sqrt, bias=eps_t[:], scale=1.0 / HD).then_inc(o_a, 1)
                act.wait_ge(o_a, h + 1)

            def dn_dve(dve, h, splits):
                left = [splits]

                def sp_lo(n):
                    n = min(n, left[0])
                    left[0] -= n
                    split_lo(dve, n)

                settle(dve)
                if isinstance(h, int):
                    tok_h, cw_h = tok[:, h], cwa[:, h]
                else:
                    tok_h = tok[:, bass.ds(h, 1)].rearrange("p a c b -> p (a c) b")
                    cw_h = cwa[:, bass.ds(h, 1)].rearrange("p a c b -> p (a c) b")
                step(nc.vector.tensor_copy(hp[:], tok_h))
                link(dve, nc.vector.tensor_copy(cw[:], cw_h))
                nc.vector.tensor_copy(v3(B["gb"][:]), bc(hp[:, C_G, :], P)).then_inc(g_rep, 1)
                for i, n in enumerate(("qp", "kp", "vp")):
                    dve.wait_ge(q_used, 16 * h + 4 * i + 4)
                    link(dve, nc.vector.tensor_scalar(B[n][:], PB[i][:], cw[:, i, 3:4], None, ALU.mult))
                    for k in (1, 2, 3):
                        ins = nc.vector.scalar_tensor_tensor(
                            B[n][:, k:SEQ], PB[i][:, 0:SEQ - k], cw[:, i, 3 - k:4 - k], B[n][:, k:SEQ],
                            ALU.mult, ALU.add)
                        if k < 3:
                            link(dve, ins)
                        else:
                            ins.then_inc(conv_v, 1)
                sp_lo(2)
                dve.wait_ge(grow_ps, h + 1)
                link(dve, nc.vector.tensor_tensor(v3(B["m1"][:]), v3(W[0][:]), bc(hp[:, C_GC, :], P), ALU.subtract))
                step(nc.vector.tensor_tensor(v3(B["D"][:]), v3(B["m1"][:]),
                                             cst[:, K_ML:K_ML + 1, :].to_broadcast([P, TB, P]), ALU.add))
                nc.vector.tensor_tensor(v3(B["DT"][:]), v3(B["m1"][:]),
                                        cst[:, K_MU:K_MU + 1, :].to_broadcast([P, TB, P]), ALU.add)\
                    .then_inc(masks_v, 1)
                for i, (r, src, dst, sc) in enumerate((("A", "qp", "qT", SCALE), ("AT", "kp", "kT", 1.0))):
                    dve.wait_ge(root_a, 2 * h + i + 1)
                    link(dve, nc.vector.reciprocal(B[r][:], B[r][:]))
                    nc.vector.scalar_tensor_tensor(B[dst][:], B[src][:], sc, B[r][:], ALU.mult, ALU.mult)\
                        .then_inc(qk_n, 1)
                sp_lo(1)
                dve.wait_ge(kk_ps, h + 1)
                dve.wait_ge(decay_a, h + 1)
                dve.wait_ge(qk_n, 2 * h + 2)
                link(dve, nc.vector.tensor_tensor(B["A"][:], W[2][:], B["D"][:], ALU.mult))
                nc.vector.tensor_tensor(v3(B["A"][:]), v3(B["A"][:]), bc(hp[:, C_BETA, :], P), ALU.mult)\
                    .then_inc(a_v, 1)
                dve.wait_ge(tr_ps, 2 * h + 1)
                step(nc.vector.tensor_tensor(v3(B["kbg"][:]), v3(W[3][:]), bc(hp[:, C_BG, :], P), ALU.mult))
                nc.vector.tensor_tensor(v3(B["kdec"][:]), v3(W[3][:]), bc(hp[:, C_KD, :], P), ALU.mult)\
                    .then_inc(tr_used, 1)
                dve.wait_ge(a_v, h + 1)
                link(dve, nc.vector.tensor_tensor(v3(B["T"][:]), v3(B["A"][:]),
                                                  cst[:, K_M1:K_M1 + 1, :].to_broadcast([P, TB, P]), ALU.mult))
                step(nc.vector.tensor_tensor(v3(B["T"][:]), cst[:, K_ID:K_ID + 1, :].to_broadcast([P, TB, P]),
                                             v3(B["T"][:]), ALU.subtract))
                dve.wait_ge(tr_ps, 2 * h + 2)
                nc.vector.tensor_tensor(v3(B["vb"][:]), v3(W[1][:]), bc(hp[:, C_BETA, :], P), ALU.mult)\
                    .then_inc(tr_used, 1)
                dve.wait_ge(at_a, h + 1)
                link(dve, nc.vector.tensor_tensor(v3(B["U"][:]), v3(B["AT"][:]),
                                                  cst[:, K_M1T:K_M1T + 1, :].to_broadcast([P, TB, P]), ALU.mult))
                nc.vector.tensor_tensor(v3(B["U"][:]), cst[:, K_ID:K_ID + 1, :].to_broadcast([P, TB, P]),
                                        v3(B["U"][:]), ALU.subtract).then_inc(t_v, 1)
                sp_lo(1)
                dve.wait_ge(qk_ps, h + 1)
                nc.vector.tensor_tensor(B["attnT"][:], W[3][:], B["DT"][:], ALU.mult).then_inc(ready_v, 1)
                sp_lo(1)
                for lv in range(NL):
                    dve.wait_ge(d_ps, NL * h + lv + 1)
                    dve.wait_ge(t_v, (NL + 1) * h + lv + 1)
                    if lv < NL - 1:
                        step(nc.vector.tensor_tensor(B["T"][:], B["T"][:], W[2][:], ALU.subtract))
                    nc.vector.tensor_tensor(B["U"][:], B["U"][:], W[3][:], ALU.subtract).then_inc(t_v, 1)
                    sp_lo(1)
                nc.vector.memset(S[:], 0.0).then_inc(s_v, 1)
                nc.vector.tensor_tensor(B["qg"][:], B["qT"][:], B["EG"][:], ALU.mult).then_inc(ready_v, 1)
                dve.wait_ge(uw_a, 2 * h + 1)
                for c in range(N_CHUNK):
                    b, o = c // 2, CHUNK * (c % 2)
                    rows, cb = slice(o, o + CHUNK), slice(b * P, (b + 1) * P)
                    dve.wait_ge(v_ps, N_CHUNK * h + c + 1)
                    nc.vector.tensor_tensor(B["qp"][rows, cb], B["u"][rows, cb], W[1][rows, cb], ALU.subtract)\
                        .then_inc(vn_v, 1)
                    last = (c + 1) * CHUNK - 1
                    dve.wait_ge(s_ps, 2 * N_CHUNK * h + 2 * c + 1)
                    dve.wait_ge(s_v, (N_CHUNK + 1) * h + c + 1)
                    nc.vector.scalar_tensor_tensor(S[:], S[:], B["EG"][:, last:last + 1], W[2][:, 0:P],
                                                   ALU.mult, ALU.add).then_inc(s_v, 1)
                    sp_lo(1)
                sp_lo(16)
                dve.wait_ge(o_a, h + 1)
                link(dve, nc.vector.reciprocal(rms[:], rms[:]))
                nc.vector.tensor_tensor(v3(B["gb"][:]), v3(W[3][:]), bc(rms[:], P), ALU.mult).then_inc(osc_v, 1)
                dve.wait_ge(o_ps, h + 1)
                dve.wait_ge(stored, 16 * h + 16)
                nc.vector.scalar_tensor_tensor(B["ob"][:], W[1][:], ng[:], B["zs"][:], ALU.mult, ALU.mult)\
                    .then_inc(o_v, 1)
                dve.wait_ge(o_v, h + 1)

            def dn_pool(pool, h):
                for lv in range(NL):
                    pool.wait_ge(at_a, h + 1)
                    nc.gpsimd.tensor_tensor(v3(LT[:, lv, :]), v3(B["AT"][:]),
                                            cst[:, K_LV + lv:K_LV + lv + 1, :].to_broadcast([P, TB, P]),
                                            ALU.mult).then_inc(lt_g, 1)

            @block.sync
            def _(sp):
                sp.dma_start(cwa[:], t["dn_conv"]).then_inc(par_in, 16)
                sp.dma_start(ng[:], t["dn_norm"]).then_inc(par_in, 16)
                load_units(sp, 2 + 2)
                for h in range(DN_H):
                    want = (16 + 16 * (h + 1 if h < DN_H - 1 else h) + (12 if h == DN_H - 1 else 0) + AHEAD + 3) // 4
                    load_units(sp, want)
                    sp.wait_ge(o_v, h + 1)
                    sp.dma_start(mix_d[h, :, :], B["ob"][:]).then_inc(stored, 16)
                sp.wait_ge(stored, 16 * DN_H + 16)

            @block.gpsimd
            def _(pool):
                pool.wait_ge(const_in, 16)
                with pool.Fori(0, DN_H) as h:
                    dn_pool(pool, h)

            @block.tensor
            def _(pe):
                for u in range(4):
                    for j in range(8):
                        project_half(pe, u, j)
                with repeat(pe, DN_H - 1, (pe_q, 16, "dn_pe quarters")) as h:
                    dn_pe(pe, h, 4)
                dn_pe(pe, DN_H - 1, 3)

            @block.scalar
            def _(act):
                split_hi(act, 16)
                with repeat(act, DN_H - 1, (act_q, 16, "dn_act quarters"), (act_c, TICKS["dn_act"], "dn_act")) as h:
                    dn_act(act, h, 16)
                dn_act(act, DN_H - 1, 12)

            @block.vector
            def _(dve):
                dve.wait_ge(par_in, 32)
                split_lo(dve, 16)
                with repeat(dve, DN_H - 1, (dve_q, 16, "dn_dve quarters"), (dve_c, TICKS["dn_dve"], "dn_dve")) as h:
                    dn_dve(dve, h, 16)
                dn_dve(dve, DN_H - 1, 12)

        (att_s, att_m, att_e, att_p, att_t, att_pt, att_o) = (
            sem(f"att_{n}") for n in (
                "scores",
                "max",
                "exp",
                "probs",
                "turned",
                "probs_t",
                "out"))

        def scores(n, b, q, k):
            m = nc.tensor.matmul(W[b % 2][:, 0:(b + 1) * P], q[:, b * P:(b + 1) * P], k[:, 0:(b + 1) * P],
                                 start=True, stop=True)
            m.then_inc(att_s, 1)

        def attend_pe(pe, n, k, q, v, lg, PT, out, start, stop, fill, fills, after=None):
            for b in range(TB):
                pe.wait_ge(att_p, 4 * n + b + 1)
                for sb_ in range(b + 1):
                    m = nc.tensor.transpose(W[2 + b % 2][:, sb_ * P:(sb_ + 1) * P], lg[:, b, sb_ * P:(sb_ + 1) * P],
                                            ident)
                m.then_inc(att_t, 1)
                if b < 2:
                    pe.wait_ge(att_m, 4 * n + b + 1)
                    scores(n, b + 2, q, k)
                elif after is not None:
                    pe.wait_ge(att_m, 4 * n + b + 1)
                    scores(n + 1, b - 2, after[0], after[1])
                fill(fills[b])
                if b < 2:
                    pe.wait_ge(att_pt, 4 * n + b + 1)
            pe.wait_ge(att_pt, 4 * n + 4)
            for sb_ in range(TB):
                m = nc.tensor.matmul(out[:, sb_ * P:SEQ], v[:, sb_, :], PT[:, sb_, sb_ * P:SEQ],
                                     start=(start and sb_ == 0), stop=(stop and sb_ == TB - 1))
            m.then_inc(att_o, 1)

        def att_rows(dve, n, b, lg, nm, bias):
            dve.wait_ge(att_s, 4 * n + b + 1)
            width = (b + 1) * P
            link(dve, nc.vector.tensor_tensor(lg[:, b, 0:width], W[b % 2][:, 0:width],
                                              bias(TB * P - width, TB * P), ALU.add))
            nc.vector.tensor_reduce(nm[:, b:b + 1], lg[:, b, 0:width], AX.X, ALU.max, negate=True).then_inc(att_m, 1)

        def att_norm(dve, n, b, lg, den, gates):
            width = (b + 1) * P
            dve.wait_ge(att_e, 4 * n + b + 1)
            link(dve, nc.vector.reciprocal(den[:, b:b + 1], den[:, b:b + 1]))
            if gates is None:
                ins = nc.vector.tensor_scalar(lg[:, b, 0:width], lg[:, b, 0:width], den[:, b:b + 1], None, ALU.mult)
            else:
                ins = nc.vector.tensor_scalar(lg[:, b, 0:width], lg[:, b, 0:width], den[:, b:b + 1],
                                              gates[:, b:b + 1], ALU.mult, ALU.mult)
            ins.then_inc(att_p, 1)

        def attend_dve(dve, n, lg, nm, den, bias, gates, first, split):
            for b in range(TB):
                if not first:
                    dve.wait_ge(att_t, 4 * (n - 1) + b + 1)
                att_rows(dve, n, b, lg, nm, bias)
                if b >= 1:
                    att_norm(dve, n, b - 1, lg, den, gates)
                split(1)
            att_norm(dve, n, TB - 1, lg, den, gates)

        def attend_act(act, n, lg, nm, den, PT, first, split):
            def turn(b):
                act.wait_ge(att_t, 4 * n + b + 1)
                if b == 0 and not first:
                    act.wait_ge(att_o, n)
                nc.scalar.activation(PT[:, 0:b + 1, b * P:(b + 1) * P],
                                     W[2 + b % 2][:, 0:(b + 1) * P].rearrange("p (s n) -> p s n", n=P),
                                     ACT.Copy).then_inc(att_pt, 1)

            for b in range(TB):
                act.wait_ge(att_m, 4 * n + b + 1)
                nc.scalar.activation(lg[:, b, 0:(b + 1) * P], lg[:, b, 0:(b + 1) * P], ACT.Exp,
                                     bias=nm[:, b:b + 1], accum_out=den[:, b:b + 1]).then_inc(att_e, 1)
                split(1)
                if b >= 1:
                    turn(b - 1)
            turn(TB - 1)

        turned_ps, turned_sb = sem("table_turned"), sem("table_back")

        def table_pieces(tab, heads, width):
            return [tab[:, h, c:min(c + QW, width)] for h in range(heads) for c in range(0, width, QW)]

        def table_load(sp, tab, first, heads, width):
            for h in range(heads):
                sp.dma_start(tab[:, h, :], bass.AP(tensor=rev_d, offset=(first + h) * YLEN,
                                                   ap=[[1, P], [1, width]])).then_inc(table_in, 16)

        def table_pe(pe, pieces, before, loaded):
            pe.wait_ge(table_in, loaded)
            for i, piece in enumerate(pieces):
                if i >= 4:
                    pe.wait_ge(turned_sb, before + i - 3)
                nc.tensor.matmul(W[i % 4][:, 0:piece.shape[1]], cst[:, K_REV, :], piece, start=True, stop=True)\
                    .then_inc(turned_ps, 1)

        def table_act(act, pieces, before):
            for i, piece in enumerate(pieces):
                act.wait_ge(turned_ps, before + i + 1)
                nc.scalar.activation(piece, W[i % 4][:, 0:piece.shape[1]], ACT.Copy).then_inc(turned_sb, 1)

        Q3 = 16 * DN_H + 12
        with ExitStack() as c3, nc.Block() as block:
            tab = sb(c3, "dil_tab", [P, DIL_H, TW_DIL])
            lg, PT = sb(c3, "dil_lg", [P, TB, SEQ]), sb(c3, "dil_PT", [P, TB, SEQ])
            qs, ks, vs, ob = (sb(c3, f"dil_{n}", [P, SEQ]) for n in ("q", "k", "v", "ob"))
            vt = sb(c3, "dil_vt", [P, TB, P])
            nm, den = sb(c3, "dil_nm", [P, TB]), sb(c3, "dil_den", [P, TB])
            q_ev, kv_ev, vtr_ps, vt_ev, ob_v = (sem(f"dil_{n}") for n in ("q_ev", "kv_ev", "vtr_ps", "vt_ev", "ob_v"))

            def dil_pe(pe, n):
                halves = iter([(u, j) for u in range(3) for j in range(8)])

                def fill(k):
                    for _ in range(k):
                        u, j = next(halves)
                        if u == 0 and j == 0:
                            pe.wait_ge(q_ev, n + 1)
                            pe.wait_ge(kv_ev, 2 * n + 2)
                        project_half(pe, u, j)

                pe.wait_ge(q_ev, n + 1)
                pe.wait_ge(kv_ev, 2 * n + 1)
                scores(n, 0, qs, ks)
                scores(n, 1, qs, ks)
                pe.wait_ge(kv_ev, 2 * n + 2)
                for b in range(TB):
                    m = nc.tensor.transpose(W[3][:, b * P:(b + 1) * P], vs[:, b * P:(b + 1) * P], ident)
                m.then_inc(vtr_ps, 1)
                fill(4)
                pe.wait_ge(vt_ev, n + 1)
                attend_pe(pe, n, ks, qs, vt, lg, PT, PB[3], True, True, fill, (4, 4, 4, 4))
                fill(4)

            def dil_act(act, n):
                act.wait_ge(q_used, Q3 + 12 * n)
                nc.scalar.activation(ks[:], PB[1][:], ACT.Copy).then_inc(kv_ev, 1)
                nc.scalar.activation(vs[:], PB[2][:], ACT.Copy).then_inc(kv_ev, 1)
                split_hi(act, 2)
                act.wait_ge(vtr_ps, n + 1)
                nc.scalar.activation(vt[:].rearrange("p b n -> p (b n)"), W[3][:], ACT.Copy).then_inc(vt_ev, 1)
                attend_act(act, n, lg, nm, den, PT, True, lambda k: split_hi(act, 2 * k))
                split_hi(act, 2)

            def dil_dve(dve, n, hd):
                settle(dve)
                dve.wait_ge(q_used, Q3 + 12 * n)
                nc.vector.tensor_scalar(qs[:], PB[0][:], SCALE, None, ALU.mult).then_inc(q_ev, 1)
                split_lo(dve, 2)

                def bias(a, e):
                    if isinstance(hd, int):
                        return tab[:, hd, a:e]
                    return tab[:, bass.ds(hd, 1), a:e].rearrange("p a n -> p (a n)")

                attend_dve(dve, n, lg, nm, den, bias, None, True, lambda k: split_lo(dve, 2 * k))
                split_lo(dve, 2)
                dve.wait_ge(att_o, n + 1)
                dve.wait_ge(stored, 16 * DN_H + 16 + 16 * n)
                nc.vector.tensor_copy(ob[:], PB[3][:]).then_inc(ob_v, 1)
                dve.wait_ge(ob_v, n + 1)

            @block.sync
            def _(sp):
                table_load(sp, tab, 0, DIL_H, TW_DIL)
                for n in range(DIL_H):
                    load_units(sp, (Q3 + 12 * (n + 1) + AHEAD + 3) // 4)
                    sp.wait_ge(ob_v, n + 1)
                    sp.dma_start(mix_d[DN_H + n, :, :], ob[:]).then_inc(stored, 16)
                sp.wait_ge(stored, 16 * (DN_H + DIL_H) + 16)

            pieces = table_pieces(tab, DIL_H, TW_DIL)

            @block.tensor
            def _(pe):
                table_pe(pe, pieces, 0, 16 * DIL_H)
                pe.wait_ge(turned_sb, DIL_H)
                with repeat(pe, DIL_H // 2, (pe_q, 24, "dil_pe quarters")) as i:
                    dil_pe(pe, 2 * i)
                    dil_pe(pe, 2 * i + 1)

            @block.scalar
            def _(act):
                table_act(act, pieces, 0)
                with repeat(act, DIL_H // 2, (act_q, 24, "dil_act quarters")) as i:
                    dil_act(act, 2 * i)
                    dil_act(act, 2 * i + 1)

            @block.vector
            def _(dve):
                dve.wait_ge(turned_sb, DIL_H)
                with repeat(dve, DIL_H // 2, (dve_q, 24, "dil_dve quarters"), (dve_c, TICKS["dil_dve"], "dil_dve")) as i:
                    dil_dve(dve, 2 * i, 2 * i)
                    dil_dve(dve, 2 * i + 1, 2 * i + 1)

        Q4 = Q3 + 12 * DIL_H
        N4 = DIL_H
        W1Q = 16
        NC2 = NSA_G * N_CMP
        with ExitStack() as c4, nc.Block() as block:
            tab = sb(c4, "nsa_tab", [P, NSA_H, TW_NSA])
            lg, PT = sb(c4, "nsa_lg", [P, TB, SEQ]), sb(c4, "nsa_PT", [P, TB, SEQ])
            qs = [sb(c4, f"nsa_q{g}", [P, SEQ]) for g in range(NSA_G)]
            ob = [sb(c4, f"nsa_ob{g}", [P, SEQ]) for g in range(NSA_G)]
            kT = [[sb(c4, f"nsa_k{br}{g}", [P, SEQ]) for g in range(NSA_G)] for br in range(2)]
            vt = [[sb(c4, f"nsa_v{br}{g}", [P, TB, P]) for g in range(NSA_G)] for br in range(2)]
            cb_hi, cb_lo = sb(c4, "cmp_hi", [P, CMP_LEN, NC2], F32R), sb(c4, "cmp_lo", [P, CMP_LEN, NC2], F32R)
            cb = PT[:].rearrange("p b n -> p (b n)")[:, 0:CMP_LEN * NC2].rearrange("p (l c) -> p l c", l=CMP_LEN)
            pos = sb(c4, "cmp_pos", [P, 2, CMP_LEN])
            w2 = sb(c4, "cmp_w2", [P, 2, 2, HD])
            hm, hmT = sb(c4, "cmp_mid", [NC2, CMP_HID]), sb(c4, "cmp_midT", [P, 2, NC2])
            kc, vc = sb(c4, "k_cmp", [P, NC2]), sb(c4, "v_cmp", [N_CMP, NSA_G, HD])
            lc, PTc = sb(c4, "cmp_lg", [P, NSA_G, TB, N_CMP]), sb(c4, "cmp_PT", [N_CMP, NSA_G, SEQ])
            nm, den = sb(c4, "nsa_nm", [P, TB]), sb(c4, "nsa_den", [P, TB])
            nmc, denc = sb(c4, "cmp_nm", [P, NSA_G, TB]), sb(c4, "cmp_den", [P, NSA_G, TB])
            gs = sb(c4, "nsa_gates", [P, 3 * NSA_G, TB])
            (par4, kv_ev, kv_tr, kv_vt, cb_v, cb_a, cb_l, cm_ps, cm_a, cm_tr, cm_t, cm_k, cm_kv, q_ev, c_s, c_m, c_e,
             c_p, c_t, c_pt, c_o, o_v4) = (sem(f"nsa_{n}") for n in (
                 "par kv_ev kv_tr kv_vt cb_v cb_a cb_l cm_ps cm_a cm_tr cm_t cm_k cm_kv q_ev c_s c_m c_e c_p c_t "
                 "c_pt c_o o_v").split())
            UNITS = 12
            V_UNITS = (5, 7, 9, 11)
            Q_CMP = Q4 + 4 * (UNITS - 3)
            Q_HEAD = Q_CMP + 2 * W1Q + 8

            def nsa_pe(pe, r, last):
                halves = iter([] if last else [(u, j) for u in range(2) for j in range(8)])

                def fill(k):
                    for _ in range(k):
                        uj = next(halves, None)
                        if uj is None:
                            return
                        project_half(pe, *uj)

                pe.wait_ge(q_ev, 2 * r + 2)
                for g in range(NSA_G):
                    for b in range(TB):
                        m = nc.tensor.matmul(W[g][:, b * N_CMP:(b + 1) * N_CMP], qs[g][:, b * P:(b + 1) * P],
                                             kc[:, g * N_CMP:(g + 1) * N_CMP], start=True, stop=True)
                    m.then_inc(c_s, 1)
                fill(2)
                for g in range(NSA_G):
                    pe.wait_ge(c_p, 2 * r + g + 1)
                    for b in range(TB):
                        m = nc.tensor.transpose(W[2 + g][0:N_CMP, b * P:(b + 1) * P], lc[:, g, b, :], ident)
                    m.then_inc(c_t, 1)
                n0 = N4 + 4 * r
                scores(n0, 0, qs[0], kT[0][0])
                scores(n0, 1, qs[0], kT[0][0])
                for g in range(NSA_G):
                    pe.wait_ge(c_pt, 2 * r + g + 1)
                    nc.tensor.matmul(PB[2 + g][:], vc[:, g, :], PTc[:, g, :], start=True, stop=False).then_inc(c_o, 1)
                seq = [(g, br) for g in range(NSA_G) for br in range(2)]
                for i, (g, br) in enumerate(seq):
                    nxt = seq[i + 1] if i < 3 else None
                    attend_pe(pe, n0 + i, kT[br][g], qs[g], vt[br][g], lg, PT, PB[2 + g], False, br == 1, fill,
                              (1, 1, 1, 1) if i else (1, 1, 0, 0),
                              None if nxt is None else (qs[nxt[0]], kT[nxt[1]][nxt[0]]))
                fill(16)

            def nsa_act(act, r, last):
                left = [0 if last else 8]

                def sp_hi(k):
                    k = min(k, left[0])
                    left[0] -= k
                    split_hi(act, k)

                for g in range(NSA_G):
                    for b in range(TB):
                        act.wait_ge(c_m, 2 * r + g + 1)
                        ins = nc.scalar.activation(lc[:, g, b, :], lc[:, g, b, :], ACT.Exp, bias=nmc[:, g, b:b + 1],
                                                   accum_out=denc[:, g, b:b + 1])
                        if b == TB - 1:
                            ins.then_inc(c_e, 1)
                        else:
                            astep(ins)
                sp_hi(1)
                for g in range(NSA_G):
                    act.wait_ge(c_t, 2 * r + g + 1)
                    nc.scalar.activation(PTc[:, g, :], W[2 + g][0:N_CMP, :], ACT.Copy).then_inc(c_pt, 1)
                for i in range(4):
                    attend_act(act, N4 + 4 * r + i, lg, nm, den, PT, i == 0, lambda k: None)
                    sp_hi(2)
                sp_hi(8)

            def nsa_dve(dve, r, last):
                left = [0 if last else 8]

                def sp_lo(k):
                    k = min(k, left[0])
                    left[0] -= k
                    split_lo(dve, k)

                settle(dve)
                for g in range(NSA_G):
                    dve.wait_ge(q_used, Q_HEAD + 8 * r - 4 * (1 - g))
                    nc.vector.tensor_scalar(qs[g][:], PB[g][:], SCALE, None, ALU.mult).then_inc(q_ev, 1)
                    c0 = 3 * (NSA_R * g + r)
                    src = gate[:, c0:c0 + 3, :] if isinstance(r, int) else gate[:, bass.ds(c0, 3), :]
                    step(nc.vector.tensor_copy(gs[:, 3 * g:3 * g + 3, :], src))

                def bias_of(g):
                    hd = NSA_R * g + r

                    def bias(a, e, s=1):
                        if isinstance(hd, int):
                            return tab[:, hd, a:e:s]
                        return tab[:, bass.ds(hd, 1), a:e:s].rearrange("p a n -> p (a n)")
                    return bias

                for g in range(NSA_G):
                    dve.wait_ge(c_s, 2 * r + g + 1)
                    for b in range(TB):
                        a = TW_DIL - P - P * b + CMP_LEN - 1
                        ins = nc.vector.tensor_tensor(lc[:, g, b, :], W[g][:, b * N_CMP:(b + 1) * N_CMP],
                                                      bias_of(g)(a, a + CMP_STRIDE * (N_CMP - 1) + 1, CMP_STRIDE), ALU.add)
                        step(ins)
                    settle(dve)
                    link(dve, nc.vector.tensor_reduce(nmc[:, g, :], lc[:, g], AX.X, ALU.max, negate=True))
                    nc.vector.tensor_scalar(nmc[:, g, :], nmc[:, g, :], BIG / 10, None, ALU.min).then_inc(c_m, 1)
                sp_lo(1)
                for g in range(NSA_G):
                    dve.wait_ge(c_e, 2 * r + g + 1)
                    link(dve, nc.vector.tensor_scalar(denc[:, g, :], denc[:, g, :], 1e-30, None, ALU.max))
                    link(dve, nc.vector.reciprocal(denc[:, g, :], denc[:, g, :]))
                    link(dve, nc.vector.tensor_tensor(denc[:, g, :], denc[:, g, :], gs[:, 3 * g, :], ALU.mult))
                    nc.vector.tensor_tensor(lc[:, g], lc[:, g], bc(denc[:, g, :], N_CMP), ALU.mult).then_inc(c_p, 1)
                for i in range(4):
                    g, br = i // 2, i % 2
                    attend_dve(dve, N4 + 4 * r + i, lg, nm, den, bias_of(g), gs[:, 3 * g + 1 + br, :], i == 0,
                               lambda k: None)
                    sp_lo(2)
                sp_lo(8)
                dve.wait_ge(stored, 16 * (DN_H + DIL_H) + 16 + 32 * r)
                for g in range(NSA_G):
                    dve.wait_ge(att_o, N4 + 4 * r + 2 * g + 2)
                    nc.vector.tensor_copy(ob[g][:], PB[2 + g][:]).then_inc(o_v4, 1)
                dve.wait_ge(o_v4, 2 * r + 2)

            @block.sync
            def _(sp):
                sp.dma_start(pos[:], t["cmp_pos"]).then_inc(par4, 16)
                sp.dma_start(w2[:], t["cmp_w2"]).then_inc(par4, 16)
                table_load(sp, tab, DIL_H, NSA_H, TW_NSA)
                load_units(sp, (Q_HEAD + AHEAD + 3) // 4)
                for r in range(NSA_R):
                    load_units(sp, (Q_HEAD + 8 * min(r + 1, NSA_R - 1) + AHEAD + 3) // 4)
                    for g in range(NSA_G):
                        sp.wait_ge(o_v4, 2 * r + g + 1)
                        sp.dma_start(mix_d[DN_H + DIL_H + NSA_R * g + r, :, :], ob[g][:]).then_inc(stored, 16)
                sp.wait_ge(stored, 16 * KT + 16)

            pieces = table_pieces(tab, NSA_H, TW_NSA)

            @block.tensor
            def _(pe):
                def turn_v(i):
                    pe.wait_ge(kv_ev, V_UNITS[i] + 1)
                    for b in range(TB):
                        m = nc.tensor.transpose(W[i][:, b * P:(b + 1) * P], qs[i % 2][:, b * P:(b + 1) * P], ident)
                    m.then_inc(kv_tr, 1)

                table_pe(pe, pieces, DIL_H, 16 * (DIL_H + NSA_H))
                pe.wait_ge(turned_sb, DIL_H + len(pieces))
                for u in range(3, UNITS):
                    pe.wait_ge(kv_ev, u - 2)
                    for j in range(8):
                        project_half(pe, u % 3, j)
                    if u - 1 in V_UNITS:
                        turn_v(V_UNITS.index(u - 1))
                for i in range(2):
                    pe.wait_ge(cb_l, i + 1)
                    for q in range(W1Q):
                        s = pe_q.n % RING
                        pe.wait_ge(lo_done, pe_q.at(1))
                        for ll in range(2):
                            l = 2 * q + ll
                            for n, (a, b) in enumerate(((cb_hi, w_hi), (cb_lo, w_hi), (cb_hi, w_lo))):
                                m = nc.tensor.matmul(PB[3][0:NC2, i * CMP_HID:(i + 1) * CMP_HID] if i == 0 else
                                                     PB[0][0:NC2, 0:CMP_HID], a[:, l, :],
                                                     b[:, s, ll * CMP_HID:(ll + 1) * CMP_HID],
                                                     start=(l == 0 and n == 0), stop=(l == CMP_LEN - 1 and n == 2))
                        m.then_inc(q_used, 1)
                        pe_q.n += 1
                    if i == 0:
                        turn_v(3)
                for i in range(2):
                    pe.wait_ge(cm_a, i + 1)
                    if i == 0:
                        pe.wait_ge(kv_vt, 4)
                    for hh in range(2):
                        m = nc.tensor.transpose(W[0][:, hh * NC2:(hh + 1) * NC2], hm[:, hh * P:(hh + 1) * P],
                                                cst[0:NC2, K_ID, 0:NC2])
                    m.then_inc(cm_tr, 1)
                    pe.wait_ge(cm_t, i + 1)
                    if i == 0:
                        for hh in range(2):
                            m = nc.tensor.matmul(W[1][:, 0:NC2], w2[:, 0, hh, :], hmT[:, hh, :],
                                                 start=(hh == 0), stop=(hh == 1))
                        m.then_inc(cm_k, 1)
                        pe.wait_ge(cm_a, 2)
                        for u in range(2):
                            for j in range(8):
                                project_half(pe, u, j)
                    else:
                        for g in range(NSA_G):
                            for hh in range(2):
                                m = nc.tensor.matmul(W[2 + g][0:N_CMP, 0:HD], hmT[:, hh, g * N_CMP:(g + 1) * N_CMP],
                                                     w2[:, 1, hh, :], start=(hh == 0), stop=(hh == 1))
                            m.then_inc(cm_k, 1)
                pe.wait_ge(cm_kv, 3)
                with repeat(pe, NSA_R - 1, (pe_q, 8, "nsa_pe quarters")) as r:
                    nsa_pe(pe, r, False)
                nsa_pe(pe, NSA_R - 1, True)

            KV_DST = [lg[:, 0], lg[:, 2], lg[:, 1], lg[:, 3], kT[0][0][:], qs[0][:], kT[0][1][:], qs[1][:],
                      kT[1][0][:], qs[0][:], kT[1][1][:], qs[1][:]]

            @block.scalar
            def _(act):
                table_act(act, pieces, DIL_H)
                for u in range(UNITS):
                    act.wait_ge(q_used, Q4 - 12 + 4 * (u + 1))
                    if u in V_UNITS[2:]:
                        act.wait_ge(kv_tr, V_UNITS.index(u) - 1)
                    nc.scalar.activation(KV_DST[u], PB[u % 3][:], ACT.Copy).then_inc(kv_ev, 1)
                    if u >= 2 and u < UNITS - 1:
                        split_hi(act, 4)
                for i in range(2):
                    act.wait_ge(cb_v, i + 1)
                    if i == 1:
                        act.wait_ge(q_used, Q_CMP + W1Q)
                    nc.scalar.activation(cb_hi[:], cb, ACT.Copy).then_inc(cb_a, 1)
                    split_hi(act, W1Q)
                    act.wait_ge(q_used, Q_CMP + W1Q * (i + 1))
                    if i == 1:
                        act.wait_ge(cm_tr, 1)
                    src = PB[3] if i == 0 else PB[0]
                    nc.scalar.activation(hm[:], src[0:NC2, 0:CMP_HID], ACT.Gelu_apprx_tanh).then_inc(cm_a, 1)
                split_hi(act, 8)
                with repeat(act, NSA_R - 1, (act_q, 8, "nsa_act quarters"), (act_c, TICKS["nsa_act"], "nsa_act")) as r:
                    nsa_act(act, r, False)
                nsa_act(act, NSA_R - 1, True)

            @block.vector
            def _(dve):
                dve.wait_ge(par4, 32)
                def take_v(i):
                    dve.wait_ge(kv_tr, i + 1)
                    nc.vector.tensor_copy(vt[i // 2][i % 2][:].rearrange("p b n -> p (b n)"), W[i][:]).then_inc(kv_vt, 1)

                def blocks(i):
                    for g in range(NSA_G):
                        for a in range(2):
                            src = lg[:, 2 * i + g, CMP_STRIDE * a:CMP_STRIDE * (a + N_CMP)]\
                                .rearrange("p (c l) -> p c l", l=CMP_STRIDE)
                            dst = cb[:, CMP_STRIDE * a:CMP_STRIDE * (a + 1), g * N_CMP:(g + 1) * N_CMP]\
                                .rearrange("p l c -> p c l")
                            pp = pos[:, i, None, CMP_STRIDE * a:CMP_STRIDE * (a + 1)].to_broadcast([P, N_CMP, CMP_STRIDE])
                            ins = nc.vector.tensor_tensor(dst, src, pp, ALU.add)
                            if g == 1 and a == 1:
                                ins.then_inc(cb_v, 1)
                            else:
                                step(ins)

                def blocks_lo(i):
                    dve.wait_ge(cb_a, i + 1)
                    nc.vector.tensor_tensor(cb_lo[:], cb, cb_hi[:].bitcast(F32), ALU.subtract).then_inc(cb_l, 1)

                for u in range(UNITS):
                    dve.wait_ge(kv_ev, u + 1)
                    if u >= 2 and u < UNITS - 1:
                        split_lo(dve, 4)
                    if u == 4:
                        settle(dve)
                        blocks(0)
                    if u in (7, 9, 11):
                        take_v((u - 7) // 2)
                blocks_lo(0)
                split_lo(dve, W1Q)
                dve.wait_ge(cb_l, 1)
                blocks(1)
                take_v(3)
                dve.wait_ge(q_used, Q_CMP + W1Q)
                blocks_lo(1)
                split_lo(dve, W1Q)

                def mid(i):
                    dve.wait_ge(cm_tr, i + 1)
                    nc.vector.tensor_copy(hmT[:].rearrange("p h c -> p (h c)"), W[0][:, 0:2 * NC2]).then_inc(cm_t, 1)

                mid(0)
                dve.wait_ge(cm_k, 1)
                nc.vector.tensor_copy(kc[:], W[1][:, 0:NC2]).then_inc(cm_kv, 1)
                split_lo(dve, 8)
                mid(1)
                for g in range(NSA_G):
                    dve.wait_ge(cm_k, 2 + g)
                    nc.vector.tensor_copy(vc[:, g, :], W[2 + g][0:N_CMP, 0:HD]).then_inc(cm_kv, 1)
                dve.wait_ge(turned_sb, DIL_H + len(pieces))
                with repeat(dve, NSA_R - 1, (dve_q, 8, "nsa_dve quarters"), (dve_c, TICKS["nsa_dve"], "nsa_dve")) as r:
                    nsa_dve(dve, r, False)
                nsa_dve(dve, NSA_R - 1, True)

        CG = D_MODEL // QW
        c5 = ctx.enter_context(ExitStack())
        xs = sb(c5, "xs", [P, TB, D_MODEL])
        xr_in, m_in, m_hi, m_lo, bank_free, wo_ps, wo_v = (
            sem(n) for n in ("xr_in", "mix_in", "mix_hi", "mix_lo", "bank_free", "wo_ps", "wo_v"))
        Q5 = Q_HEAD + 8 * (NSA_R - 1)
        with ExitStack() as c6, nc.Block() as block:
            mraw = sb(c6, "mix_raw", [P, KT, SEQ])

            @block.sync
            def _(sp):
                for i in range(4):
                    sp.dma_start(mraw[:, 4 * i:4 * i + 4, :], mix_d[4 * i:4 * i + 4, :, :].rearrange("k p n -> p k n"))\
                        .then_inc(m_in, 16)
                    sp.wait_ge(m_in, 16 * (i + 1))
                sp.dma_start(xs[:], t["x"].rearrange("(b p) d -> p b d", p=P)).then_inc(xr_in, 16)
                load_units(sp, (Q5 + 16 * CG + AHEAD + 3) // 4)

            @block.tensor
            def _(pe):
                with repeat(pe, CG // 2, (pe_q, 32, "wo_pe quarters")) as i:
                    for c in range(2):
                        for kt in range(KT):
                            s = pe_q.n % RING
                            pe.wait_ge(lo_done, pe_q.at(1))
                            pe.wait_ge(m_lo, kt + 1)
                            for b in range(TB):
                                if kt == 0:
                                    pe.wait_ge(bank_free, 8 * i + 4 * c + b + 1)
                                for n, (x, w) in enumerate(((h_hi, w_hi), (h_lo, w_hi), (h_hi, w_lo))):
                                    m = nc.tensor.matmul(bank[4 * c + b][:], x[:, kt, b * P:(b + 1) * P], w[:, s, :],
                                                         start=(kt == 0 and n == 0), stop=(kt == KT - 1 and n == 2))
                                if kt == KT - 1 and b < TB - 1:
                                    m.then_inc(wo_ps, 1)
                            m.then_inc(q_used, 1)
                            pe_q.n += 1

            @block.scalar
            def _(act):
                for kt in range(KT):
                    act.wait_ge(m_in, 16 * (kt // 4 + 1))
                    nc.scalar.activation(h_hi[:, kt, :], mraw[:, kt, :], ACT.Copy).then_inc(m_hi, 1)
                with repeat(act, CG // 2, (act_q, 32, "wo_act quarters")) as i:
                    split_hi(act, 32)

            @block.vector
            def _(dve):
                dve.sem_inc(bank_free, 8)
                for kt in range(KT):
                    dve.wait_ge(m_hi, kt + 1)
                    nc.vector.tensor_tensor(h_lo[:, kt, :], mraw[:, kt, :], h_hi[:, kt, :].bitcast(F32), ALU.subtract)\
                        .then_inc(m_lo, 1)
                dve.wait_ge(xr_in, 16)
                with repeat(dve, CG // 2, (dve_q, 32, "wo_dve quarters")) as i:
                    for c in range(2):
                        split_lo(dve, KT)
                        for b in range(TB):
                            if b < TB - 1:
                                dve.wait_ge(wo_ps, 6 * i + 3 * c + b + 1)
                            else:
                                dve.wait_ge(q_used, Q5 + 32 * i + 16 * (c + 1))
                            dst = xs[:, b, bass.ds(i * 2 * QW + c * QW, QW)]
                            nc.vector.tensor_tensor(dst, dst, bank[4 * c + b][:], ALU.add).then_inc(bank_free, 1)
                dve.wait_ge(bank_free, 8 + 4 * CG)

        with ExitStack() as c6, nc.Block() as block:
            n2_sp, n2_act, n2_dve, n2_pe, _ = normalize("n2", (lambda e, b: None, None), t["g2"], xs, c6)

            @block.sync
            def _(sp):
                n2_sp(sp)

            @block.scalar
            def _(act):
                n2_act(act)

            @block.vector
            def _(dve):
                n2_dve(dve)

            @block.tensor
            def _(pe):
                n2_pe(pe)

        Q7 = Q5 + 16 * CG
        GQ = 8 * GT + 4 * CG
        with ExitStack() as c7, nc.Block() as block:
            g_hi = sb(c7, "g_hi", [P, 2, GT, SEQ], F32R)
            g_lo = sb(c7, "g_lo", [P, 2, GT, SEQ], F32R)
            cg, cv, gf = (sb(c7, f"ffn_{n}", [P, SEQ]) for n in ("gate", "val", "prod"))
            fw = sb(c7, "ffn_w", [P, 2, 3, FT])
            fwg = sb(c7, "ffn_wg", [P, 2, 3, GT])
            fwd = sb(c7, "ffn_wd", [P, 2, 3, GT])
            fg, squares = sb(c7, "final_g", [P, D_MODEL]), sb(c7, "fin_squares", [P, D_MODEL])
            ss, rs = sb(c7, "fin_ss", [P, TB]), sb(c7, "fin_rs", [P, TB])
            (par7, up_free, tap_a, silu7, prod_v, gh_a, gl_v, dn_free, dn_ps, taps_v, fin_a, fin_v, out_s) = (
                sem(f"ffn_{n}") for n in ("par up_free tap silu prod g_hi g_lo down_free down_ps taps fin_a fin_v "
                                          "out").split())

            def up_pe(pe, g, slot):
                for j in range(GT):
                    for v in range(2):
                        bk = 2 * (j % 2) + v
                        pe.wait_ge(up_free, 8 * g + 2 * j + v + 1)
                        for hh in range(8):
                            project_half(pe, bk, hh)

            def down_pe(pe, g, slot):
                for c in range(CG):
                    for kt in range(GT):
                        s = pe_q.n % RING
                        pe.wait_ge(lo_done, pe_q.at(1))
                        if c == 0:
                            pe.wait_ge(gl_v, 4 * g + kt + 1)
                        for b in range(TB):
                            if kt == 0:
                                pe.wait_ge(dn_free, 16 * g + 4 * c + b + 1)
                            for n, (x, w) in enumerate(((g_hi, w_hi), (g_lo, w_hi), (g_hi, w_lo))):
                                m = nc.tensor.matmul(W[b][:], x[:, slot, kt, b * P:(b + 1) * P], w[:, s, :],
                                                     start=(kt == 0 and n == 0), stop=(kt == GT - 1 and n == 2))
                            if kt == GT - 1 and b < TB - 1:
                                m.then_inc(dn_ps, 1)
                        m.then_inc(q_used, 1)
                        pe_q.n += 1

            def up_act(act, g, slot, q_start):
                for j in range(GT):
                    split_hi(act, 8)
                    for v, dst in ((0, cg), (1, cv)):
                        act.wait_ge(q_used, q_start + 8 * j + 4 * v + 4)
                        if v == 0 and j == 0:
                            act.wait_ge(taps_v, g + 1)
                        if v == 0:
                            act.wait_ge(prod_v, 4 * g + j)
                        nc.scalar.activation(dst[:], PB[2 * (j % 2) + v][:], ACT.Copy, scale=fwg[:, v, 2, j:j + 1])\
                            .then_inc(tap_a, 1)
                    act.wait_ge(up_free, 4 + 8 * g + 2 * j + 1)
                    nc.scalar.activation(cg[:], cg[:], ACT.Silu).then_inc(silu7, 1)
                    act.wait_ge(prod_v, 4 * g + j + 1)
                    nc.scalar.activation(g_hi[:, slot, j, :], gf[:], ACT.Copy).then_inc(gh_a, 1)

            def up_dve(dve, g, slot):
                g4 = g * GT
                for v in range(2):
                    for k in range(3):
                        src = fw[:, v, k, g4:g4 + GT] if isinstance(g, int) else \
                            fw[:, v, k, bass.ds(g4, GT)]
                        ins = nc.vector.tensor_copy(fwg[:, v, k, :], src)
                        if v == 1 and k == 2:
                            ins.then_inc(taps_v, 1)
                        else:
                            step(ins)
                dve.wait_ge(taps_v, g + 1)
                for j in range(GT):
                    split_lo(dve, 8)
                    for v, dst in ((0, cg), (1, cv)):
                        dve.wait_ge(tap_a, 8 * g + 2 * j + v + 1)
                        bk = PB[2 * (j % 2) + v]
                        link(dve, nc.vector.scalar_tensor_tensor(dst[:, 1:SEQ], bk[:, 0:SEQ - 1], fwg[:, v, 1, j:j + 1],
                                                                 dst[:, 1:SEQ], ALU.mult, ALU.add))
                        nc.vector.scalar_tensor_tensor(dst[:, 2:SEQ], bk[:, 0:SEQ - 2], fwg[:, v, 0, j:j + 1],
                                                       dst[:, 2:SEQ], ALU.mult, ALU.add).then_inc(up_free, 1)
                        dve.wait_ge(up_free, 4 + 8 * g + 2 * j + v + 1)
                    dve.wait_ge(silu7, 4 * g + j + 1)
                    dve.wait_ge(gl_v, 4 * g + j)
                    nc.vector.tensor_tensor(gf[:], cg[:], cv[:], ALU.mult).then_inc(prod_v, 1)
                    dve.wait_ge(gh_a, 4 * g + j + 1)
                    nc.vector.tensor_tensor(g_lo[:, slot, j, :], gf[:], g_hi[:, slot, j, :].bitcast(F32), ALU.subtract)\
                        .then_inc(gl_v, 1)

            def down_dve(dve, g, q_start, splits=4 * CG):
                for c in range(CG):
                    split_lo(dve, max(0, min(4, splits - 4 * c)))
                    for b in range(TB):
                        if b < TB - 1:
                            dve.wait_ge(dn_ps, 12 * g + 3 * c + b + 1)
                        else:
                            dve.wait_ge(q_used, q_start + 4 * (c + 1))
                        dve.wait_ge(dn_free, 4 + 16 * g + 4 * c + b)
                        dst = xs[:, b, c * QW:(c + 1) * QW]
                        nc.vector.tensor_tensor(dst, dst, W[b][:], ALU.add).then_inc(dn_free, 1)

            @block.sync
            def _(sp):
                sp.dma_start(fw[:], t["ffn_conv"]).then_inc(par7, 16)
                sp.dma_start(fg[:], t["final_g"]).then_inc(par7, 16)
                load_units(sp, (Q7 + GQ * N_GROUP) // 4)
                for b in range(TB):
                    sp.wait_ge(fin_v, b + 1)
                    sp.dma_start(t["out"][b * P:(b + 1) * P, :], xs[:, b, :]).then_inc(out_s, 16)
                sp.wait_ge(out_s, 16 * TB)

            @block.tensor
            def _(pe):
                up_pe(pe, 0, 0)
                with repeat(pe, N_GROUP // 2, (pe_q, 2 * GQ, "ffn_pe quarters")) as i:
                    up_pe(pe, 2 * i + 1, 1)
                    down_pe(pe, 2 * i, 0)
                    up_pe(pe, 2 * i + 2, 0)
                    down_pe(pe, 2 * i + 1, 1)
                down_pe(pe, N_GROUP - 1, 0)

            UPQ, DNQ = 8 * GT, 4 * CG

            @block.scalar
            def _(act):
                act.wait_ge(par7, 32)
                up_act(act, 0, 0, Q7)
                with repeat(act, N_GROUP // 2, (act_q, 2 * GQ, "ffn_act quarters")) as i:
                    q0 = Q7 + UPQ + 2 * GQ * i
                    up_act(act, 2 * i + 1, 1, q0)
                    split_hi(act, DNQ)
                    up_act(act, 2 * i + 2, 0, q0 + GQ)
                    split_hi(act, DNQ)
                split_hi(act, DNQ - AHEAD)
                act.wait_ge(dn_free, 4 + 16 * N_GROUP)
                for b in range(TB):
                    alink(act, nc.scalar.activation(squares[:], xs[:, b, :], ACT.Square, accum_out=ss[:, b:b + 1]))
                nc.scalar.activation(rs[:], ss[:], ACT.Sqrt, bias=eps_t[:], scale=1.0 / D_MODEL).then_inc(fin_a, 1)

            @block.vector
            def _(dve):
                dve.wait_ge(par7, 32)
                dve.sem_inc(up_free, 4)
                dve.sem_inc(dn_free, 4)
                up_dve(dve, 0, 0)
                with repeat(dve, N_GROUP // 2, (dve_q, 2 * GQ, "ffn_dve quarters"),
                            (dve_c, TICKS["ffn_dve"], "ffn_dve")) as i:
                    q0 = Q7 + UPQ + 2 * GQ * i
                    up_dve(dve, 2 * i + 1, 1)
                    down_dve(dve, 2 * i, q0 + UPQ)
                    up_dve(dve, 2 * i + 2, 0)
                    down_dve(dve, 2 * i + 1, q0 + GQ + UPQ)
                down_dve(dve, N_GROUP - 1, Q7 + GQ * N_GROUP - DNQ, DNQ - AHEAD)
                dve.wait_ge(fin_a, 1)
                link(dve, nc.vector.reciprocal(rs[:], rs[:]))
                for b in range(TB):
                    nc.vector.scalar_tensor_tensor(xs[:, b, :], xs[:, b, :], rs[:, b:b + 1], fg[:], ALU.mult, ALU.mult)\
                        .then_inc(fin_v, 1)


def rel_bucket(dist):
    exact = BUCKETS // 2
    n = np.maximum(dist, 0)
    nf = np.maximum(n, 1).astype(np.float32)
    large = exact + (np.log(nf / np.float32(exact)) / np.float32(math.log(REL_MAX / exact))
                     * np.float32(BUCKETS - exact)).astype(np.int32)
    return np.where(n < exact, n, np.minimum(large, BUCKETS - 1))


def constant_tiles():
    i, j = np.arange(P)[:, None], np.arange(P)[None, :]
    same = i // CHUNK == j // CHUNK

    def level(b):
        return (i // (2 * b) == j // (2 * b)) & ((i // b) % 2 == 1) & ((j // b) % 2 == 0)

    out = np.zeros((P, N_CST, P), np.float32)
    out[:, K_ID] = i == j
    out[:, K_ONE] = 1
    out[:, K_TRI] = same & (i <= j)
    out[:, K_BLK] = same
    out[:, K_ML] = np.where(same & (i > j), 0, BIG)
    out[:, K_MU] = np.where(same & (i <= j), 0, -BIG)
    out[:, K_M1] = level(1)
    out[:, K_REV] = i + j == P - 1
    out[:, K_M1T] = level(1).T
    for n, b in enumerate(LEVELS):
        out[:, K_LV + n] = level(b).T
    return out


def bias_columns():
    d = TW_DIL - 1 - np.arange(YLEN)
    out = np.zeros((BUCKETS + 2, YLEN), np.float32)
    out[rel_bucket(d), np.arange(YLEN)] = d >= 0
    count = (d <= 128).astype(int) + (d % 4 == 0) + (d % 16 == 0)
    ok = (d >= 0) & (count > 0)
    out[BUCKETS] = np.where(ok, np.log(np.where(ok, count, 1)), -BIG)
    out[BUCKETS + 1] = np.where(d >= 0, 0, -BIG)
    return out


def stream(w_in, cmp_w1, w_out, ffn_up, ffn_down):
    units = []

    def columns(w, c):
        units.append(w[:, c:c + P].reshape(KT, P, P).transpose(1, 0, 2).reshape(P, -1))

    def rows(w, r, c):
        units.append(w[r:r + 4 * P, c:c + QW].reshape(4, P, QW).transpose(1, 0, 2).reshape(P, -1))

    dn_w, dil_w = DN_H * HD, DIL_H * HD
    dil0 = 4 * dn_w + 2 * DN_H
    q0 = dil0 + 3 * dil_w
    kv0 = q0 + NSA_H * HD
    for h in range(DN_H):
        for part in range(4):
            columns(w_in, part * dn_w + h * HD)
    for h in range(DIL_H):
        for part in range(3):
            columns(w_in, dil0 + part * dil_w + h * HD)

    def kv(br, which, g):
        columns(w_in, kv0 + ((br * 2 + which) * NSA_G + g) * HD)

    for br in range(3):
        for g in range(NSA_G):
            for which in range(2):
                kv(br, which, g)
    for i in range(2):
        w = cmp_w1[i].reshape(CMP_LEN, P, CMP_HID)
        for l in range(0, CMP_LEN, 8):
            units.append(w[l:l + 8].transpose(1, 0, 2).reshape(P, -1))
    for r in range(NSA_R):
        for g in range(NSA_G):
            columns(w_in, q0 + (g * NSA_R + r) * HD)
    for c in range(0, D_MODEL, QW):
        for r in range(0, D_MODEL, 4 * P):
            rows(w_out, r, c)

    def up(g):
        for j in range(GT):
            for v in range(2):
                columns(ffn_up, v * D_FF + (g * GT + j) * P)

    def down(g):
        for c in range(0, D_MODEL, QW):
            rows(ffn_down, g * GT * P, c)

    up(0)
    for g in range(1, N_GROUP):
        up(g)
        down(g - 1)
    down(N_GROUP - 1)
    return np.stack(units)


def kernel(x, norm1_g, w_in, dn_conv, dn_a_log, dn_dt_bias, dn_norm_g, cmp_pos, cmp_w1, cmp_w2,
           w_out, norm2_g, ffn_up, ffn_conv, ffn_down, rel_bias, final_g):
    import concourse.bacc as bacc
    from concourse.bass_utils import run_bass_kernel_spmd

    x, w = np.asarray(x)[0], np.asarray(w_in)[0]
    small = np.concatenate([w[:, 4 * DN_H * HD:4 * DN_H * HD + 2 * DN_H], w[:, -3 * NSA_H:]], axis=1)
    extra = np.zeros((2, DIL_H + NSA_H), np.float32)
    extra[0, :DIL_H] = 1
    extra[1, DIL_H:] = 1
    arrays = {
        "x": x,
        "weights": stream(w, np.asarray(cmp_w1)[0], np.asarray(w_out)[0], np.asarray(ffn_up)[0],
                          np.asarray(ffn_down)[0]),
        "w_small": small.reshape(KT, P, N_SMALL).transpose(1, 0, 2),
        "ab": np.broadcast_to(np.stack([np.asarray(dn_a_log)[0], np.asarray(dn_dt_bias)[0]])[None], (P, 2, DN_H)),
        "g1": np.asarray(norm1_g)[0].reshape(KT, P).T,
        "g2": np.asarray(norm2_g)[0].reshape(KT, P).T,
        "final_g": np.broadcast_to(np.asarray(final_g)[None], (P, D_MODEL)),
        "dn_conv": np.asarray(dn_conv)[0].reshape(4, 3, DN_H, P).transpose(3, 2, 1, 0),
        "dn_norm": np.asarray(dn_norm_g)[0].reshape(P, 1),
        "cmp_pos": np.asarray(cmp_pos)[0].transpose(2, 0, 1),
        "cmp_w2": np.asarray(cmp_w2)[0].reshape(2, 2, P, HD).transpose(2, 0, 1, 3),
        "ffn_conv": np.asarray(ffn_conv)[0].reshape(3, 2, FT, P).transpose(3, 1, 0, 2),
        "bias_lhs": np.concatenate([np.asarray(rel_bias).T, extra]),
        "cst": constant_tiles(),
        "onehot": bias_columns(),
    }
    arrays = {k: np.ascontiguousarray(a) for k, a in arrays.items()}
    nc = bacc.Bacc("TRN2", target_bir_lowering=False, num_devices=1)
    t = {k: nc.dram_tensor(f"in_{k}", a.shape, mybir.dt.from_np(a.dtype), kind="ExternalInput").ap()
         for k, a in arrays.items()}
    t["out"] = nc.dram_tensor("out", (SEQ, D_MODEL), F32, kind="ExternalOutput").ap()
    program(nc, t)
    r = run_bass_kernel_spmd(nc, [{f"in_{k}": a for k, a in arrays.items()}], core_ids=[0])
    return r.results[0]["out"].reshape(1, SEQ, D_MODEL)
```

```python
import math
from contextlib import ExitStack, contextmanager
from itertools import islice

import numpy as np
import concourse.bass as bass
from concourse import mybir

F32 = mybir.dt.float32
F32R = mybir.dt.float32r
ALU = mybir.AluOpType
ACT = mybir.ActivationFunctionType
AX = mybir.AxisListType

P = 128
SEQ = 512
D_MODEL = 2048
HD = 128
TB = SEQ // P
KT = D_MODEL // P
DN_H, DIL_H, NSA_H, NSA_G = 6, 4, 6, 2
NSA_R = NSA_H // NSA_G
CHUNK = 64
N_CHUNK = SEQ // CHUNK
D_FF = 5632
FT = D_FF // P
GT = 4
N_GROUP = FT // GT
CMP_LEN, CMP_STRIDE, CMP_HID = 32, 16, 256
N_CMP = (SEQ - CMP_LEN) // CMP_STRIDE + 1
BUCKETS, REL_MAX = 32, 2048
EPS = 1e-6
SCALE = HD ** -0.5
BIG = 1e30
FILL_NORM, FILL_A, FILL_AT, FILL_Y, FILL_D, FILL_UW = 11, 5, 4, 2, 3, 3
QW = 512
RING = 8
AHEAD = 4
TW_DIL, TW_NSA = 512, 896
YLEN = 1024
C_G, C_BETA, C_GC, C_BG, C_KD = range(5)
LEVELS = (2, 4, 8, 16, 32)
(K_ID, K_ONE, K_TRI, K_BLK, K_ML, K_MU, K_M1, K_M1T, K_REV) = range(9)
K_LV = 9
N_CST = K_LV + len(LEVELS)
N_SMALL = 2 * DN_H + 3 * NSA_H
TICKS = {"dn_dve": 21, "dn_act": 4, "dil_dve": 16, "nsa_dve": 50, "dil_act": 10, "nsa_act": 6,
         "ffn_dve": 26, "ffn_act": 24}


class Count:

    def __init__(self):
        self.n, self.reg, self.per = 0, None, 0

    def at(self, k=0, div=1, scale=1):
        v = scale * ((self.n + k) // div)
        return v if self.reg is None else self.reg * (scale * self.per // div) + v

    def enter(self, reg, per):
        self.reg, self.per, self.first = reg, per, self.n

    def leave(self, times, what):
        assert self.n - self.first == self.per, (what, self.n - self.first, self.per)
        self.n, self.reg = self.first + self.per * times, None


@contextmanager
def repeat(engine, times, *counts):
    with engine.Fori(0, times) as i:
        for c, per, _ in counts:
            c.enter(i, per)
        yield i
    for c, per, name in counts:
        c.leave(times, name)


def bc(ap, n):
    return ap[:, :, None].to_broadcast([ap.shape[0], ap.shape[1], n])


def program(nc, t):
    with ExitStack() as ctx:
        def sem(name):
            return ctx.enter_context(nc.semaphore(name))

        def sb(c, name, shape, dt=F32):
            return c.enter_context(nc.sbuf_tensor(name, shape, dt))

        h_hi = sb(ctx, "h_hi", [P, KT, SEQ], F32R)
        h_lo = sb(ctx, "h_lo", [P, KT, SEQ], F32R)
        w_raw = sb(ctx, "w_raw", [P, 2, 4 * QW])
        w_hi = sb(ctx, "w_hi", [P, RING, QW], F32R)
        w_lo = sb(ctx, "w_lo", [P, RING, QW], F32R)
        cst = sb(ctx, "cst", [P, N_CST, P])
        eps_t = sb(ctx, "eps_t", [P, 1])
        one_t = sb(ctx, "one_t", [P, 1])
        bank = [ctx.enter_context(nc.psum_tensor(f"bank{i}", [P, QW], F32)) for i in range(8)]
        PB, W = bank[:4], bank[4:]
        ident, ones = cst[:, K_ID, :], cst[:, K_ONE, :]
        mix_d = nc.dram_tensor("mix_scratch", (KT, P, SEQ), F32).ap()
        rev_d = nc.dram_tensor("bias_scratch", (DIL_H + NSA_H, YLEN), F32)

        raw_in = [sem("raw_in_even"), sem("raw_in_odd")]
        hi_done = sem("hi_done")
        lo_done = sem("lo_done")
        q_used = sem("q_used")
        pe_q, act_q, dve_q, sp_u = Count(), Count(), Count(), Count()

        def load_unit(sp):
            if sp_u.n >= 2:
                sp.wait_ge(lo_done, sp_u.at(-1, scale=4))
            u = sp_u.at()
            s = sp_u.n % 2
            src = t["weights"][u, :, :] if sp_u.reg is None else t["weights"][bass.ds(u, 1), :, :]
            if sp_u.reg is not None:
                src = src.rearrange("u p n -> p (u n)")
            sp.dma_start(w_raw[:, s, :], src).then_inc(raw_in[s], 16)
            sp_u.n += 1

        def load_units(sp, last):
            if sp_u.n < 2:
                load_unit(sp)
                load_unit(sp)
            if sp_u.n % 2 and sp_u.n < last:
                load_unit(sp)
            pairs = (last - sp_u.n) // 2
            if pairs > 0:
                with repeat(sp, pairs, (sp_u, 2, "units")):
                    load_unit(sp)
                    load_unit(sp)
            if sp_u.n < last:
                load_unit(sp)

        def raw_quarter(c):
            return w_raw[:, (c.n // 4) % 2, (c.n % 4) * QW:(c.n % 4 + 1) * QW]

        def split_hi(act, n=1):
            for _ in range(n):
                act.wait_ge(raw_in[(act_q.n // 4) % 2], act_q.at(8, div=8, scale=16))
                if act_q.n >= RING:
                    act.wait_ge(q_used, act_q.at(1 - RING))
                nc.scalar.activation(w_hi[:, act_q.n % RING, :], raw_quarter(act_q), ACT.Copy)\
                    .then_inc(hi_done, 1)
                act_q.n += 1

        def split_lo(dve, n=1):
            for _ in range(n):
                dve.wait_ge(hi_done, dve_q.at(1))
                s = dve_q.n % RING
                nc.vector.tensor_tensor(w_lo[:, s, :], raw_quarter(dve_q), w_hi[:, s, :].bitcast(F32),
                                        ALU.subtract).then_inc(lo_done, 1)
                dve_q.n += 1

        dve_chain, act_chain = sem("dve_chain"), sem("act_chain")
        dve_c, act_c = Count(), Count()

        def step(ins):
            ins.then_inc(dve_chain, 1)
            dve_c.n += 1

        def settle(dve):
            dve.wait_ge(dve_chain, dve_c.at())

        def link(dve, ins):
            step(ins)
            settle(dve)

        def astep(ins):
            ins.then_inc(act_chain, 1)
            act_c.n += 1

        def asettle(act):
            act.wait_ge(act_chain, act_c.at())

        def alink(act, ins):
            astep(ins)
            asettle(act)

        def project(pe, pb, kt):
            s = pe_q.n % RING
            if kt % 4 == 0:
                pe.wait_ge(lo_done, pe_q.at(1))
            k = slice(kt % 4 * P, (kt % 4 + 1) * P)
            for n, (a, b) in enumerate(((w_hi, h_hi), (w_lo, h_hi), (w_hi, h_lo))):
                m = nc.tensor.matmul(PB[pb][:], a[:, s, k], b[:, kt, :],
                                     start=(kt == 0 and n == 0), stop=(kt == KT - 1 and n == 2))
            if kt % 4 == 3:
                m.then_inc(q_used, 1)
                pe_q.n += 1

        def filler(pe, units, before=None):
            steps = iter([(u, kt) for u in range(units) for kt in range(KT)])

            def fill(n):
                for u, kt in islice(steps, n):
                    if kt == 0 and before is not None:
                        before(u)
                    project(pe, u, kt)
            return fill

        tok = sb(ctx, "tok", [P, DN_H, 5, TB])
        gate = sb(ctx, "gate", [P, 3 * NSA_H, TB])
        in_small = sem("in_small")
        const_in, table_in = sem("const_in"), sem("table_in")
        stored = sem("stored")

        def normalize(name, x_ready, g_dram, xs, c1, ident):
            sq, y = sb(c1, f"{name}_sq", [P, D_MODEL]), sb(c1, f"{name}_y", [P, 2, D_MODEL])
            ss, rs = sb(c1, f"{name}_ss", [P, TB]), sb(c1, f"{name}_rs", [P, TB])
            g_row = sb(c1, f"{name}_g", [P, D_MODEL])
            g_in, sums, root, y_v, turned, hi, lo = (
                sem(f"{name}_{k}") for k in ("g_in", "sums", "root", "y", "turned", "hi", "lo"))
            parts = [(b, kg) for b in range(TB) for kg in range(KT // 4)]

            def h_part(h, i):
                b, kg = parts[i]
                return h[:, 4 * kg:4 * kg + 4, b * P:(b + 1) * P]

            def psum_part(i):
                return PB[i % 4][:].rearrange("p (k n) -> p k n", k=4)

            def sp_part(sp):
                sp.dma_start(g_row[:], g_dram).then_inc(g_in, 16)

            def act_part(act):
                def root_of(b):
                    x_ready(act, b)
                    if b:
                        act.wait_ge(sums, b)
                    nc.scalar.activation(sq[:], xs[:, b, :], ACT.Square, accum_out=ss[:, b:b + 1]).then_inc(sums, 1)
                    act.wait_ge(sums, b + 1)
                    nc.scalar.activation(rs[:, b:b + 1], ss[:, b:b + 1], ACT.Sqrt, bias=eps_t[:],
                                         scale=1.0 / D_MODEL).then_inc(root, 1)

                root_of(0)
                root_of(1)
                for i, (b, kg) in enumerate(parts):
                    if kg == 0 and b + 2 < TB:
                        root_of(b + 2)
                    act.wait_ge(turned, i + 1)
                    nc.scalar.activation(h_part(h_hi, i), psum_part(i), ACT.Copy).then_inc(hi, 1)

            def dve_part(dve):
                def scaled(b):
                    dve.wait_ge(root, b + 1)
                    link(dve, nc.vector.reciprocal(rs[:, b:b + 1], rs[:, b:b + 1]))
                    if b >= 2:
                        dve.wait_ge(turned, 4 * (b - 1))
                    nc.vector.scalar_tensor_tensor(y[:, b % 2, :], xs[:, b, :], rs[:, b:b + 1], g_row[:],
                                                   ALU.mult, ALU.mult).then_inc(y_v, 1)

                dve.wait_ge(g_in, 16)
                scaled(0)
                scaled(1)
                for i, (b, kg) in enumerate(parts):
                    if kg == 0 and 1 <= b < TB - 1:
                        scaled(b + 1)
                    dve.wait_ge(hi, i + 1)
                    nc.vector.tensor_tensor(h_part(h_lo, i), psum_part(i), h_part(h_hi, i).bitcast(F32), ALU.subtract)\
                        .then_inc(lo, 1)

            def pe_part(pe, between=lambda b: None):
                for i, (b, kg) in enumerate(parts):
                    if kg == 0:
                        pe.wait_ge(y_v, b + 1)
                    if i >= 4:
                        pe.wait_ge(lo, i - 3)
                    for k in range(4):
                        kt = 4 * kg + k
                        m = nc.tensor.transpose(PB[i % 4][:, k * P:(k + 1) * P], y[:, b % 2, kt * P:(kt + 1) * P],
                                                ident)
                    m.then_inc(turned, 1)
                    if kg == 3:
                        between(b)

            return sp_part, act_part, dve_part, pe_part, lo

        toep_d = nc.dram_tensor("toeplitz_scratch", (DIL_H + NSA_H, P, TW_NSA), F32).ap()
        PIECES = [(h, 0, QW) for h in range(DIL_H + NSA_H)] + [(h, QW, TW_NSA - QW) for h in range(DIL_H, DIL_H + NSA_H)]
        ROUNDS = (PIECES[:8], PIECES[8:])

        with ExitStack() as c1, nc.Block() as block:
            xs = sb(c1, "xs1", [P, TB, D_MODEL])
            bl, oh = sb(c1, "bias_lhs", [BUCKETS + 2, DIL_H + NSA_H]), sb(c1, "onehot", [BUCKETS + 2, YLEN])
            rev = oh[0:DIL_H + NSA_H, :]
            tq = sb(c1, "toeplitz_pieces", [P, 8, QW])
            id1 = sb(c1, "ident_first", [P, P])
            x_in = [sem(f"x_in{b}") for b in range(TB)]
            const_ready, id_in, bias_in, rev_ps, rev_sb, piece_ps, piece_sb = (
                sem(n) for n in ("const_ready", "id_in", "bias_in", "rev_ps", "rev_sb", "piece_ps", "piece_sb"))
            n1_sp, n1_act, n1_dve, n1_pe, n1_lo = normalize(
                "n1", lambda e, b: e.wait_ge(x_in[b], 16), t["g1"], xs, c1, id1[:])

            @block.sync
            def _(sp):
                sp.dma_start(bl[:], t["bias_lhs"]).then_inc(bias_in, 16)
                sp.dma_start(oh[:], t["onehot"]).then_inc(bias_in, 16)
                sp.dma_start(xs[:, 0, :], t["x"][0:P, :]).then_inc(x_in[0], 16)
                n1_sp(sp)
                sp.dma_start(id1[:], t["cst"][:, K_ID, :]).then_inc(id_in, 16)
                sp.dma_start(xs[:, 1, :], t["x"][P:2 * P, :]).then_inc(x_in[1], 16)
                sp.dma_start(cst[:], t["cst"]).then_inc(const_in, 16)
                for b in range(2, TB):
                    sp.dma_start(xs[:, b, :], t["x"][b * P:(b + 1) * P, :]).then_inc(x_in[b], 16)
                sp.wait_ge(rev_sb, 1)
                sp.dma_start(rev_d.ap()[:, :], rev).then_inc(stored, 16)
                sp.wait_ge(stored, 16)
                for r, pieces in enumerate(ROUNDS):
                    if r:
                        sp.wait_ge(stored, 16 + 16 * 8)
                    for i, (h, c, w) in enumerate(pieces):
                        sp.dma_start(tq[:, i, 0:w], bass.AP(tensor=rev_d, offset=h * YLEN + c, ap=[[1, P], [1, w]]))\
                            .then_inc(table_in, 16)
                    if r == 0:
                        load_units(sp, 2)
                    for i, (h, c, w) in enumerate(pieces):
                        sp.wait_ge(piece_sb, 8 * r + i + 1)
                        sp.dma_start(toep_d[h, :, c:c + w], tq[:, i, 0:w]).then_inc(stored, 16)
                sp.wait_ge(stored, 16 + 16 * len(PIECES))

            @block.gpsimd
            def _(pool):
                nc.gpsimd.memset(eps_t[:], EPS).then_inc(const_ready, 1)
                nc.gpsimd.memset(one_t[:], 1.0).then_inc(const_ready, 1)

            @block.scalar
            def _(act):
                act.wait_ge(const_ready, 2)
                n1_act(act)
                split_hi(act, AHEAD)

            @block.vector
            def _(dve):
                dve.wait_ge(rev_ps, 1)
                step(nc.vector.tensor_copy(rev[:, 0:512], W[0][0:DIL_H + NSA_H, :]))
                nc.vector.tensor_copy(rev[:, 512:1024], W[1][0:DIL_H + NSA_H, :]).then_inc(rev_sb, 1)
                n1_dve(dve)
                split_lo(dve, AHEAD)
                for i, (h, c, w) in enumerate(PIECES):
                    dve.wait_ge(piece_ps, i + 1)
                    nc.vector.tensor_copy(tq[:, i % 8, 0:w], W[i % 4][:, 0:w]).then_inc(piece_sb, 1)

            @block.tensor
            def _(pe):
                pe.wait_ge(bias_in, 32)
                for i in range(2):
                    m = nc.tensor.matmul(W[i][0:DIL_H + NSA_H, :], bl[:], oh[:, i * 512:(i + 1) * 512],
                                         start=True, stop=True)
                m.then_inc(rev_ps, 1)
                pe.wait_ge(id_in, 16)
                n1_pe(pe)
                pe.wait_ge(const_in, 16)
                pe.wait_ge(rev_sb, 1)
                for i, (h, c, w) in enumerate(PIECES):
                    if i % 8 == 0:
                        pe.wait_ge(table_in, 16 * (i + 8))
                    if i >= 4:
                        pe.wait_ge(piece_sb, i - 3)
                    nc.tensor.matmul(W[i % 4][:, 0:w], cst[:, K_REV, :], tq[:, i % 8, 0:w], start=True, stop=True)\
                        .then_inc(piece_ps, 1)

        STORED2 = 16 + 16 * len(PIECES)

        with ExitStack() as c2, nc.Block() as block:
            names = ("gb qp kp vp zs qT kT kbg kdec vb m1 D DT EG qg A AT T U Y attnT u wT vn sk osc ob").split()
            B = {n: sb(c2, f"dn_{n}", [P, SEQ]) for n in names}
            LT = sb(c2, "dn_LT", [P, len(LEVELS), SEQ])
            S = sb(c2, "dn_S", [P, P])
            hp, hg, cw = sb(c2, "dn_hp", [P, 5, TB]), sb(c2, "dn_hg", [P, TB]), sb(c2, "dn_cw", [P, 3, 4])
            cwa = sb(c2, "dn_cwa", [P, DN_H, 3, 4])
            ng = sb(c2, "dn_ng", [P, 1])
            ssq, rms = sb(c2, "dn_ssq", [P, TB]), sb(c2, "dn_rms", [P, TB])
            trash = sb(c2, "dn_trash", [P, P])
            sw = sb(c2, "small_raw", [P, KT, N_SMALL])
            sw_hi = sb(c2, "small_hi", [P, KT, N_SMALL], F32R)
            sw_lo = sb(c2, "small_lo", [P, KT, N_SMALL], F32R)
            st, sk = sb(c2, "small_t", [N_SMALL, SEQ]), sb(c2, "small_tok", [P, TB, N_SMALL])
            ab = sb(c2, "a_log_bc", [P, 2, DN_H])
            xa, ax, gr, gt, eb = (sb(c2, f"gate_{n}", [P, DN_H, TB]) for n in ("xa", "ax", "gr", "gt", "eb"))
            ps_small, sm_hi, sm_lo, sm_t, sm_tp, sm_tok, g_e, g_a, g_cum, g_ok = (
                sem(n) for n in ("ps_small sm_hi sm_lo sm_t sm_tp sm_tok g_exp g_act g_cum g_ok").split())

            def v3(ap):
                return ap.rearrange("p (b n) -> p b n", b=TB)

            def c3b(k):
                return cst[:, k:k + 1, :].to_broadcast([P, TB, P])

            par_in = sem("dn_par_in")
            (g_rep, grow_ps, conv_v, z_free, silu_a, sqr_a, norm_ps, root_a, qk_n, tr_ps, tr_used, masks_v, decay_a,
             kk_ps, qk_ps, a_v, at_ps, at_a, lt_g, t_v, u_v, y_ps, y_a, d_ps, uw_ps, uw_a, ready_v, v_ps, vn_v,
             s_ps, s_v, o_a, osc_v, o_ps, o_v) = (
                sem(f"dn_{n}") for n in (
                    "g_rep grow_ps conv_v z_free silu_a sqr_a norm_ps root_a qk_n tr_ps tr_used masks_v decay_a "
                    "kk_ps qk_ps a_v at_ps at_a lt_g t_v u_v y_ps y_a d_ps uw_ps uw_a ready_v v_ps vn_v "
                    "s_ps s_v o_a osc_v o_ps o_v").split())
            NL = len(LEVELS)

            def small_pe(pe):
                pe.wait_ge(sm_lo, 1)
                for kt in range(KT):
                    for n, (a, b) in enumerate(((sw_hi, h_hi), (sw_lo, h_hi), (sw_hi, h_lo))):
                        m = nc.tensor.matmul(W[0][0:N_SMALL, :], a[:, kt, :], b[:, kt, :],
                                             start=(kt == 0 and n == 0), stop=(kt == KT - 1 and n == 2))
                m.then_inc(ps_small, 1)

            def small_turn_pe(pe):
                pe.wait_ge(sm_t, 1)
                for b in range(TB):
                    m = nc.tensor.transpose(W[1][:, b * 32:b * 32 + N_SMALL], st[:, b * P:(b + 1) * P],
                                            cst[0:N_SMALL, K_ID, 0:N_SMALL])
                m.then_inc(sm_tp, 1)

            def cumulate_pe(pe):
                pe.wait_ge(g_ok, 1)
                flat = gr[:].rearrange("p h b -> p (h b)")
                nc.tensor.matmul(W[2][:, 0:DN_H * TB], cst[:, K_TRI, :], flat, start=True, stop=True)
                nc.tensor.matmul(W[3][:, 0:DN_H * TB], cst[:, K_BLK, :], flat, start=True, stop=True).then_inc(g_cum, 1)

            def small_act(act):
                act.wait_ge(ps_small, 1)
                nc.scalar.activation(st[:], W[0][0:N_SMALL, :], ACT.Copy).then_inc(sm_t, 1)
                split_hi(act, 3)
                act.wait_ge(sm_tok, 2)
                astep(nc.scalar.activation(eb[:], sk[:, :, 0:DN_H].rearrange("p b h -> p h b"), ACT.Exp,
                                           scale=-1.0))
                astep(nc.scalar.activation(gate[:], sk[:, :, 2 * DN_H:].rearrange("p b c -> p c b"), ACT.Exp,
                                           scale=-1.0))
                astep(nc.scalar.activation(ab[:, 0, :], ab[:, 0, :], ACT.Exp))
                alink(act, nc.scalar.activation(ax[:], xa[:], ACT.Abs))
                alink(act, nc.scalar.activation(ax[:], ax[:], ACT.Exp, scale=-1.0))
                nc.scalar.activation(ax[:], ax[:], ACT.Ln, bias=one_t[:]).then_inc(g_a, 1)
                split_hi(act, 3)
                act.wait_ge(g_ok, 2)
                nc.scalar.activation(tok[:, :, C_BG, :], tok[:, :, C_GC, :], ACT.Exp).then_inc(g_e, 1)
                nc.scalar.activation(tok[:, :, C_KD, :], gt[:], ACT.Exp).then_inc(g_e, 1)

            def small_dve(dve):
                split_lo(dve, 3)
                dve.wait_ge(sm_tp, 1)
                nc.vector.tensor_copy(sk[:], W[1][:, 0:TB * 32].rearrange("p (b c) -> p b c", b=TB)[:, :, 0:N_SMALL])\
                    .then_inc(sm_tok, 1)
                dve.wait_ge(sm_tok, 1)
                nc.vector.tensor_tensor(xa[:], sk[:, :, DN_H:2 * DN_H].rearrange("p b h -> p h b"),
                                        bc(ab[:, 1, :], TB), ALU.add).then_inc(sm_tok, 1)
                dve.wait_ge(g_a, 1)
                link(dve, nc.vector.tensor_scalar(eb[:], eb[:], 1.0, None, ALU.add))
                step(nc.vector.reciprocal(tok[:, :, C_BETA, :], eb[:]))
                link(dve, nc.vector.tensor_scalar(gate[:], gate[:], 1.0, None, ALU.add))
                step(nc.vector.reciprocal(gate[:], gate[:]))
                link(dve, nc.vector.scalar_tensor_tensor(gr[:], xa[:], 0.0, ax[:], ALU.max, ALU.add))
                link(dve, nc.vector.scalar_tensor_tensor(gr[:], gr[:], -1.0, bc(ab[:, 0, :], TB), ALU.mult, ALU.mult))
                nc.vector.tensor_copy(tok[:, :, C_G, :], gr[:]).then_inc(g_ok, 1)
                split_lo(dve, 3)
                dve.wait_ge(g_cum, 1)
                link(dve, nc.vector.tensor_copy(tok[:, :, C_GC, :], W[2][:, 0:DN_H * TB].rearrange("p (h b) -> p h b", h=DN_H)))
                nc.vector.tensor_tensor(gt[:], W[3][:, 0:DN_H * TB].rearrange("p (h b) -> p h b", h=DN_H),
                                        tok[:, :, C_GC, :], ALU.subtract).then_inc(g_ok, 1)
                dve.wait_ge(g_e, 2)
                link(dve, nc.vector.tensor_tensor(tok[:, :, C_BG, :], tok[:, :, C_BG, :], tok[:, :, C_BETA, :], ALU.mult))

            def dn_pe(pe, h, next_units):
                def bank_read(u):
                    if u < 3:
                        pe.wait_ge(conv_v, 3 * h + u + 1)
                    else:
                        pe.wait_ge(z_free, h + 1)

                fill = filler(pe, next_units, bank_read)
                pe.wait_ge(sqr_a, 2 * h + 2)
                pe.wait_ge(o_v, h + 1)
                nc.tensor.matmul(W[1][:], ones, B["Y"][:], start=True, stop=True).then_inc(norm_ps, 1)
                nc.tensor.matmul(W[2][:], ones, B["sk"][:], start=True, stop=True).then_inc(norm_ps, 1)
                pe.wait_ge(g_rep, h + 1)
                for b in range(TB):
                    m = nc.tensor.matmul(W[0][:, b * P:(b + 1) * P], B["gb"][:, b * P:(b + 1) * P],
                                         cst[:, K_TRI, :], start=True, stop=True)
                m.then_inc(grow_ps, 1)
                pe.wait_ge(silu_a, 3 * h + 3)
                for b in range(TB):
                    m = nc.tensor.transpose(W[3][:, b * P:(b + 1) * P], B["vp"][:, b * P:(b + 1) * P], ident)
                m.then_inc(tr_ps, 1)
                fill(FILL_NORM)
                pe.wait_ge(qk_n, 2 * h + 2)
                for b in range(TB):
                    m = nc.tensor.matmul(W[2][:, b * P:(b + 1) * P], B["kT"][:, b * P:(b + 1) * P],
                                         B["kT"][:, b * P:(b + 1) * P], start=True, stop=True)
                m.then_inc(kk_ps, 1)
                for b in range(TB):
                    m = nc.tensor.transpose(W[1][:, b * P:(b + 1) * P], B["kT"][:, b * P:(b + 1) * P], ident)
                m.then_inc(tr_ps, 1)
                pe.wait_ge(tr_used, 2 * h + 1)
                for b in range(TB):
                    m = nc.tensor.matmul(W[3][:, b * P:(b + 1) * P], B["kT"][:, b * P:(b + 1) * P],
                                         B["qT"][:, b * P:(b + 1) * P], start=True, stop=True)
                m.then_inc(qk_ps, 1)
                fill(FILL_A)
                pe.wait_ge(a_v, h + 1)
                pe.wait_ge(decay_a, 3 * h + 1)
                for b in range(TB):
                    m = nc.tensor.transpose(W[0][:, b * P:(b + 1) * P], B["A"][:, b * P:(b + 1) * P], ident)
                m.then_inc(at_ps, 1)
                fill(FILL_AT)
                for lv in range(NL):
                    pe.wait_ge(lt_g, NL * h + lv + 1)
                    pe.wait_ge(t_v, NL * h + lv + 1)
                    if lv == 0:
                        pe.wait_ge(tr_used, 2 * h + 2)
                    for b in range(TB):
                        c = slice(b * P, (b + 1) * P)
                        m = nc.tensor.matmul(W[1][:, c], LT[:, lv, c], B["T"][:, c], start=True, stop=True)
                    m.then_inc(y_ps, 1)
                    fill(FILL_Y)
                    pe.wait_ge(y_a, NL * h + lv + 1)
                    pe.wait_ge(u_v, (NL + 1) * h + lv + 1)
                    if lv == 0:
                        pe.wait_ge(ready_v, 2 * h + 1)
                    if lv < NL - 1:
                        for b in range(TB):
                            c = slice(b * P, (b + 1) * P)
                            m = nc.tensor.matmul(W[2][:, c], B["U"][:, c], B["Y"][:, c], start=True, stop=True)
                        m.then_inc(d_ps, 1)
                    for b in range(TB):
                        c = slice(b * P, (b + 1) * P)
                        m = nc.tensor.matmul(W[3][:, c], B["Y"][:, c], B["U"][:, c], start=True, stop=True)
                    m.then_inc(d_ps, 1)
                    fill(FILL_D)
                pe.wait_ge(u_v, (NL + 1) * h + NL + 1)
                for b in range(TB):
                    c = slice(b * P, (b + 1) * P)
                    m = nc.tensor.matmul(W[2][:, c], B["kbg"][:, c], B["U"][:, c], start=True, stop=True)
                m.then_inc(uw_ps, 1)
                for b in range(TB):
                    c = slice(b * P, (b + 1) * P)
                    m = nc.tensor.matmul(W[1][:, c], B["U"][:, c], B["vb"][:, c], start=True, stop=True)
                m.then_inc(uw_ps, 1)
                fill(FILL_UW)
                for c in range(N_CHUNK):
                    b, o = c // 2, CHUNK * (c % 2)
                    rows, cc = slice(o, o + CHUNK), slice(c * CHUNK, (c + 1) * CHUNK)
                    cb = slice(b * P, (b + 1) * P)
                    if c == 0:
                        pe.wait_ge(uw_a, 2 * h + 2)
                        pe.wait_ge(ready_v, 2 * h + 2)
                    pe.wait_ge(s_v, (N_CHUNK + 1) * h + c + 1)
                    nc.tensor.matmul(W[1][rows, cb], B["wT"][:, cc], S[:], start=True, stop=True)\
                        .then_inc(v_ps, 1)
                    nc.tensor.matmul(W[3][rows, cb], B["qg"][:, cc], S[:], start=True, stop=False)
                    fill(1)
                    pe.wait_ge(vn_v, N_CHUNK * h + c + 1)
                    nc.tensor.matmul(W[2][:, 0:P], B["kdec"][rows, cb], B["vn"][rows, cb],
                                     start=True, stop=True).then_inc(s_ps, 1)
                    nc.tensor.matmul(W[3][rows, cb], B["attnT"][rows, cc.start:cc.stop],
                                     B["vn"][rows, cb], start=False, stop=True).then_inc(s_ps, 1)
                    if c % 2:
                        fill(1)
                fill(1000)
                pe.wait_ge(osc_v, h + 1)
                for b in range(TB):
                    m = nc.tensor.transpose(W[1][:, b * P:(b + 1) * P], B["osc"][:, b * P:(b + 1) * P], ident)
                m.then_inc(o_ps, 1)

            def silu_part(act, h):
                for i, n in enumerate(("qp", "kp", "vp")):
                    act.wait_ge(conv_v, 3 * h + i + 1)
                    nc.scalar.activation(B[n][:], B[n][:], ACT.Silu).then_inc(silu_a, 1)
                    act.wait_ge(silu_a, 3 * h + i + 1)
                    if i < 2:
                        nc.scalar.activation(B[("Y", "sk")[i]][:], B[n][:], ACT.Square).then_inc(sqr_a, 1)

            def of_head(table, h):
                if isinstance(h, int):
                    return table[:, h]
                return table[:, bass.ds(h, 1)].rearrange("p a c b -> p (a c) b")

            def conv_steps(dve, h):
                step(nc.vector.tensor_copy(hg[:], of_head(tok, h)[:, C_G, :]))
                link(dve, nc.vector.tensor_copy(cw[:], of_head(cwa, h)))
                nc.vector.tensor_copy(v3(B["gb"][:]), bc(hg[:], P)).then_inc(g_rep, 1)
                yield
                for i, n in enumerate(("qp", "kp", "vp")):
                    dve.wait_ge(q_used, 16 * h + 4 * i + 4)
                    step(nc.vector.tensor_scalar(B[n][:], PB[i][:], cw[:, i, 3:4], None, ALU.mult))
                    yield
                    for k in (1, 2, 3):
                        settle(dve)
                        ins = nc.vector.scalar_tensor_tensor(
                            B[n][:, k:SEQ], PB[i][:, 0:SEQ - k], cw[:, i, 3 - k:4 - k], B[n][:, k:SEQ],
                            ALU.mult, ALU.add)
                        if k < 3:
                            step(ins)
                        else:
                            ins.then_inc(conv_v, 1)
                        yield

            def dn_act(act, h, splits, last):
                left = [splits]

                def sp_hi(n):
                    n = min(n, left[0])
                    left[0] -= n
                    split_hi(act, n)

                for i, n in enumerate(("A", "AT")):
                    act.wait_ge(norm_ps, 2 * h + i + 1)
                    nc.scalar.activation(B[n][:], W[1 + i][:], ACT.Sqrt, bias=eps_t[:]).then_inc(root_a, 1)
                sp_hi(2)
                act.wait_ge(masks_v, h + 1)
                nc.scalar.activation(B["EG"][:], W[0][:], ACT.Exp).then_inc(decay_a, 1)
                nc.scalar.activation(B["D"][:], B["D"][:], ACT.Exp, scale=-1.0).then_inc(decay_a, 1)
                nc.scalar.activation(B["DT"][:], B["DT"][:], ACT.Exp).then_inc(decay_a, 1)
                sp_hi(2)
                act.wait_ge(q_used, 16 * h + 16)
                nc.scalar.activation(B["zs"][:], PB[3][:], ACT.Silu).then_inc(z_free, 1)
                act.wait_ge(at_ps, h + 1)
                nc.scalar.activation(B["AT"][:], W[0][:], ACT.Copy).then_inc(at_a, 1)
                sp_hi(2)
                for lv in range(NL):
                    act.wait_ge(y_ps, NL * h + lv + 1)
                    nc.scalar.activation(B["Y"][:], W[1][:], ACT.Copy).then_inc(y_a, 1)
                    sp_hi(1)
                for i, n in enumerate(("wT", "u")):
                    act.wait_ge(uw_ps, 2 * h + i + 1)
                    nc.scalar.activation(B[n][:], W[2 - i][:], ACT.Copy).then_inc(uw_a, 1)
                sp_hi(16)
                if not last:
                    silu_part(act, h + 1)
                act.wait_ge(s_ps, 2 * N_CHUNK * (h + 1))
                for b in range(TB):
                    alink(act, nc.scalar.activation(trash[:], W[3][:, b * P:(b + 1) * P], ACT.Square,
                                                    accum_out=ssq[:, b:b + 1]))
                nc.scalar.activation(rms[:], ssq[:], ACT.Sqrt, bias=eps_t[:], scale=1.0 / HD).then_inc(o_a, 1)
                act.wait_ge(o_a, h + 1)

            def dn_dve(dve, h, splits, last):
                left = [splits]

                def sp_lo(n):
                    n = min(n, left[0])
                    left[0] -= n
                    split_lo(dve, n)

                link(dve, nc.vector.tensor_copy(hp[:], of_head(tok, h)))
                for i, (r, src, dst, sc) in enumerate((("A", "qp", "qT", SCALE), ("AT", "kp", "kT", 1.0))):
                    dve.wait_ge(root_a, 2 * h + i + 1)
                    link(dve, nc.vector.reciprocal(B[r][:], B[r][:]))
                    nc.vector.scalar_tensor_tensor(B[dst][:], B[src][:], sc, B[r][:], ALU.mult, ALU.mult)\
                        .then_inc(qk_n, 1)
                dve.wait_ge(grow_ps, h + 1)
                link(dve, nc.vector.tensor_tensor(v3(B["m1"][:]), v3(W[0][:]), bc(hp[:, C_GC, :], P), ALU.subtract))
                step(nc.vector.tensor_tensor(v3(B["D"][:]), v3(B["m1"][:]), c3b(K_ML), ALU.add))
                nc.vector.tensor_tensor(v3(B["DT"][:]), v3(B["m1"][:]), c3b(K_MU), ALU.add).then_inc(masks_v, 1)
                dve.wait_ge(tr_ps, 2 * h + 1)
                nc.vector.tensor_tensor(v3(B["vb"][:]), v3(W[3][:]), bc(hp[:, C_BETA, :], P), ALU.mult)\
                    .then_inc(tr_used, 1)
                dve.wait_ge(kk_ps, h + 1)
                dve.wait_ge(decay_a, 3 * h + 2)
                dve.wait_ge(qk_n, 2 * h + 2)
                link(dve, nc.vector.tensor_tensor(B["A"][:], W[2][:], B["D"][:], ALU.mult))
                nc.vector.tensor_tensor(v3(B["A"][:]), v3(B["A"][:]), bc(hp[:, C_BETA, :], P), ALU.mult)\
                    .then_inc(a_v, 1)
                dve.wait_ge(a_v, h + 1)
                link(dve, nc.vector.tensor_tensor(v3(B["T"][:]), v3(B["A"][:]), c3b(K_M1), ALU.mult))
                nc.vector.tensor_tensor(v3(B["T"][:]), c3b(K_ID), v3(B["T"][:]), ALU.subtract).then_inc(t_v, 1)
                dve.wait_ge(tr_ps, 2 * h + 2)
                step(nc.vector.tensor_tensor(v3(B["kbg"][:]), v3(W[1][:]), bc(hp[:, C_BG, :], P), ALU.mult))
                nc.vector.tensor_tensor(v3(B["kdec"][:]), v3(W[1][:]), bc(hp[:, C_KD, :], P), ALU.mult)\
                    .then_inc(tr_used, 1)
                sp_lo(1)
                dve.wait_ge(at_a, h + 1)
                link(dve, nc.vector.tensor_tensor(v3(B["U"][:]), v3(B["AT"][:]), c3b(K_M1T), ALU.mult))
                nc.vector.tensor_tensor(v3(B["U"][:]), c3b(K_ID), v3(B["U"][:]), ALU.subtract).then_inc(u_v, 1)
                dve.wait_ge(decay_a, 3 * h + 3)
                dve.wait_ge(qk_ps, h + 1)
                nc.vector.tensor_tensor(B["attnT"][:], W[3][:], B["DT"][:], ALU.mult).then_inc(ready_v, 1)
                sp_lo(3)
                for lv in range(NL):
                    if lv < NL - 1:
                        dve.wait_ge(d_ps, (2 * NL - 1) * h + 2 * lv + 1)
                        dve.wait_ge(u_v, (NL + 1) * h + lv + 1)
                        nc.vector.tensor_tensor(B["T"][:], B["T"][:], W[2][:], ALU.subtract).then_inc(t_v, 1)
                        dve.wait_ge(d_ps, (2 * NL - 1) * h + 2 * lv + 2)
                    else:
                        dve.wait_ge(d_ps, (2 * NL - 1) * (h + 1))
                    nc.vector.tensor_tensor(B["U"][:], B["U"][:], W[3][:], ALU.subtract).then_inc(u_v, 1)
                    sp_lo(2 if lv < 3 else 1)
                nc.vector.memset(S[:], 0.0).then_inc(s_v, 1)
                nc.vector.tensor_tensor(B["qg"][:], B["qT"][:], B["EG"][:], ALU.mult).then_inc(ready_v, 1)
                convs = iter(()) if last else conv_steps(dve, h + 1)
                next(convs, None)
                sp_lo(16)
                dve.wait_ge(uw_a, 2 * h + 2)
                for c in range(N_CHUNK):
                    b, o = c // 2, CHUNK * (c % 2)
                    rows, cb = slice(o, o + CHUNK), slice(b * P, (b + 1) * P)
                    dve.wait_ge(v_ps, N_CHUNK * h + c + 1)
                    nc.vector.tensor_tensor(B["vn"][rows, cb], B["u"][rows, cb], W[1][rows, cb], ALU.subtract)\
                        .then_inc(vn_v, 1)
                    end = (c + 1) * CHUNK - 1
                    dve.wait_ge(s_v, (N_CHUNK + 1) * h + c + 1)
                    dve.wait_ge(s_ps, 2 * N_CHUNK * h + 2 * c + 1)
                    nc.vector.scalar_tensor_tensor(S[:], S[:], B["EG"][:, end:end + 1], W[2][:, 0:P],
                                                   ALU.mult, ALU.add).then_inc(s_v, 1)
                    next(convs, None)
                    if c % 2:
                        next(convs, None)
                for _ in convs:
                    pass
                dve.wait_ge(o_a, h + 1)
                link(dve, nc.vector.reciprocal(rms[:], rms[:]))
                nc.vector.tensor_tensor(v3(B["osc"][:]), v3(W[3][:]), bc(rms[:], P), ALU.mult).then_inc(osc_v, 1)
                dve.wait_ge(stored, 16 * h + STORED2)
                dve.wait_ge(o_ps, h + 1)
                nc.vector.scalar_tensor_tensor(B["ob"][:], W[1][:], ng[:], B["zs"][:], ALU.mult, ALU.mult)\
                    .then_inc(o_v, 1)
                dve.wait_ge(o_v, h + 2)

            def dn_pool(pool, h):
                for lv in range(NL):
                    pool.wait_ge(at_a, h + 1)
                    nc.gpsimd.tensor_tensor(v3(LT[:, lv, :]), v3(B["AT"][:]), c3b(K_LV + lv), ALU.mult)\
                        .then_inc(lt_g, 1)

            @block.sync
            def _(sp):
                sp.dma_start(sw[:], t["w_small"]).then_inc(in_small, 16)
                sp.dma_start(ab[:], t["ab"]).then_inc(in_small, 16)
                sp.dma_start(cwa[:], t["dn_conv"]).then_inc(par_in, 16)
                sp.dma_start(ng[:], t["dn_norm"]).then_inc(par_in, 16)
                for h in range(DN_H):
                    load_units(sp, (16 + 16 * min(h + 1, DN_H - 1) + 12 * (h == DN_H - 1) + AHEAD + 3) // 4)
                    sp.wait_ge(o_v, h + 2)
                    sp.dma_start(mix_d[h, :, :], B["ob"][:]).then_inc(stored, 16)
                sp.wait_ge(stored, 16 * DN_H + STORED2)

            @block.gpsimd
            def _(pool):
                with pool.Fori(0, DN_H) as h:
                    dn_pool(pool, h)

            @block.tensor
            def _(pe):
                fill = filler(pe, 4)
                fill(10)
                small_pe(pe)
                fill(8)
                small_turn_pe(pe)
                fill(14)
                cumulate_pe(pe)
                fill(1000)
                with repeat(pe, DN_H - 1, (pe_q, 16, "dn_pe quarters")) as h:
                    dn_pe(pe, h, 4)
                dn_pe(pe, DN_H - 1, 3)

            @block.scalar
            def _(act):
                act.wait_ge(in_small, 32)
                nc.scalar.activation(sw_hi[:], sw[:], ACT.Copy).then_inc(sm_hi, 1)
                split_hi(act, 2)
                small_act(act)
                split_hi(act, 8)
                silu_part(act, 0)
                with repeat(act, DN_H - 1, (act_q, 16, "dn_act quarters"), (act_c, TICKS["dn_act"], "dn_act")) as h:
                    dn_act(act, h, 16, False)
                dn_act(act, DN_H - 1, 12, True)

            @block.vector
            def _(dve):
                dve.wait_ge(sm_hi, 1)
                nc.vector.tensor_tensor(sw_lo[:], sw[:], sw_hi[:].bitcast(F32), ALU.subtract).then_inc(sm_lo, 1)
                split_lo(dve, 2)
                small_dve(dve)
                dve.wait_ge(par_in, 32)
                split_lo(dve, 8)
                nc.vector.memset(S[:], 0.0).then_inc(o_v, 1)
                for _ in conv_steps(dve, 0):
                    pass
                with repeat(dve, DN_H - 1, (dve_q, 16, "dn_dve quarters"), (dve_c, TICKS["dn_dve"], "dn_dve")) as h:
                    dn_dve(dve, h, 16, False)
                dn_dve(dve, DN_H - 1, 12, True)

        (att_s, att_m, att_e, att_p, att_t, att_pt, att_o) = (
            sem(f"att_{n}") for n in (
                "scores",
                "max",
                "exp",
                "probs",
                "turned",
                "probs_t",
                "out"))

        def scores(n, b, q, k):
            m = nc.tensor.matmul(W[b % 2][:, 0:(b + 1) * P], q[:, b * P:(b + 1) * P], k[:, 0:(b + 1) * P],
                                 start=True, stop=True)
            m.then_inc(att_s, 1)

        def attend_pe(pe, n, k, q, v, lg, PT, out, start, stop, fill, fills, after=None):
            for b in range(TB):
                pe.wait_ge(att_p, 4 * n + b + 1)
                for sb_ in range(b + 1):
                    m = nc.tensor.transpose(W[2 + b % 2][:, sb_ * P:(sb_ + 1) * P], lg[:, b, sb_ * P:(sb_ + 1) * P],
                                            ident)
                m.then_inc(att_t, 1)
                if b < 2:
                    pe.wait_ge(att_m, 4 * n + b + 1)
                    scores(n, b + 2, q, k)
                elif after is not None:
                    pe.wait_ge(att_m, 4 * n + b + 1)
                    scores(n + 1, b - 2, after[0], after[1])
                fill(fills[b])
                if b < 2:
                    pe.wait_ge(att_pt, 4 * n + b + 1)
            pe.wait_ge(att_pt, 4 * n + 4)
            for sb_ in range(TB):
                m = nc.tensor.matmul(out[:, sb_ * P:SEQ], v[:, sb_, :], PT[:, sb_, sb_ * P:SEQ],
                                     start=(start and sb_ == 0), stop=(stop and sb_ == TB - 1))
            m.then_inc(att_o, 1)

        def att_rows(dve, n, b, lg, nm, bias):
            dve.wait_ge(att_s, 4 * n + b + 1)
            width = (b + 1) * P
            link(dve, nc.vector.tensor_tensor(lg[:, b, 0:width], W[b % 2][:, 0:width],
                                              bias(TB * P - width, TB * P), ALU.add))
            nc.vector.tensor_reduce(nm[:, b:b + 1], lg[:, b, 0:width], AX.X, ALU.max, negate=True).then_inc(att_m, 1)

        def att_norm(dve, n, b, lg, den, gates):
            width = (b + 1) * P
            dve.wait_ge(att_e, 4 * n + b + 1)
            link(dve, nc.vector.reciprocal(den[:, b:b + 1], den[:, b:b + 1]))
            if gates is None:
                ins = nc.vector.tensor_scalar(lg[:, b, 0:width], lg[:, b, 0:width], den[:, b:b + 1], None, ALU.mult)
            else:
                ins = nc.vector.tensor_scalar(lg[:, b, 0:width], lg[:, b, 0:width], den[:, b:b + 1],
                                              gates[:, b:b + 1], ALU.mult, ALU.mult)
            ins.then_inc(att_p, 1)

        def attend_dve(dve, n, lg, nm, den, bias, gates, first, split):
            for b in range(TB):
                if not first:
                    dve.wait_ge(att_t, 4 * (n - 1) + b + 1)
                att_rows(dve, n, b, lg, nm, bias)
                if b >= 1:
                    att_norm(dve, n, b - 1, lg, den, gates)
                split(1)
            att_norm(dve, n, TB - 1, lg, den, gates)

        def attend_act(act, n, lg, nm, den, PT, first, split):
            def turn(b):
                act.wait_ge(att_t, 4 * n + b + 1)
                if b == 0 and not first:
                    act.wait_ge(att_o, n)
                nc.scalar.activation(PT[:, 0:b + 1, b * P:(b + 1) * P],
                                     W[2 + b % 2][:, 0:(b + 1) * P].rearrange("p (s n) -> p s n", n=P),
                                     ACT.Copy).then_inc(att_pt, 1)

            for b in range(TB):
                act.wait_ge(att_m, 4 * n + b + 1)
                nc.scalar.activation(lg[:, b, 0:(b + 1) * P], lg[:, b, 0:(b + 1) * P], ACT.Exp,
                                     bias=nm[:, b:b + 1], accum_out=den[:, b:b + 1]).then_inc(att_e, 1)
                split(1)
                if b >= 1:
                    turn(b - 1)
            turn(TB - 1)

        Q3 = 16 * DN_H + 12
        with ExitStack() as c3, nc.Block() as block:
            tab = sb(c3, "dil_tab", [P, DIL_H, TW_DIL])
            lg, PT = sb(c3, "dil_lg", [P, TB, SEQ]), sb(c3, "dil_PT", [P, TB, SEQ])
            qs, ks, vs, ob = (sb(c3, f"dil_{n}", [P, SEQ]) for n in ("q", "k", "v", "ob"))
            vt = sb(c3, "dil_vt", [P, TB, P])
            nm, den = sb(c3, "dil_nm", [P, TB]), sb(c3, "dil_den", [P, TB])
            q_ev, kv_ev, vtr_ps, vt_ev, ob_v = (sem(f"dil_{n}") for n in ("q_ev", "kv_ev", "vtr_ps", "vt_ev", "ob_v"))

            def dil_pe(pe, n):
                fill = filler(pe, 3)
                pe.wait_ge(q_ev, n + 1)
                pe.wait_ge(kv_ev, 2 * n + 1)
                scores(n, 0, qs, ks)
                scores(n, 1, qs, ks)
                pe.wait_ge(kv_ev, 2 * n + 2)
                for b in range(TB):
                    m = nc.tensor.transpose(W[3][:, b * P:(b + 1) * P], vs[:, b * P:(b + 1) * P], ident)
                m.then_inc(vtr_ps, 1)
                fill(8)
                pe.wait_ge(vt_ev, n + 1)
                attend_pe(pe, n, ks, qs, vt, lg, PT, PB[3], True, True, fill, (9, 9, 9, 9))
                fill(1000)

            def dil_act(act, n):
                act.wait_ge(q_used, Q3 + 12 * n)
                nc.scalar.activation(ks[:], PB[1][:], ACT.Copy).then_inc(kv_ev, 1)
                nc.scalar.activation(vs[:], PB[2][:], ACT.Copy).then_inc(kv_ev, 1)
                split_hi(act, 2)
                act.wait_ge(vtr_ps, n + 1)
                nc.scalar.activation(vt[:].rearrange("p b n -> p (b n)"), W[3][:], ACT.Copy).then_inc(vt_ev, 1)
                attend_act(act, n, lg, nm, den, PT, True, lambda k: split_hi(act, 2 * k))
                split_hi(act, 2)

            def dil_dve(dve, n, hd):
                settle(dve)
                dve.wait_ge(q_used, Q3 + 12 * n)
                nc.vector.tensor_scalar(qs[:], PB[0][:], SCALE, None, ALU.mult).then_inc(q_ev, 1)
                split_lo(dve, 2)

                def bias(a, e):
                    if isinstance(hd, int):
                        return tab[:, hd, a:e]
                    return tab[:, bass.ds(hd, 1), a:e].rearrange("p a n -> p (a n)")

                attend_dve(dve, n, lg, nm, den, bias, None, True, lambda k: split_lo(dve, 2 * k))
                split_lo(dve, 2)
                dve.wait_ge(att_o, n + 1)
                dve.wait_ge(stored, 16 * DN_H + STORED2 + 16 * n)
                nc.vector.tensor_copy(ob[:], PB[3][:]).then_inc(ob_v, 1)
                dve.wait_ge(ob_v, n + 1)

            @block.sync
            def _(sp):
                sp.dma_start(tab[:], toep_d[0:DIL_H, :, 0:TW_DIL].rearrange("h p c -> p h c")).then_inc(table_in, 16)
                for n in range(DIL_H):
                    load_units(sp, (Q3 + 12 * (n + 1) + AHEAD + 3) // 4)
                    sp.wait_ge(ob_v, n + 1)
                    sp.dma_start(mix_d[DN_H + n, :, :], ob[:]).then_inc(stored, 16)
                sp.wait_ge(stored, 16 * (DN_H + DIL_H) + STORED2)

            @block.tensor
            def _(pe):
                with repeat(pe, DIL_H // 2, (pe_q, 24, "dil_pe quarters")) as i:
                    dil_pe(pe, 2 * i)
                    dil_pe(pe, 2 * i + 1)

            @block.scalar
            def _(act):
                with repeat(act, DIL_H // 2, (act_q, 24, "dil_act quarters")) as i:
                    dil_act(act, 2 * i)
                    dil_act(act, 2 * i + 1)

            @block.vector
            def _(dve):
                dve.wait_ge(table_in, 16 * len(PIECES) + 16)
                with repeat(dve, DIL_H // 2, (dve_q, 24, "dil_dve quarters"), (dve_c, TICKS["dil_dve"], "dil_dve")) as i:
                    dil_dve(dve, 2 * i, 2 * i)
                    dil_dve(dve, 2 * i + 1, 2 * i + 1)

        Q4 = Q3 + 12 * DIL_H
        N4 = DIL_H
        W1Q = 16
        NC2 = NSA_G * N_CMP
        with ExitStack() as c4, nc.Block() as block:
            tab = sb(c4, "nsa_tab", [P, NSA_H, TW_NSA])
            lg, PT = sb(c4, "nsa_lg", [P, TB, SEQ]), sb(c4, "nsa_PT", [P, TB, SEQ])
            qs = [sb(c4, f"nsa_q{g}", [P, SEQ]) for g in range(NSA_G)]
            ob = [sb(c4, f"nsa_ob{g}", [P, SEQ]) for g in range(NSA_G)]
            kT = [[sb(c4, f"nsa_k{br}{g}", [P, SEQ]) for g in range(NSA_G)] for br in range(2)]
            vt = [[sb(c4, f"nsa_v{br}{g}", [P, TB, P]) for g in range(NSA_G)] for br in range(2)]
            cb_hi, cb_lo = sb(c4, "cmp_hi", [P, CMP_LEN, NC2], F32R), sb(c4, "cmp_lo", [P, CMP_LEN, NC2], F32R)
            cb = PT[:].rearrange("p b n -> p (b n)")[:, 0:CMP_LEN * NC2].rearrange("p (l c) -> p l c", l=CMP_LEN)
            pos = sb(c4, "cmp_pos", [P, 2, CMP_LEN])
            w2 = sb(c4, "cmp_w2", [P, 2, 2, HD])
            hm, hmT = sb(c4, "cmp_mid", [NC2, CMP_HID]), sb(c4, "cmp_midT", [P, 2, NC2])
            kc, vc = sb(c4, "k_cmp", [P, NC2]), sb(c4, "v_cmp", [N_CMP, NSA_G, HD])
            lc, PTc = sb(c4, "cmp_lg", [P, NSA_G, TB, N_CMP]), sb(c4, "cmp_PT", [N_CMP, NSA_G, SEQ])
            nm, den = sb(c4, "nsa_nm", [P, TB]), sb(c4, "nsa_den", [P, TB])
            nmc, denc = sb(c4, "cmp_nm", [P, NSA_G, TB]), sb(c4, "cmp_den", [P, NSA_G, TB])
            gs = sb(c4, "nsa_gates", [P, 3 * NSA_G, TB])
            (par4, kv_ev, kv_tr, kv_vt, cb_v, cb_a, cb_l, cm_ps, cm_a, cm_tr, cm_t, cm_k, cm_kv, q_ev, c_s, c_m, c_e,
             c_p, c_t, c_pt, c_o, o_v4) = (sem(f"nsa_{n}") for n in (
                 "par kv_ev kv_tr kv_vt cb_v cb_a cb_l cm_ps cm_a cm_tr cm_t cm_k cm_kv q_ev c_s c_m c_e c_p c_t "
                 "c_pt c_o o_v").split())
            UNITS = 12
            V_UNITS = (5, 7, 9, 11)
            Q_CMP = Q4 + 4 * (UNITS - 3)
            Q_HEAD = Q_CMP + 2 * W1Q + 8

            def nsa_pe(pe, r, last):
                fill = filler(pe, 0 if last else 2)
                pe.wait_ge(q_ev, 2 * r + 2)
                for g in range(NSA_G):
                    for b in range(TB):
                        m = nc.tensor.matmul(W[g][:, b * N_CMP:(b + 1) * N_CMP], qs[g][:, b * P:(b + 1) * P],
                                             kc[:, g * N_CMP:(g + 1) * N_CMP], start=True, stop=True)
                    m.then_inc(c_s, 1)
                fill(4)
                for g in range(NSA_G):
                    pe.wait_ge(c_p, 2 * r + g + 1)
                    for b in range(TB):
                        m = nc.tensor.transpose(W[2 + g][0:N_CMP, b * P:(b + 1) * P], lc[:, g, b, :], ident)
                    m.then_inc(c_t, 1)
                n0 = N4 + 4 * r
                scores(n0, 0, qs[0], kT[0][0])
                scores(n0, 1, qs[0], kT[0][0])
                for g in range(NSA_G):
                    pe.wait_ge(c_pt, 2 * r + g + 1)
                    nc.tensor.matmul(PB[2 + g][:], vc[:, g, :], PTc[:, g, :], start=True, stop=False).then_inc(c_o, 1)
                seq = [(g, br) for g in range(NSA_G) for br in range(2)]
                for i, (g, br) in enumerate(seq):
                    nxt = seq[i + 1] if i < 3 else None
                    attend_pe(pe, n0 + i, kT[br][g], qs[g], vt[br][g], lg, PT, PB[2 + g], False, br == 1, fill,
                              (2, 2, 2, 2) if i else (2, 2, 0, 0),
                              None if nxt is None else (qs[nxt[0]], kT[nxt[1]][nxt[0]]))
                fill(1000)

            def nsa_act(act, r, last):
                left = [0 if last else 8]

                def sp_hi(k):
                    k = min(k, left[0])
                    left[0] -= k
                    split_hi(act, k)

                for g in range(NSA_G):
                    for b in range(TB):
                        act.wait_ge(c_m, 2 * r + g + 1)
                        ins = nc.scalar.activation(lc[:, g, b, :], lc[:, g, b, :], ACT.Exp, bias=nmc[:, g, b:b + 1],
                                                   accum_out=denc[:, g, b:b + 1])
                        if b == TB - 1:
                            ins.then_inc(c_e, 1)
                        else:
                            astep(ins)
                sp_hi(1)
                for g in range(NSA_G):
                    act.wait_ge(c_t, 2 * r + g + 1)
                    nc.scalar.activation(PTc[:, g, :], W[2 + g][0:N_CMP, :], ACT.Copy).then_inc(c_pt, 1)
                for i in range(4):
                    attend_act(act, N4 + 4 * r + i, lg, nm, den, PT, i == 0, lambda k: None)
                    sp_hi(2)
                sp_hi(8)

            def nsa_dve(dve, r, last):
                left = [0 if last else 8]

                def sp_lo(k):
                    k = min(k, left[0])
                    left[0] -= k
                    split_lo(dve, k)

                settle(dve)
                for g in range(NSA_G):
                    dve.wait_ge(q_used, Q_HEAD + 8 * r - 4 * (1 - g))
                    nc.vector.tensor_scalar(qs[g][:], PB[g][:], SCALE, None, ALU.mult).then_inc(q_ev, 1)
                    c0 = 3 * (NSA_R * g + r)
                    src = gate[:, c0:c0 + 3, :] if isinstance(r, int) else gate[:, bass.ds(c0, 3), :]
                    step(nc.vector.tensor_copy(gs[:, 3 * g:3 * g + 3, :], src))

                def bias_of(g):
                    hd = NSA_R * g + r

                    def bias(a, e, s=1):
                        if isinstance(hd, int):
                            return tab[:, hd, a:e:s]
                        return tab[:, bass.ds(hd, 1), a:e:s].rearrange("p a n -> p (a n)")
                    return bias

                for g in range(NSA_G):
                    dve.wait_ge(c_s, 2 * r + g + 1)
                    for b in range(TB):
                        a = TW_DIL - P - P * b + CMP_LEN - 1
                        ins = nc.vector.tensor_tensor(lc[:, g, b, :], W[g][:, b * N_CMP:(b + 1) * N_CMP],
                                                      bias_of(g)(a, a + CMP_STRIDE * (N_CMP - 1) + 1, CMP_STRIDE), ALU.add)
                        step(ins)
                    settle(dve)
                    link(dve, nc.vector.tensor_reduce(nmc[:, g, :], lc[:, g], AX.X, ALU.max, negate=True))
                    nc.vector.tensor_scalar(nmc[:, g, :], nmc[:, g, :], BIG / 10, None, ALU.min).then_inc(c_m, 1)
                sp_lo(1)
                for g in range(NSA_G):
                    dve.wait_ge(c_e, 2 * r + g + 1)
                    link(dve, nc.vector.tensor_scalar(denc[:, g, :], denc[:, g, :], 1e-30, None, ALU.max))
                    link(dve, nc.vector.reciprocal(denc[:, g, :], denc[:, g, :]))
                    link(dve, nc.vector.tensor_tensor(denc[:, g, :], denc[:, g, :], gs[:, 3 * g, :], ALU.mult))
                    nc.vector.tensor_tensor(lc[:, g], lc[:, g], bc(denc[:, g, :], N_CMP), ALU.mult).then_inc(c_p, 1)
                for i in range(4):
                    g, br = i // 2, i % 2
                    attend_dve(dve, N4 + 4 * r + i, lg, nm, den, bias_of(g), gs[:, 3 * g + 1 + br, :], i == 0,
                               lambda k: None)
                    sp_lo(2)
                sp_lo(8)
                dve.wait_ge(stored, 16 * (DN_H + DIL_H) + STORED2 + 32 * r)
                for g in range(NSA_G):
                    dve.wait_ge(att_o, N4 + 4 * r + 2 * g + 2)
                    nc.vector.tensor_copy(ob[g][:], PB[2 + g][:]).then_inc(o_v4, 1)
                dve.wait_ge(o_v4, 2 * r + 2)

            @block.sync
            def _(sp):
                sp.dma_start(pos[:], t["cmp_pos"]).then_inc(par4, 16)
                sp.dma_start(w2[:], t["cmp_w2"]).then_inc(par4, 16)
                sp.dma_start(tab[:], toep_d[DIL_H:, :, :].rearrange("h p c -> p h c")).then_inc(table_in, 16)
                load_units(sp, (Q_HEAD + AHEAD + 3) // 4)
                for r in range(NSA_R):
                    load_units(sp, (Q_HEAD + 8 * min(r + 1, NSA_R - 1) + AHEAD + 3) // 4)
                    for g in range(NSA_G):
                        sp.wait_ge(o_v4, 2 * r + g + 1)
                        sp.dma_start(mix_d[DN_H + DIL_H + NSA_R * g + r, :, :], ob[g][:]).then_inc(stored, 16)
                sp.wait_ge(stored, 16 * KT + STORED2)

            @block.tensor
            def _(pe):
                def turn_v(i):
                    pe.wait_ge(kv_ev, V_UNITS[i] + 1)
                    for b in range(TB):
                        m = nc.tensor.transpose(W[i][:, b * P:(b + 1) * P], qs[i % 2][:, b * P:(b + 1) * P], ident)
                    m.then_inc(kv_tr, 1)

                for u in range(3, UNITS):
                    pe.wait_ge(kv_ev, u - 2)
                    for kt in range(KT):
                        project(pe, u % 3, kt)
                    if u - 1 in V_UNITS:
                        turn_v(V_UNITS.index(u - 1))
                for i in range(2):
                    pe.wait_ge(cb_l, i + 1)
                    for q in range(W1Q):
                        s = pe_q.n % RING
                        pe.wait_ge(lo_done, pe_q.at(1))
                        for ll in range(2):
                            l = 2 * q + ll
                            for n, (a, b) in enumerate(((cb_hi, w_hi), (cb_lo, w_hi), (cb_hi, w_lo))):
                                m = nc.tensor.matmul(PB[3][0:NC2, i * CMP_HID:(i + 1) * CMP_HID] if i == 0 else
                                                     PB[0][0:NC2, 0:CMP_HID], a[:, l, :],
                                                     b[:, s, ll * CMP_HID:(ll + 1) * CMP_HID],
                                                     start=(l == 0 and n == 0), stop=(l == CMP_LEN - 1 and n == 2))
                        m.then_inc(q_used, 1)
                        pe_q.n += 1
                    if i == 0:
                        turn_v(3)
                for i in range(2):
                    pe.wait_ge(cm_a, i + 1)
                    if i == 0:
                        pe.wait_ge(kv_vt, 4)
                    for hh in range(2):
                        m = nc.tensor.transpose(W[0][:, hh * NC2:(hh + 1) * NC2], hm[:, hh * P:(hh + 1) * P],
                                                cst[0:NC2, K_ID, 0:NC2])
                    m.then_inc(cm_tr, 1)
                    pe.wait_ge(cm_t, i + 1)
                    if i == 0:
                        for hh in range(2):
                            m = nc.tensor.matmul(W[1][:, 0:NC2], w2[:, 0, hh, :], hmT[:, hh, :],
                                                 start=(hh == 0), stop=(hh == 1))
                        m.then_inc(cm_k, 1)
                        pe.wait_ge(cm_a, 2)
                        filler(pe, 2)(1000)
                    else:
                        for g in range(NSA_G):
                            for hh in range(2):
                                m = nc.tensor.matmul(W[2 + g][0:N_CMP, 0:HD], hmT[:, hh, g * N_CMP:(g + 1) * N_CMP],
                                                     w2[:, 1, hh, :], start=(hh == 0), stop=(hh == 1))
                            m.then_inc(cm_k, 1)
                pe.wait_ge(cm_kv, 3)
                with repeat(pe, NSA_R - 1, (pe_q, 8, "nsa_pe quarters")) as r:
                    nsa_pe(pe, r, False)
                nsa_pe(pe, NSA_R - 1, True)

            KV_DST = [lg[:, 0], lg[:, 2], lg[:, 1], lg[:, 3], kT[0][0][:], qs[0][:], kT[0][1][:], qs[1][:],
                      kT[1][0][:], qs[0][:], kT[1][1][:], qs[1][:]]

            @block.scalar
            def _(act):
                for u in range(UNITS):
                    act.wait_ge(q_used, Q4 - 12 + 4 * (u + 1))
                    if u in V_UNITS[2:]:
                        act.wait_ge(kv_tr, V_UNITS.index(u) - 1)
                    nc.scalar.activation(KV_DST[u], PB[u % 3][:], ACT.Copy).then_inc(kv_ev, 1)
                    if u >= 2 and u < UNITS - 1:
                        split_hi(act, 4)
                for i in range(2):
                    act.wait_ge(cb_v, i + 1)
                    if i == 1:
                        act.wait_ge(q_used, Q_CMP + W1Q)
                    nc.scalar.activation(cb_hi[:], cb, ACT.Copy).then_inc(cb_a, 1)
                    split_hi(act, W1Q)
                    act.wait_ge(q_used, Q_CMP + W1Q * (i + 1))
                    if i == 1:
                        act.wait_ge(cm_tr, 1)
                    src = PB[3] if i == 0 else PB[0]
                    nc.scalar.activation(hm[:], src[0:NC2, 0:CMP_HID], ACT.Gelu_apprx_tanh).then_inc(cm_a, 1)
                split_hi(act, 8)
                with repeat(act, NSA_R - 1, (act_q, 8, "nsa_act quarters"), (act_c, TICKS["nsa_act"], "nsa_act")) as r:
                    nsa_act(act, r, False)
                nsa_act(act, NSA_R - 1, True)

            @block.vector
            def _(dve):
                dve.wait_ge(par4, 32)
                def take_v(i):
                    dve.wait_ge(kv_tr, i + 1)
                    nc.vector.tensor_copy(vt[i // 2][i % 2][:].rearrange("p b n -> p (b n)"), W[i][:]).then_inc(kv_vt, 1)

                def blocks(i):
                    for g in range(NSA_G):
                        for a in range(2):
                            src = lg[:, 2 * i + g, CMP_STRIDE * a:CMP_STRIDE * (a + N_CMP)]\
                                .rearrange("p (c l) -> p c l", l=CMP_STRIDE)
                            dst = cb[:, CMP_STRIDE * a:CMP_STRIDE * (a + 1), g * N_CMP:(g + 1) * N_CMP]\
                                .rearrange("p l c -> p c l")
                            pp = pos[:, i, None, CMP_STRIDE * a:CMP_STRIDE * (a + 1)].to_broadcast([P, N_CMP, CMP_STRIDE])
                            ins = nc.vector.tensor_tensor(dst, src, pp, ALU.add)
                            if g == 1 and a == 1:
                                ins.then_inc(cb_v, 1)
                            else:
                                step(ins)

                def blocks_lo(i):
                    dve.wait_ge(cb_a, i + 1)
                    nc.vector.tensor_tensor(cb_lo[:], cb, cb_hi[:].bitcast(F32), ALU.subtract).then_inc(cb_l, 1)

                for u in range(UNITS):
                    dve.wait_ge(kv_ev, u + 1)
                    if u >= 2 and u < UNITS - 1:
                        split_lo(dve, 4)
                    if u == 4:
                        settle(dve)
                        blocks(0)
                    if u in (7, 9, 11):
                        take_v((u - 7) // 2)
                blocks_lo(0)
                split_lo(dve, W1Q)
                dve.wait_ge(cb_l, 1)
                blocks(1)
                take_v(3)
                dve.wait_ge(q_used, Q_CMP + W1Q)
                blocks_lo(1)
                split_lo(dve, W1Q)

                def mid(i):
                    dve.wait_ge(cm_tr, i + 1)
                    nc.vector.tensor_copy(hmT[:].rearrange("p h c -> p (h c)"), W[0][:, 0:2 * NC2]).then_inc(cm_t, 1)

                mid(0)
                dve.wait_ge(cm_k, 1)
                nc.vector.tensor_copy(kc[:], W[1][:, 0:NC2]).then_inc(cm_kv, 1)
                split_lo(dve, 8)
                mid(1)
                for g in range(NSA_G):
                    dve.wait_ge(cm_k, 2 + g)
                    nc.vector.tensor_copy(vc[:, g, :], W[2 + g][0:N_CMP, 0:HD]).then_inc(cm_kv, 1)
                dve.wait_ge(table_in, 16 * len(PIECES) + 32)
                with repeat(dve, NSA_R - 1, (dve_q, 8, "nsa_dve quarters"), (dve_c, TICKS["nsa_dve"], "nsa_dve")) as r:
                    nsa_dve(dve, r, False)
                nsa_dve(dve, NSA_R - 1, True)

        CG = D_MODEL // QW
        c5 = ctx.enter_context(ExitStack())
        xs = sb(c5, "xs", [P, TB, D_MODEL])
        xr_in, m_in, m_hi, m_lo, bank_free, wo_ps, wo_v = (
            sem(n) for n in ("xr_in", "mix_in", "mix_hi", "mix_lo", "bank_free", "wo_ps", "wo_v"))
        Q5 = Q_HEAD + 8 * (NSA_R - 1)
        with ExitStack() as c6, nc.Block() as block:
            mraw = sb(c6, "mix_raw", [P, KT, SEQ])

            @block.sync
            def _(sp):
                for i in range(4):
                    sp.dma_start(mraw[:, 4 * i:4 * i + 4, :], mix_d[4 * i:4 * i + 4, :, :].rearrange("k p n -> p k n"))\
                        .then_inc(m_in, 16)
                    sp.wait_ge(m_in, 16 * (i + 1))
                sp.dma_start(xs[:], t["x"].rearrange("(b p) d -> p b d", p=P)).then_inc(xr_in, 16)
                load_units(sp, (Q5 + 16 * CG + AHEAD + 3) // 4)

            @block.tensor
            def _(pe):
                with repeat(pe, CG // 2, (pe_q, 32, "wo_pe quarters")) as i:
                    for c in range(2):
                        for kt in range(KT):
                            s = pe_q.n % RING
                            pe.wait_ge(lo_done, pe_q.at(1))
                            pe.wait_ge(m_lo, kt + 1)
                            for b in range(TB):
                                if kt == 0:
                                    pe.wait_ge(bank_free, 8 * i + 4 * c + b + 1)
                                for n, (x, w) in enumerate(((h_hi, w_hi), (h_lo, w_hi), (h_hi, w_lo))):
                                    m = nc.tensor.matmul(bank[4 * c + b][:], x[:, kt, b * P:(b + 1) * P], w[:, s, :],
                                                         start=(kt == 0 and n == 0), stop=(kt == KT - 1 and n == 2))
                                if kt == KT - 1 and b < TB - 1:
                                    m.then_inc(wo_ps, 1)
                            m.then_inc(q_used, 1)
                            pe_q.n += 1

            @block.scalar
            def _(act):
                for kt in range(KT):
                    act.wait_ge(m_in, 16 * (kt // 4 + 1))
                    nc.scalar.activation(h_hi[:, kt, :], mraw[:, kt, :], ACT.Copy).then_inc(m_hi, 1)
                with repeat(act, CG // 2, (act_q, 32, "wo_act quarters")) as i:
                    split_hi(act, 32)

            @block.vector
            def _(dve):
                dve.sem_inc(bank_free, 8)
                for kt in range(KT):
                    dve.wait_ge(m_hi, kt + 1)
                    nc.vector.tensor_tensor(h_lo[:, kt, :], mraw[:, kt, :], h_hi[:, kt, :].bitcast(F32), ALU.subtract)\
                        .then_inc(m_lo, 1)
                dve.wait_ge(xr_in, 16)
                with repeat(dve, CG // 2, (dve_q, 32, "wo_dve quarters")) as i:
                    for c in range(2):
                        split_lo(dve, KT)
                        for b in range(TB):
                            if b < TB - 1:
                                dve.wait_ge(wo_ps, 6 * i + 3 * c + b + 1)
                            else:
                                dve.wait_ge(q_used, Q5 + 32 * i + 16 * (c + 1))
                            dst = xs[:, b, bass.ds(i * 2 * QW + c * QW, QW)]
                            nc.vector.tensor_tensor(dst, dst, bank[4 * c + b][:], ALU.add).then_inc(bank_free, 1)
                dve.wait_ge(bank_free, 8 + 4 * CG)

        with ExitStack() as c6, nc.Block() as block:
            n2_sp, n2_act, n2_dve, n2_pe, _ = normalize("n2", lambda e, b: None, t["g2"], xs, c6, ident)

            @block.sync
            def _(sp):
                n2_sp(sp)

            @block.scalar
            def _(act):
                n2_act(act)

            @block.vector
            def _(dve):
                n2_dve(dve)

            @block.tensor
            def _(pe):
                n2_pe(pe)

        Q7 = Q5 + 16 * CG
        GQ = 8 * GT + 4 * CG
        with ExitStack() as c7, nc.Block() as block:
            g_hi = sb(c7, "g_hi", [P, 2, GT, SEQ], F32R)
            g_lo = sb(c7, "g_lo", [P, 2, GT, SEQ], F32R)
            cg, cv, gf = (sb(c7, f"ffn_{n}", [P, SEQ]) for n in ("gate", "val", "prod"))
            fw = sb(c7, "ffn_w", [P, 2, 3, FT])
            fwg = sb(c7, "ffn_wg", [P, 2, 3, GT])
            fwd = sb(c7, "ffn_wd", [P, 2, 3, GT])
            fg, squares = sb(c7, "final_g", [P, D_MODEL]), sb(c7, "fin_squares", [P, D_MODEL])
            ss, rs = sb(c7, "fin_ss", [P, TB]), sb(c7, "fin_rs", [P, TB])
            (par7, up_free, tap_a, silu7, prod_v, gh_a, gl_v, dn_free, dn_ps, taps_v, fin_a, fin_v, out_s) = (
                sem(f"ffn_{n}") for n in ("par up_free tap silu prod g_hi g_lo down_free down_ps taps fin_a fin_v "
                                          "out").split())

            def up_pe(pe, g, slot):
                for j in range(GT):
                    for v in range(2):
                        bk = 2 * (j % 2) + v
                        pe.wait_ge(up_free, 8 * g + 2 * j + v + 1)
                        for kt in range(KT):
                            project(pe, bk, kt)

            def down_pe(pe, g, slot):
                for c in range(CG):
                    for kt in range(GT):
                        s = pe_q.n % RING
                        pe.wait_ge(lo_done, pe_q.at(1))
                        if c == 0:
                            pe.wait_ge(gl_v, 4 * g + kt + 1)
                        for b in range(TB):
                            if kt == 0:
                                pe.wait_ge(dn_free, 16 * g + 4 * c + b + 1)
                            for n, (x, w) in enumerate(((g_hi, w_hi), (g_lo, w_hi), (g_hi, w_lo))):
                                m = nc.tensor.matmul(W[b][:], x[:, slot, kt, b * P:(b + 1) * P], w[:, s, :],
                                                     start=(kt == 0 and n == 0), stop=(kt == GT - 1 and n == 2))
                            if kt == GT - 1 and b < TB - 1:
                                m.then_inc(dn_ps, 1)
                        m.then_inc(q_used, 1)
                        pe_q.n += 1

            def up_act(act, g, slot, q_start):
                for j in range(GT):
                    split_hi(act, 8)
                    for v, dst in ((0, cg), (1, cv)):
                        act.wait_ge(q_used, q_start + 8 * j + 4 * v + 4)
                        if v == 0 and j == 0:
                            act.wait_ge(taps_v, g + 1)
                        if v == 0:
                            act.wait_ge(prod_v, 4 * g + j)
                        nc.scalar.activation(dst[:], PB[2 * (j % 2) + v][:], ACT.Copy, scale=fwg[:, v, 2, j:j + 1])\
                            .then_inc(tap_a, 1)
                    act.wait_ge(up_free, 4 + 8 * g + 2 * j + 1)
                    nc.scalar.activation(cg[:], cg[:], ACT.Silu).then_inc(silu7, 1)
                    act.wait_ge(prod_v, 4 * g + j + 1)
                    nc.scalar.activation(g_hi[:, slot, j, :], gf[:], ACT.Copy).then_inc(gh_a, 1)

            def up_dve(dve, g, slot):
                g4 = g * GT
                for v in range(2):
                    for k in range(3):
                        src = fw[:, v, k, g4:g4 + GT] if isinstance(g, int) else \
                            fw[:, v, k, bass.ds(g4, GT)]
                        ins = nc.vector.tensor_copy(fwg[:, v, k, :], src)
                        if v == 1 and k == 2:
                            ins.then_inc(taps_v, 1)
                        else:
                            step(ins)
                dve.wait_ge(taps_v, g + 1)
                for j in range(GT):
                    split_lo(dve, 8)
                    for v, dst in ((0, cg), (1, cv)):
                        dve.wait_ge(tap_a, 8 * g + 2 * j + v + 1)
                        bk = PB[2 * (j % 2) + v]
                        link(dve, nc.vector.scalar_tensor_tensor(dst[:, 1:SEQ], bk[:, 0:SEQ - 1], fwg[:, v, 1, j:j + 1],
                                                                 dst[:, 1:SEQ], ALU.mult, ALU.add))
                        nc.vector.scalar_tensor_tensor(dst[:, 2:SEQ], bk[:, 0:SEQ - 2], fwg[:, v, 0, j:j + 1],
                                                       dst[:, 2:SEQ], ALU.mult, ALU.add).then_inc(up_free, 1)
                        dve.wait_ge(up_free, 4 + 8 * g + 2 * j + v + 1)
                    dve.wait_ge(silu7, 4 * g + j + 1)
                    dve.wait_ge(gl_v, 4 * g + j)
                    nc.vector.tensor_tensor(gf[:], cg[:], cv[:], ALU.mult).then_inc(prod_v, 1)
                    dve.wait_ge(gh_a, 4 * g + j + 1)
                    nc.vector.tensor_tensor(g_lo[:, slot, j, :], gf[:], g_hi[:, slot, j, :].bitcast(F32), ALU.subtract)\
                        .then_inc(gl_v, 1)

            def down_dve(dve, g, q_start, splits=4 * CG):
                for c in range(CG):
                    split_lo(dve, max(0, min(4, splits - 4 * c)))
                    for b in range(TB):
                        if b < TB - 1:
                            dve.wait_ge(dn_ps, 12 * g + 3 * c + b + 1)
                        else:
                            dve.wait_ge(q_used, q_start + 4 * (c + 1))
                        dve.wait_ge(dn_free, 4 + 16 * g + 4 * c + b)
                        dst = xs[:, b, c * QW:(c + 1) * QW]
                        nc.vector.tensor_tensor(dst, dst, W[b][:], ALU.add).then_inc(dn_free, 1)

            @block.sync
            def _(sp):
                sp.dma_start(fw[:], t["ffn_conv"]).then_inc(par7, 16)
                sp.dma_start(fg[:], t["final_g"]).then_inc(par7, 16)
                load_units(sp, (Q7 + GQ * N_GROUP) // 4)
                for b in range(TB):
                    sp.wait_ge(fin_v, b + 1)
                    sp.dma_start(t["out"][b * P:(b + 1) * P, :], xs[:, b, :]).then_inc(out_s, 16)
                sp.wait_ge(out_s, 16 * TB)

            @block.tensor
            def _(pe):
                up_pe(pe, 0, 0)
                with repeat(pe, N_GROUP // 2, (pe_q, 2 * GQ, "ffn_pe quarters")) as i:
                    up_pe(pe, 2 * i + 1, 1)
                    down_pe(pe, 2 * i, 0)
                    up_pe(pe, 2 * i + 2, 0)
                    down_pe(pe, 2 * i + 1, 1)
                down_pe(pe, N_GROUP - 1, 0)

            UPQ, DNQ = 8 * GT, 4 * CG

            @block.scalar
            def _(act):
                act.wait_ge(par7, 32)
                up_act(act, 0, 0, Q7)
                with repeat(act, N_GROUP // 2, (act_q, 2 * GQ, "ffn_act quarters")) as i:
                    q0 = Q7 + UPQ + 2 * GQ * i
                    up_act(act, 2 * i + 1, 1, q0)
                    split_hi(act, DNQ)
                    up_act(act, 2 * i + 2, 0, q0 + GQ)
                    split_hi(act, DNQ)
                split_hi(act, DNQ - AHEAD)
                act.wait_ge(dn_free, 4 + 16 * N_GROUP)
                for b in range(TB):
                    alink(act, nc.scalar.activation(squares[:], xs[:, b, :], ACT.Square, accum_out=ss[:, b:b + 1]))
                nc.scalar.activation(rs[:], ss[:], ACT.Sqrt, bias=eps_t[:], scale=1.0 / D_MODEL).then_inc(fin_a, 1)

            @block.vector
            def _(dve):
                dve.wait_ge(par7, 32)
                dve.sem_inc(up_free, 4)
                dve.sem_inc(dn_free, 4)
                up_dve(dve, 0, 0)
                with repeat(dve, N_GROUP // 2, (dve_q, 2 * GQ, "ffn_dve quarters"),
                            (dve_c, TICKS["ffn_dve"], "ffn_dve")) as i:
                    q0 = Q7 + UPQ + 2 * GQ * i
                    up_dve(dve, 2 * i + 1, 1)
                    down_dve(dve, 2 * i, q0 + UPQ)
                    up_dve(dve, 2 * i + 2, 0)
                    down_dve(dve, 2 * i + 1, q0 + GQ + UPQ)
                down_dve(dve, N_GROUP - 1, Q7 + GQ * N_GROUP - DNQ, DNQ - AHEAD)
                dve.wait_ge(fin_a, 1)
                link(dve, nc.vector.reciprocal(rs[:], rs[:]))
                for b in range(TB):
                    nc.vector.scalar_tensor_tensor(xs[:, b, :], xs[:, b, :], rs[:, b:b + 1], fg[:], ALU.mult, ALU.mult)\
                        .then_inc(fin_v, 1)


def rel_bucket(dist):
    exact = BUCKETS // 2
    n = np.maximum(dist, 0)
    nf = np.maximum(n, 1).astype(np.float32)
    large = exact + (np.log(nf / np.float32(exact)) / np.float32(math.log(REL_MAX / exact))
                     * np.float32(BUCKETS - exact)).astype(np.int32)
    return np.where(n < exact, n, np.minimum(large, BUCKETS - 1))


def constant_tiles():
    i, j = np.arange(P)[:, None], np.arange(P)[None, :]
    same = i // CHUNK == j // CHUNK

    def level(b):
        return (i // (2 * b) == j // (2 * b)) & ((i // b) % 2 == 1) & ((j // b) % 2 == 0)

    out = np.zeros((P, N_CST, P), np.float32)
    out[:, K_ID] = i == j
    out[:, K_ONE] = 1
    out[:, K_TRI] = same & (i <= j)
    out[:, K_BLK] = same
    out[:, K_ML] = np.where(same & (i > j), 0, BIG)
    out[:, K_MU] = np.where(same & (i <= j), 0, -BIG)
    out[:, K_M1] = level(1)
    out[:, K_REV] = i + j == P - 1
    out[:, K_M1T] = level(1).T
    for n, b in enumerate(LEVELS):
        out[:, K_LV + n] = level(b).T
    return out


def bias_columns():
    d = TW_DIL - 1 - np.arange(YLEN)
    out = np.zeros((BUCKETS + 2, YLEN), np.float32)
    out[rel_bucket(d), np.arange(YLEN)] = d >= 0
    count = (d <= 128).astype(int) + (d % 4 == 0) + (d % 16 == 0)
    ok = (d >= 0) & (count > 0)
    out[BUCKETS] = np.where(ok, np.log(np.where(ok, count, 1)), -BIG)
    out[BUCKETS + 1] = np.where(d >= 0, 0, -BIG)
    return out


def stream(w_in, cmp_w1, w_out, ffn_up, ffn_down):
    units = []

    def columns(w, c):
        units.append(w[:, c:c + P].reshape(KT, P, P).transpose(1, 0, 2).reshape(P, -1))

    def rows(w, r, c):
        units.append(w[r:r + 4 * P, c:c + QW].reshape(4, P, QW).transpose(1, 0, 2).reshape(P, -1))

    dn_w, dil_w = DN_H * HD, DIL_H * HD
    dil0 = 4 * dn_w + 2 * DN_H
    q0 = dil0 + 3 * dil_w
    kv0 = q0 + NSA_H * HD
    for h in range(DN_H):
        for part in range(4):
            columns(w_in, part * dn_w + h * HD)
    for h in range(DIL_H):
        for part in range(3):
            columns(w_in, dil0 + part * dil_w + h * HD)

    def kv(br, which, g):
        columns(w_in, kv0 + ((br * 2 + which) * NSA_G + g) * HD)

    for br in range(3):
        for g in range(NSA_G):
            for which in range(2):
                kv(br, which, g)
    for i in range(2):
        w = cmp_w1[i].reshape(CMP_LEN, P, CMP_HID)
        for l in range(0, CMP_LEN, 8):
            units.append(w[l:l + 8].transpose(1, 0, 2).reshape(P, -1))
    for r in range(NSA_R):
        for g in range(NSA_G):
            columns(w_in, q0 + (g * NSA_R + r) * HD)
    for c in range(0, D_MODEL, QW):
        for r in range(0, D_MODEL, 4 * P):
            rows(w_out, r, c)

    def up(g):
        for j in range(GT):
            for v in range(2):
                columns(ffn_up, v * D_FF + (g * GT + j) * P)

    def down(g):
        for c in range(0, D_MODEL, QW):
            rows(ffn_down, g * GT * P, c)

    up(0)
    for g in range(1, N_GROUP):
        up(g)
        down(g - 1)
    down(N_GROUP - 1)
    return np.stack(units)


def kernel(x, norm1_g, w_in, dn_conv, dn_a_log, dn_dt_bias, dn_norm_g, cmp_pos, cmp_w1, cmp_w2,
           w_out, norm2_g, ffn_up, ffn_conv, ffn_down, rel_bias, final_g):
    import concourse.bacc as bacc
    from concourse.bass_utils import run_bass_kernel_spmd

    x, w = np.asarray(x)[0], np.asarray(w_in)[0]
    small = np.concatenate([w[:, 4 * DN_H * HD:4 * DN_H * HD + 2 * DN_H], w[:, -3 * NSA_H:]], axis=1)
    extra = np.zeros((2, DIL_H + NSA_H), np.float32)
    extra[0, :DIL_H] = 1
    extra[1, DIL_H:] = 1
    arrays = {
        "x": x,
        "weights": stream(w, np.asarray(cmp_w1)[0], np.asarray(w_out)[0], np.asarray(ffn_up)[0],
                          np.asarray(ffn_down)[0]),
        "w_small": small.reshape(KT, P, N_SMALL).transpose(1, 0, 2),
        "ab": np.broadcast_to(np.stack([np.asarray(dn_a_log)[0], np.asarray(dn_dt_bias)[0]])[None], (P, 2, DN_H)),
        "g1": np.broadcast_to(np.asarray(norm1_g), (P, D_MODEL)),
        "g2": np.broadcast_to(np.asarray(norm2_g), (P, D_MODEL)),
        "final_g": np.broadcast_to(np.asarray(final_g)[None], (P, D_MODEL)),
        "dn_conv": np.asarray(dn_conv)[0].reshape(4, 3, DN_H, P).transpose(3, 2, 1, 0),
        "dn_norm": np.asarray(dn_norm_g)[0].reshape(P, 1),
        "cmp_pos": np.asarray(cmp_pos)[0].transpose(2, 0, 1),
        "cmp_w2": np.asarray(cmp_w2)[0].reshape(2, 2, P, HD).transpose(2, 0, 1, 3),
        "ffn_conv": np.asarray(ffn_conv)[0].reshape(3, 2, FT, P).transpose(3, 1, 0, 2),
        "bias_lhs": np.concatenate([np.asarray(rel_bias).T, extra]),
        "cst": constant_tiles(),
        "onehot": bias_columns(),
    }
    arrays = {k: np.ascontiguousarray(a) for k, a in arrays.items()}
    nc = bacc.Bacc("TRN2", target_bir_lowering=False, num_devices=1)
    t = {k: nc.dram_tensor(f"in_{k}", a.shape, mybir.dt.from_np(a.dtype), kind="ExternalInput").ap()
         for k, a in arrays.items()}
    t["out"] = nc.dram_tensor("out", (SEQ, D_MODEL), F32, kind="ExternalOutput").ap()
    program(nc, t)
    r = run_bass_kernel_spmd(nc, [{f"in_{k}": a for k, a in arrays.items()}], core_ids=[0])
    return r.results[0]["out"].reshape(1, SEQ, D_MODEL)
```

```python
import math
from contextlib import ExitStack, contextmanager
from itertools import islice

import numpy as np
import concourse.bass as bass
from concourse import mybir

F32 = mybir.dt.float32
F32R = mybir.dt.float32r
ALU = mybir.AluOpType
ACT = mybir.ActivationFunctionType
AX = mybir.AxisListType

P = 128
SEQ = 512
D_MODEL = 2048
HD = 128
TB = SEQ // P
KT = D_MODEL // P
DN_H, DIL_H, NSA_H, NSA_G = 6, 4, 6, 2
NSA_R = NSA_H // NSA_G
CHUNK = 64
N_CHUNK = SEQ // CHUNK
D_FF = 5632
FT = D_FF // P
GT = 4
N_GROUP = FT // GT
CMP_LEN, CMP_STRIDE, CMP_HID = 32, 16, 256
N_CMP = (SEQ - CMP_LEN) // CMP_STRIDE + 1
BUCKETS, REL_MAX = 32, 2048
EPS = 1e-6
SCALE = HD ** -0.5
BIG = 1e30
FILL_NORM, FILL_A, FILL_AT, FILL_Y, FILL_D, FILL_UW = 10, 2, 3, 2, 2, 3
QW = 512
RING = 8
AHEAD = 4
TW_DIL, TW_NSA = 512, 896
YLEN = 1024
C_G, C_BETA, C_GC, C_BG, C_KD = range(5)
LEVELS = (2, 4, 8, 16, 32)
(K_ID, K_ONE, K_TRI, K_BLK, K_ML, K_MU, K_M1, K_M1T, K_REV) = range(9)
K_LV = 9
N_CST = K_LV + len(LEVELS)
N_SMALL = 2 * DN_H + 3 * NSA_H
TICKS = {"dn_dve": 21, "dn_act": 4, "dil_dve": 16, "nsa_dve": 50, "dil_act": 10, "nsa_act": 6,
         "ffn_dve": 26, "ffn_act": 24}


class Count:

    def __init__(self):
        self.n, self.reg, self.per = 0, None, 0

    def at(self, k=0, div=1, scale=1):
        v = scale * ((self.n + k) // div)
        return v if self.reg is None else self.reg * (scale * self.per // div) + v

    def enter(self, reg, per):
        self.reg, self.per, self.first = reg, per, self.n

    def leave(self, times, what):
        assert self.n - self.first == self.per, (what, self.n - self.first, self.per)
        self.n, self.reg = self.first + self.per * times, None


@contextmanager
def repeat(engine, times, *counts):
    with engine.Fori(0, times) as i:
        for c, per, _ in counts:
            c.enter(i, per)
        yield i
    for c, per, name in counts:
        c.leave(times, name)


def bc(ap, n):
    return ap[:, :, None].to_broadcast([ap.shape[0], ap.shape[1], n])


def program(nc, t):
    with ExitStack() as ctx:
        def sem(name):
            return ctx.enter_context(nc.semaphore(name))

        def sb(c, name, shape, dt=F32):
            return c.enter_context(nc.sbuf_tensor(name, shape, dt))

        h_hi = sb(ctx, "h_hi", [P, KT, SEQ], F32R)
        h_lo = sb(ctx, "h_lo", [P, KT, SEQ], F32R)
        w_raw = sb(ctx, "w_raw", [P, 2, 4 * QW])
        w_hi = sb(ctx, "w_hi", [P, RING, QW], F32R)
        w_lo = sb(ctx, "w_lo", [P, RING, QW], F32R)
        cst = sb(ctx, "cst", [P, N_CST, P])
        eps_t = sb(ctx, "eps_t", [P, 1])
        one_t = sb(ctx, "one_t", [P, 1])
        bank = [ctx.enter_context(nc.psum_tensor(f"bank{i}", [P, QW], F32)) for i in range(8)]
        PB, W = bank[:4], bank[4:]
        ident, ones = cst[:, K_ID, :], cst[:, K_ONE, :]
        ob = [sb(ctx, f"head_out{g}", [P, SEQ]) for g in range(NSA_G)]
        mix_d = nc.dram_tensor("mix_scratch", (KT, P, SEQ), F32).ap()
        rev_d = nc.dram_tensor("bias_scratch", (DIL_H + NSA_H, YLEN), F32)

        raw_in = [sem("raw_in_even"), sem("raw_in_odd")]
        hi_done = sem("hi_done")
        lo_done = sem("lo_done")
        q_used = sem("q_used")
        pe_q, act_q, dve_q, sp_u = Count(), Count(), Count(), Count()

        def load_unit(sp):
            if sp_u.n >= 2:
                sp.wait_ge(lo_done, sp_u.at(-1, scale=4))
            u = sp_u.at()
            s = sp_u.n % 2
            src = t["weights"][u, :, :] if sp_u.reg is None else t["weights"][bass.ds(u, 1), :, :]
            if sp_u.reg is not None:
                src = src.rearrange("u p n -> p (u n)")
            sp.dma_start(w_raw[:, s, :], src).then_inc(raw_in[s], 16)
            sp_u.n += 1

        def load_units(sp, last):
            if sp_u.n < 2:
                load_unit(sp)
                load_unit(sp)
            if sp_u.n % 2 and sp_u.n < last:
                load_unit(sp)
            pairs = (last - sp_u.n) // 2
            if pairs > 0:
                with repeat(sp, pairs, (sp_u, 2, "units")):
                    load_unit(sp)
                    load_unit(sp)
            if sp_u.n < last:
                load_unit(sp)

        def raw_quarter(c):
            return w_raw[:, (c.n // 4) % 2, (c.n % 4) * QW:(c.n % 4 + 1) * QW]

        def split_hi(act, n=1):
            for _ in range(n):
                act.wait_ge(raw_in[(act_q.n // 4) % 2], act_q.at(8, div=8, scale=16))
                if act_q.n >= RING:
                    act.wait_ge(q_used, act_q.at(1 - RING))
                nc.scalar.activation(w_hi[:, act_q.n % RING, :], raw_quarter(act_q), ACT.Copy)\
                    .then_inc(hi_done, 1)
                act_q.n += 1

        def split_lo(dve, n=1):
            for _ in range(n):
                dve.wait_ge(hi_done, dve_q.at(1))
                s = dve_q.n % RING
                nc.vector.tensor_tensor(w_lo[:, s, :], raw_quarter(dve_q), w_hi[:, s, :].bitcast(F32),
                                        ALU.subtract).then_inc(lo_done, 1)
                dve_q.n += 1

        dve_chain, act_chain = sem("dve_chain"), sem("act_chain")
        dve_c, act_c = Count(), Count()

        def step(ins):
            ins.then_inc(dve_chain, 1)
            dve_c.n += 1

        def settle(dve):
            dve.wait_ge(dve_chain, dve_c.at())

        def link(dve, ins):
            step(ins)
            settle(dve)

        def astep(ins):
            ins.then_inc(act_chain, 1)
            act_c.n += 1

        def asettle(act):
            act.wait_ge(act_chain, act_c.at())

        def alink(act, ins):
            astep(ins)
            asettle(act)

        def project(pe, pb, kt):
            s = pe_q.n % RING
            if kt % 4 == 0:
                pe.wait_ge(lo_done, pe_q.at(1))
            k = slice(kt % 4 * P, (kt % 4 + 1) * P)
            for n, (a, b) in enumerate(((w_hi, h_hi), (w_lo, h_hi), (w_hi, h_lo))):
                m = nc.tensor.matmul(PB[pb][:], a[:, s, k], b[:, kt, :],
                                     start=(kt == 0 and n == 0), stop=(kt == KT - 1 and n == 2))
            if kt % 4 == 3:
                m.then_inc(q_used, 1)
                pe_q.n += 1

        def filler(pe, units, before=None, first=0):
            steps = iter([(u, kt) for u in range(first, units) for kt in range(KT)])

            def fill(n):
                for u, kt in islice(steps, n):
                    if kt == 0 and before is not None:
                        before(u)
                    project(pe, u, kt)
            return fill

        tok = sb(ctx, "tok", [P, DN_H, 5, TB])
        gate = sb(ctx, "gate", [P, 3 * NSA_H, TB])
        in_small = sem("in_small")
        const_in, table_in = sem("const_in"), sem("table_in")
        stored = sem("stored")

        def normalize(name, x_ready, g_row, g_in, xs, c1, ident, done=0, rest=None):
            sq, y = sb(c1, f"{name}_sq", [P, D_MODEL]), sb(c1, f"{name}_y", [P, 2, D_MODEL])
            ss, rs = sb(c1, f"{name}_ss", [P, TB]), sb(c1, f"{name}_rs", [P, TB])
            sums, root, y_v, turned, hi, lo = (sem(f"{name}_{k}") for k in ("sums", "root", "y", "turned", "hi", "lo"))
            parts = [(b, kg) for b in range(TB) for kg in range(KT // 4)]

            def h_part(h, i):
                b, kg = parts[i]
                return h[:, 4 * kg:4 * kg + 4, b * P:(b + 1) * P]

            def psum_part(i):
                return PB[i % 4][:].rearrange("p (k n) -> p k n", k=4)

            def act_part(act):
                def root_of(b):
                    x_ready(act, b)
                    if b:
                        act.wait_ge(sums, b)
                    nc.scalar.activation(sq[:, done:], xs[:, b, done:], ACT.Square, accum_out=ss[:, b:b + 1])\
                        .then_inc(sums, 1)
                    act.wait_ge(sums, b + 1)
                    nc.scalar.activation(rs[:, b:b + 1], ss[:, b:b + 1], ACT.Sqrt,
                                         bias=eps_t[:] if rest is None else rest[:, b:b + 1],
                                         scale=1.0 / D_MODEL).then_inc(root, 1)

                root_of(0)
                root_of(1)
                for i, (b, kg) in enumerate(parts):
                    act.wait_ge(turned, i + 1)
                    nc.scalar.activation(h_part(h_hi, i), psum_part(i), ACT.Copy).then_inc(hi, 1)
                    if kg == 3 and b + 2 < TB:
                        root_of(b + 2)

            def dve_part(dve):
                def scaled(b):
                    dve.wait_ge(root, b + 1)
                    link(dve, nc.vector.reciprocal(rs[:, b:b + 1], rs[:, b:b + 1]))
                    if b >= 2:
                        dve.wait_ge(turned, 4 * (b - 1))
                    for kg in range(KT // 4):
                        c = slice(kg * QW, (kg + 1) * QW)
                        nc.vector.scalar_tensor_tensor(y[:, b % 2, c], xs[:, b, c], rs[:, b:b + 1], g_row[:, c],
                                                       ALU.mult, ALU.mult).then_inc(y_v, 1)

                dve.wait_ge(g_in, 16)
                scaled(0)
                scaled(1)
                for i, (b, kg) in enumerate(parts):
                    if kg == 0 and 1 <= b < TB - 1:
                        scaled(b + 1)
                    dve.wait_ge(hi, i + 1)
                    nc.vector.tensor_tensor(h_part(h_lo, i), psum_part(i), h_part(h_hi, i).bitcast(F32), ALU.subtract)\
                        .then_inc(lo, 1)

            def pe_part(pe):
                for i, (b, kg) in enumerate(parts):
                    pe.wait_ge(y_v, i + 1)
                    if i >= 4:
                        pe.wait_ge(lo, i - 3)
                    for k in range(4):
                        kt = 4 * kg + k
                        m = nc.tensor.transpose(PB[i % 4][:, k * P:(k + 1) * P], y[:, b % 2, kt * P:(kt + 1) * P],
                                                ident)
                    m.then_inc(turned, 1)

            return act_part, dve_part, pe_part, y_v, lo

        toep_d = nc.dram_tensor("toeplitz_scratch", (DIL_H + NSA_H, P, TW_NSA), F32).ap()
        PIECES = [(h, 0, QW) for h in range(DIL_H + NSA_H)] + [(h, QW, TW_NSA - QW) for h in range(DIL_H, DIL_H + NSA_H)]
        ROUNDS = (PIECES[:8], PIECES[8:])

        with ExitStack() as c1, nc.Block() as block:
            xs = sb(c1, "xs1", [P, TB, D_MODEL])
            bl, oh = sb(c1, "bias_lhs", [BUCKETS + 2, DIL_H + NSA_H]), sb(c1, "onehot", [BUCKETS + 2, YLEN])
            rev = oh[0:DIL_H + NSA_H, :]
            id1 = sb(c1, "ident_first", [P, P])

            def piece(i, w):
                return xs[:, i // 4, i % 4 * QW:i % 4 * QW + w]

            x_in = [sem(f"x_in{b}") for b in range(TB)]
            const_ready, id_in, bias_in, rev_ps, rev_sb, piece_ps, piece_sb = (
                sem(n) for n in ("const_ready", "id_in", "bias_in", "rev_ps", "rev_sb", "piece_ps", "piece_sb"))
            g_row, g_in = sb(c1, "n1_g", [P, D_MODEL]), sem("n1_g_in")
            n1_act, n1_dve, n1_pe, n1_y, n1_lo = normalize(
                "n1", lambda e, b: e.wait_ge(x_in[b], 16), g_row, g_in, xs, c1, id1[:])

            @block.sync
            def _(sp):
                sp.dma_start(bl[:], t["bias_lhs"]).then_inc(bias_in, 16)
                sp.dma_start(oh[:], t["onehot"]).then_inc(bias_in, 16)
                sp.dma_start(xs[:, 0, :], t["x"][0:P, :]).then_inc(x_in[0], 16)
                sp.dma_start(id1[:], t["cst"][:, K_ID, :]).then_inc(id_in, 16)
                sp.dma_start(g_row[:], t["g1"]).then_inc(g_in, 16)
                sp.dma_start(xs[:, 1, :], t["x"][P:2 * P, :]).then_inc(x_in[1], 16)
                sp.dma_start(cst[:], t["cst"]).then_inc(const_in, 16)
                for b in range(2, TB):
                    sp.dma_start(xs[:, b, :], t["x"][b * P:(b + 1) * P, :]).then_inc(x_in[b], 16)
                sp.wait_ge(rev_sb, 1)
                sp.dma_start(rev_d.ap()[:, :], rev).then_inc(stored, 16)
                sp.wait_ge(stored, 16)
                for r, pieces in enumerate(ROUNDS):
                    sp.wait_ge(n1_y, 8 * (r + 1))
                    for i, (h, c, w) in enumerate(pieces):
                        sp.dma_start(piece(8 * r + i, w), bass.AP(tensor=rev_d, offset=h * YLEN + c, ap=[[1, P], [1, w]]))\
                            .then_inc(table_in, 16)
                    if r == 0:
                        load_units(sp, 2)
                for i, (h, c, w) in enumerate(PIECES):
                    sp.wait_ge(piece_sb, i + 1)
                    sp.dma_start(toep_d[h, :, c:c + w], piece(i, w)).then_inc(stored, 16)
                sp.wait_ge(stored, 16 + 16 * len(PIECES))

            @block.gpsimd
            def _(pool):
                nc.gpsimd.memset(eps_t[:], EPS).then_inc(const_ready, 1)
                nc.gpsimd.memset(one_t[:], 1.0).then_inc(const_ready, 1)

            @block.scalar
            def _(act):
                act.wait_ge(const_ready, 2)
                n1_act(act)
                split_hi(act, AHEAD + 4)

            @block.vector
            def _(dve):
                dve.wait_ge(rev_ps, 1)
                step(nc.vector.tensor_copy(rev[:, 0:512], W[0][0:DIL_H + NSA_H, :]))
                nc.vector.tensor_copy(rev[:, 512:1024], W[1][0:DIL_H + NSA_H, :]).then_inc(rev_sb, 1)
                n1_dve(dve)
                split_lo(dve, AHEAD + 4)
                for i, (h, c, w) in enumerate(PIECES):
                    dve.wait_ge(piece_ps, i + 1)
                    nc.vector.tensor_copy(piece(i, w), W[i % 4][:, 0:w]).then_inc(piece_sb, 1)

            @block.tensor
            def _(pe):
                pe.wait_ge(bias_in, 32)
                for i in range(2):
                    m = nc.tensor.matmul(W[i][0:DIL_H + NSA_H, :], bl[:], oh[:, i * 512:(i + 1) * 512],
                                         start=True, stop=True)
                m.then_inc(rev_ps, 1)
                pe.wait_ge(id_in, 16)
                n1_pe(pe)
                pe.wait_ge(n1_lo, 4 * TB)
                filler(pe, 1)(KT)
                pe.wait_ge(const_in, 16)
                pe.wait_ge(rev_sb, 1)
                for i, (h, c, w) in enumerate(PIECES):
                    if i % 8 == 0:
                        pe.wait_ge(table_in, 16 * (i + 8))
                    if i >= 4:
                        pe.wait_ge(piece_sb, i - 3)
                    nc.tensor.matmul(W[i % 4][:, 0:w], cst[:, K_REV, :], piece(i, w), start=True, stop=True)\
                        .then_inc(piece_ps, 1)

        STORED2 = 16 + 16 * len(PIECES)

        with ExitStack() as c2, nc.Block() as block:
            names = ("gb qp kp vp zs qT kT kbg kdec vb m1 D DT EG qg A AT T U Y attnT u wT vn sk osc").split()
            B = {n: sb(c2, f"dn_{n}", [P, SEQ]) for n in names}
            LT = sb(c2, "dn_LT", [P, len(LEVELS), SEQ])
            S = sb(c2, "dn_S", [P, P])
            hp, hg, cw = sb(c2, "dn_hp", [P, 5, TB]), sb(c2, "dn_hg", [P, TB]), sb(c2, "dn_cw", [P, 3, 4])
            cwa = sb(c2, "dn_cwa", [P, DN_H, 3, 4])
            ng = sb(c2, "dn_ng", [P, 1])
            ssq, rms = sb(c2, "dn_ssq", [P, TB]), sb(c2, "dn_rms", [P, TB])
            trash = sb(c2, "dn_trash", [P, P])
            sw = sb(c2, "small_raw", [P, KT, N_SMALL])
            sw_hi = sb(c2, "small_hi", [P, KT, N_SMALL], F32R)
            sw_lo = sb(c2, "small_lo", [P, KT, N_SMALL], F32R)
            st, sk = sb(c2, "small_t", [N_SMALL, SEQ]), sb(c2, "small_tok", [P, TB, N_SMALL])
            ab = sb(c2, "a_log_bc", [P, 2, DN_H])
            xa, ax, gr, gt, eb = (sb(c2, f"gate_{n}", [P, DN_H, TB]) for n in ("xa", "ax", "gr", "gt", "eb"))
            ps_small, sm_hi, sm_lo, sm_t, sm_tp, sm_tok, g_e, g_a, g_cum, g_ok = (
                sem(n) for n in ("ps_small sm_hi sm_lo sm_t sm_tp sm_tok g_exp g_act g_cum g_ok").split())

            def v3(ap):
                return ap.rearrange("p (b n) -> p b n", b=TB)

            def c3b(k):
                return cst[:, k:k + 1, :].to_broadcast([P, TB, P])

            par_in = sem("dn_par_in")
            (g_rep, grow_ps, conv_v, z_free, silu_a, sqr_a, norm_ps, root_a, qk_n, tr_ps, tr_used, masks_v, decay_a,
             kk_ps, qk_ps, a_v, at_ps, at_a, lt_g, t_v, u_v, y_ps, y_a, d_ps, uw_ps, uw_a, ready_v, v_ps, vn_v,
             s_ps, s_v, o_a, osc_v, o_ps, o_v) = (
                sem(f"dn_{n}") for n in (
                    "g_rep grow_ps conv_v z_free silu_a sqr_a norm_ps root_a qk_n tr_ps tr_used masks_v decay_a "
                    "kk_ps qk_ps a_v at_ps at_a lt_g t_v u_v y_ps y_a d_ps uw_ps uw_a ready_v v_ps vn_v "
                    "s_ps s_v o_a osc_v o_ps o_v").split())
            NL = len(LEVELS)
            EARLY = 14

            def small_pe(pe):
                pe.wait_ge(sm_lo, 1)
                for kt in range(KT):
                    for n, (a, b) in enumerate(((sw_hi, h_hi), (sw_lo, h_hi), (sw_hi, h_lo))):
                        m = nc.tensor.matmul(W[0][0:N_SMALL, :], a[:, kt, :], b[:, kt, :],
                                             start=(kt == 0 and n == 0), stop=(kt == KT - 1 and n == 2))
                m.then_inc(ps_small, 1)

            def small_turn_pe(pe):
                pe.wait_ge(sm_t, 1)
                for b in range(TB):
                    m = nc.tensor.transpose(W[1][:, b * 32:b * 32 + N_SMALL], st[:, b * P:(b + 1) * P],
                                            cst[0:N_SMALL, K_ID, 0:N_SMALL])
                m.then_inc(sm_tp, 1)

            def cumulate_pe(pe):
                pe.wait_ge(g_ok, 1)
                flat = gr[:].rearrange("p h b -> p (h b)")
                nc.tensor.matmul(W[2][:, 0:DN_H * TB], cst[:, K_TRI, :], flat, start=True, stop=True)
                nc.tensor.matmul(W[3][:, 0:DN_H * TB], cst[:, K_BLK, :], flat, start=True, stop=True).then_inc(g_cum, 1)

            def small_act(act):
                act.wait_ge(ps_small, 1)
                nc.scalar.activation(st[:], W[0][0:N_SMALL, :], ACT.Copy).then_inc(sm_t, 1)
                split_hi(act, 3)
                act.wait_ge(sm_tok, 2)
                astep(nc.scalar.activation(eb[:], sk[:, :, 0:DN_H].rearrange("p b h -> p h b"), ACT.Exp,
                                           scale=-1.0))
                astep(nc.scalar.activation(gate[:], sk[:, :, 2 * DN_H:].rearrange("p b c -> p c b"), ACT.Exp,
                                           scale=-1.0))
                astep(nc.scalar.activation(ab[:, 0, :], ab[:, 0, :], ACT.Exp))
                alink(act, nc.scalar.activation(ax[:], xa[:], ACT.Abs))
                alink(act, nc.scalar.activation(ax[:], ax[:], ACT.Exp, scale=-1.0))
                nc.scalar.activation(ax[:], ax[:], ACT.Ln, bias=one_t[:]).then_inc(g_a, 1)
                split_hi(act, 3)
                act.wait_ge(g_ok, 2)
                nc.scalar.activation(tok[:, :, C_BG, :], tok[:, :, C_GC, :], ACT.Exp).then_inc(g_e, 1)
                nc.scalar.activation(tok[:, :, C_KD, :], gt[:], ACT.Exp).then_inc(g_e, 1)

            def small_dve(dve):
                split_lo(dve, 3)
                dve.wait_ge(sm_tp, 1)
                nc.vector.tensor_copy(sk[:], W[1][:, 0:TB * 32].rearrange("p (b c) -> p b c", b=TB)[:, :, 0:N_SMALL])\
                    .then_inc(sm_tok, 1)
                dve.wait_ge(sm_tok, 1)
                nc.vector.tensor_tensor(xa[:], sk[:, :, DN_H:2 * DN_H].rearrange("p b h -> p h b"),
                                        bc(ab[:, 1, :], TB), ALU.add).then_inc(sm_tok, 1)
                dve.wait_ge(g_a, 1)
                link(dve, nc.vector.tensor_scalar(eb[:], eb[:], 1.0, None, ALU.add))
                step(nc.vector.reciprocal(tok[:, :, C_BETA, :], eb[:]))
                link(dve, nc.vector.tensor_scalar(gate[:], gate[:], 1.0, None, ALU.add))
                step(nc.vector.reciprocal(gate[:], gate[:]))
                link(dve, nc.vector.scalar_tensor_tensor(gr[:], xa[:], 0.0, ax[:], ALU.max, ALU.add))
                link(dve, nc.vector.scalar_tensor_tensor(gr[:], gr[:], -1.0, bc(ab[:, 0, :], TB), ALU.mult, ALU.mult))
                nc.vector.tensor_copy(tok[:, :, C_G, :], gr[:]).then_inc(g_ok, 1)
                split_lo(dve, 3)
                dve.wait_ge(g_cum, 1)
                link(dve, nc.vector.tensor_copy(tok[:, :, C_GC, :], W[2][:, 0:DN_H * TB].rearrange("p (h b) -> p h b", h=DN_H)))
                nc.vector.tensor_tensor(gt[:], W[3][:, 0:DN_H * TB].rearrange("p (h b) -> p h b", h=DN_H),
                                        tok[:, :, C_GC, :], ALU.subtract).then_inc(g_ok, 1)
                dve.wait_ge(g_e, 2)
                link(dve, nc.vector.tensor_tensor(tok[:, :, C_BG, :], tok[:, :, C_BG, :], tok[:, :, C_BETA, :], ALU.mult))

            def dn_pe(pe, h, next_units):
                def bank_read(u):
                    if u < 3:
                        pe.wait_ge(conv_v, 3 * h + u + 1)
                    else:
                        pe.wait_ge(z_free, h + 1)

                fill = filler(pe, next_units, bank_read)
                pe.wait_ge(g_rep, h + 1)
                for b in range(TB):
                    m = nc.tensor.matmul(W[0][:, b * P:(b + 1) * P], B["gb"][:, b * P:(b + 1) * P],
                                         cst[:, K_TRI, :], start=True, stop=True)
                m.then_inc(grow_ps, 1)
                pe.wait_ge(sqr_a, 2 * h + 2)
                pe.wait_ge(o_v, h + 1)
                nc.tensor.matmul(W[1][:], ones, B["Y"][:], start=True, stop=True).then_inc(norm_ps, 1)
                nc.tensor.matmul(W[2][:], ones, B["sk"][:], start=True, stop=True).then_inc(norm_ps, 1)
                pe.wait_ge(silu_a, 3 * h + 3)
                for b in range(TB):
                    m = nc.tensor.transpose(W[3][:, b * P:(b + 1) * P], B["vp"][:, b * P:(b + 1) * P], ident)
                m.then_inc(tr_ps, 1)
                fill(FILL_NORM)
                pe.wait_ge(qk_n, 2 * h + 2)
                for b in range(TB):
                    m = nc.tensor.matmul(W[2][:, b * P:(b + 1) * P], B["kT"][:, b * P:(b + 1) * P],
                                         B["kT"][:, b * P:(b + 1) * P], start=True, stop=True)
                m.then_inc(kk_ps, 1)
                for b in range(TB):
                    m = nc.tensor.transpose(W[1][:, b * P:(b + 1) * P], B["kT"][:, b * P:(b + 1) * P], ident)
                m.then_inc(tr_ps, 1)
                fill(2)
                pe.wait_ge(tr_used, 2 * h + 1)
                for b in range(TB):
                    m = nc.tensor.matmul(W[3][:, b * P:(b + 1) * P], B["kT"][:, b * P:(b + 1) * P],
                                         B["qT"][:, b * P:(b + 1) * P], start=True, stop=True)
                m.then_inc(qk_ps, 1)
                fill(FILL_A)
                pe.wait_ge(a_v, h + 1)
                pe.wait_ge(decay_a, 3 * h + 1)
                for b in range(TB):
                    m = nc.tensor.transpose(W[0][:, b * P:(b + 1) * P], B["A"][:, b * P:(b + 1) * P], ident)
                m.then_inc(at_ps, 1)
                fill(FILL_AT)
                for lv in range(NL):
                    pe.wait_ge(lt_g, NL * h + lv + 1)
                    pe.wait_ge(t_v, NL * h + lv + 1)
                    if lv == 0:
                        pe.wait_ge(tr_used, 2 * h + 2)
                    for b in range(TB):
                        c = slice(b * P, (b + 1) * P)
                        m = nc.tensor.matmul(W[1][:, c], LT[:, lv, c], B["T"][:, c], start=True, stop=True)
                    m.then_inc(y_ps, 1)
                    fill(FILL_Y)
                    pe.wait_ge(y_a, NL * h + lv + 1)
                    pe.wait_ge(u_v, (NL + 1) * h + lv + 1)
                    if lv == 0:
                        pe.wait_ge(ready_v, 2 * h + 1)
                    if lv < NL - 1:
                        for b in range(TB):
                            c = slice(b * P, (b + 1) * P)
                            m = nc.tensor.matmul(W[2][:, c], B["U"][:, c], B["Y"][:, c], start=True, stop=True)
                        m.then_inc(d_ps, 1)
                    for b in range(TB):
                        c = slice(b * P, (b + 1) * P)
                        m = nc.tensor.matmul(W[3][:, c], B["Y"][:, c], B["U"][:, c], start=True, stop=True)
                    m.then_inc(d_ps, 1)
                    fill(FILL_D)
                pe.wait_ge(u_v, (NL + 1) * h + NL + 1)
                for b in range(TB):
                    c = slice(b * P, (b + 1) * P)
                    m = nc.tensor.matmul(W[2][:, c], B["kbg"][:, c], B["U"][:, c], start=True, stop=True)
                m.then_inc(uw_ps, 1)
                for b in range(TB):
                    c = slice(b * P, (b + 1) * P)
                    m = nc.tensor.matmul(W[1][:, c], B["U"][:, c], B["vb"][:, c], start=True, stop=True)
                m.then_inc(uw_ps, 1)
                fill(FILL_UW)
                for c in range(N_CHUNK):
                    b, o = c // 2, CHUNK * (c % 2)
                    rows, cc = slice(o, o + CHUNK), slice(c * CHUNK, (c + 1) * CHUNK)
                    cb = slice(b * P, (b + 1) * P)
                    if c == 0:
                        pe.wait_ge(uw_a, 2 * h + 2)
                        pe.wait_ge(ready_v, 2 * h + 2)
                    pe.wait_ge(s_v, (N_CHUNK + 1) * h + c + 1)
                    nc.tensor.matmul(W[1][rows, cb], B["wT"][:, cc], S[:], start=True, stop=True)\
                        .then_inc(v_ps, 1)
                    nc.tensor.matmul(W[3][rows, cb], B["qg"][:, cc], S[:], start=True, stop=False)
                    fill(1)
                    pe.wait_ge(vn_v, N_CHUNK * h + c + 1)
                    nc.tensor.matmul(W[2][:, 0:P], B["kdec"][rows, cb], B["vn"][rows, cb],
                                     start=True, stop=True).then_inc(s_ps, 1)
                    nc.tensor.matmul(W[3][rows, cb], B["attnT"][rows, cc.start:cc.stop],
                                     B["vn"][rows, cb], start=False, stop=True).then_inc(s_ps, 1)
                    fill(1)
                fill(1000)
                pe.wait_ge(osc_v, h + 1)
                for b in range(TB):
                    m = nc.tensor.transpose(W[1][:, b * P:(b + 1) * P], B["osc"][:, b * P:(b + 1) * P], ident)
                m.then_inc(o_ps, 1)

            def silu_part(act, h):
                for i, n in enumerate(("qp", "kp", "vp")):
                    act.wait_ge(conv_v, 3 * h + i + 1)
                    nc.scalar.activation(B[n][:], B[n][:], ACT.Silu).then_inc(silu_a, 1)
                    act.wait_ge(silu_a, 3 * h + i + 1)
                    if i < 2:
                        nc.scalar.activation(B[("Y", "sk")[i]][:], B[n][:], ACT.Square).then_inc(sqr_a, 1)

            def of_head(table, h):
                if isinstance(h, int):
                    return table[:, h]
                return table[:, bass.ds(h, 1)].rearrange("p a c b -> p (a c) b")

            def conv_steps(dve, h):
                step(nc.vector.tensor_copy(hg[:], of_head(tok, h)[:, C_G, :]))
                link(dve, nc.vector.tensor_copy(cw[:], of_head(cwa, h)))
                nc.vector.tensor_copy(v3(B["gb"][:]), bc(hg[:], P)).then_inc(g_rep, 1)
                yield
                for i, n in enumerate(("qp", "kp", "vp")):
                    dve.wait_ge(q_used, 16 * h + 4 * i + 4)
                    step(nc.vector.tensor_scalar(B[n][:], PB[i][:], cw[:, i, 3:4], None, ALU.mult))
                    yield
                    for k in (1, 2, 3):
                        settle(dve)
                        ins = nc.vector.scalar_tensor_tensor(
                            B[n][:, k:SEQ], PB[i][:, 0:SEQ - k], cw[:, i, 3 - k:4 - k], B[n][:, k:SEQ],
                            ALU.mult, ALU.add)
                        if k < 3:
                            step(ins)
                        else:
                            ins.then_inc(conv_v, 1)
                        yield

            def dn_act(act, h, splits, last):
                left = [splits]

                def sp_hi(n):
                    n = min(n, left[0])
                    left[0] -= n
                    split_hi(act, n)

                for i, n in enumerate(("A", "AT")):
                    act.wait_ge(norm_ps, 2 * h + i + 1)
                    nc.scalar.activation(B[n][:], W[1 + i][:], ACT.Sqrt, bias=eps_t[:]).then_inc(root_a, 1)
                sp_hi(2)
                act.wait_ge(masks_v, h + 1)
                nc.scalar.activation(B["EG"][:], W[0][:], ACT.Exp).then_inc(decay_a, 1)
                nc.scalar.activation(B["D"][:], B["D"][:], ACT.Exp, scale=-1.0).then_inc(decay_a, 1)
                nc.scalar.activation(B["DT"][:], B["DT"][:], ACT.Exp).then_inc(decay_a, 1)
                sp_hi(2)
                act.wait_ge(q_used, 16 * h + 16)
                nc.scalar.activation(B["zs"][:], PB[3][:], ACT.Silu).then_inc(z_free, 1)
                act.wait_ge(at_ps, h + 1)
                nc.scalar.activation(B["AT"][:], W[0][:], ACT.Copy).then_inc(at_a, 1)
                sp_hi(2)
                for lv in range(NL):
                    act.wait_ge(y_ps, NL * h + lv + 1)
                    nc.scalar.activation(B["Y"][:], W[1][:], ACT.Copy).then_inc(y_a, 1)
                    sp_hi(1)
                for i, n in enumerate(("wT", "u")):
                    act.wait_ge(uw_ps, 2 * h + i + 1)
                    nc.scalar.activation(B[n][:], W[2 - i][:], ACT.Copy).then_inc(uw_a, 1)
                sp_hi(16)
                if not last:
                    silu_part(act, h + 1)
                act.wait_ge(s_ps, 2 * N_CHUNK * (h + 1))
                for b in range(TB):
                    alink(act, nc.scalar.activation(trash[:], W[3][:, b * P:(b + 1) * P], ACT.Square,
                                                    accum_out=ssq[:, b:b + 1]))
                nc.scalar.activation(rms[:], ssq[:], ACT.Sqrt, bias=eps_t[:], scale=1.0 / HD).then_inc(o_a, 1)
                act.wait_ge(o_a, h + 1)

            def dn_dve(dve, h, splits, last):
                left = [min(splits, EARLY)]

                def sp_lo(n):
                    n = min(n, left[0])
                    left[0] -= n
                    split_lo(dve, n)

                link(dve, nc.vector.tensor_copy(hp[:], of_head(tok, h)))
                for i, (r, src, dst, sc) in enumerate((("A", "qp", "qT", SCALE), ("AT", "kp", "kT", 1.0))):
                    dve.wait_ge(root_a, 2 * h + i + 1)
                    link(dve, nc.vector.reciprocal(B[r][:], B[r][:]))
                    nc.vector.scalar_tensor_tensor(B[dst][:], B[src][:], sc, B[r][:], ALU.mult, ALU.mult)\
                        .then_inc(qk_n, 1)
                dve.wait_ge(grow_ps, h + 1)
                link(dve, nc.vector.tensor_tensor(v3(B["m1"][:]), v3(W[0][:]), bc(hp[:, C_GC, :], P), ALU.subtract))
                step(nc.vector.tensor_tensor(v3(B["D"][:]), v3(B["m1"][:]), c3b(K_ML), ALU.add))
                nc.vector.tensor_tensor(v3(B["DT"][:]), v3(B["m1"][:]), c3b(K_MU), ALU.add).then_inc(masks_v, 1)
                dve.wait_ge(tr_ps, 2 * h + 1)
                nc.vector.tensor_tensor(v3(B["vb"][:]), v3(W[3][:]), bc(hp[:, C_BETA, :], P), ALU.mult)\
                    .then_inc(tr_used, 1)
                dve.wait_ge(kk_ps, h + 1)
                dve.wait_ge(decay_a, 3 * h + 2)
                dve.wait_ge(qk_n, 2 * h + 2)
                link(dve, nc.vector.tensor_tensor(B["A"][:], W[2][:], B["D"][:], ALU.mult))
                nc.vector.tensor_tensor(v3(B["A"][:]), v3(B["A"][:]), bc(hp[:, C_BETA, :], P), ALU.mult)\
                    .then_inc(a_v, 1)
                dve.wait_ge(a_v, h + 1)
                link(dve, nc.vector.tensor_tensor(v3(B["T"][:]), v3(B["A"][:]), c3b(K_M1), ALU.mult))
                nc.vector.tensor_tensor(v3(B["T"][:]), c3b(K_ID), v3(B["T"][:]), ALU.subtract).then_inc(t_v, 1)
                dve.wait_ge(tr_ps, 2 * h + 2)
                step(nc.vector.tensor_tensor(v3(B["kbg"][:]), v3(W[1][:]), bc(hp[:, C_BG, :], P), ALU.mult))
                nc.vector.tensor_tensor(v3(B["kdec"][:]), v3(W[1][:]), bc(hp[:, C_KD, :], P), ALU.mult)\
                    .then_inc(tr_used, 1)
                sp_lo(1)
                dve.wait_ge(at_a, h + 1)
                link(dve, nc.vector.tensor_tensor(v3(B["U"][:]), v3(B["AT"][:]), c3b(K_M1T), ALU.mult))
                nc.vector.tensor_tensor(v3(B["U"][:]), c3b(K_ID), v3(B["U"][:]), ALU.subtract).then_inc(u_v, 1)
                dve.wait_ge(decay_a, 3 * h + 3)
                dve.wait_ge(qk_ps, h + 1)
                nc.vector.tensor_tensor(B["attnT"][:], W[3][:], B["DT"][:], ALU.mult).then_inc(ready_v, 1)
                sp_lo(3)
                for lv in range(NL):
                    if lv < NL - 1:
                        dve.wait_ge(d_ps, (2 * NL - 1) * h + 2 * lv + 1)
                        dve.wait_ge(u_v, (NL + 1) * h + lv + 1)
                        nc.vector.tensor_tensor(B["T"][:], B["T"][:], W[2][:], ALU.subtract).then_inc(t_v, 1)
                        dve.wait_ge(d_ps, (2 * NL - 1) * h + 2 * lv + 2)
                    else:
                        dve.wait_ge(d_ps, (2 * NL - 1) * (h + 1))
                    nc.vector.tensor_tensor(B["U"][:], B["U"][:], W[3][:], ALU.subtract).then_inc(u_v, 1)
                    sp_lo(2 if lv < 3 else 1)
                nc.vector.memset(S[:], 0.0).then_inc(s_v, 1)
                nc.vector.tensor_tensor(B["qg"][:], B["qT"][:], B["EG"][:], ALU.mult).then_inc(ready_v, 1)
                convs = iter(()) if last else conv_steps(dve, h + 1)
                next(convs, None)
                sp_lo(16)
                dve.wait_ge(uw_a, 2 * h + 2)
                for c in range(N_CHUNK):
                    b, o = c // 2, CHUNK * (c % 2)
                    rows, cb = slice(o, o + CHUNK), slice(b * P, (b + 1) * P)
                    dve.wait_ge(v_ps, N_CHUNK * h + c + 1)
                    nc.vector.tensor_tensor(B["vn"][rows, cb], B["u"][rows, cb], W[1][rows, cb], ALU.subtract)\
                        .then_inc(vn_v, 1)
                    end = (c + 1) * CHUNK - 1
                    dve.wait_ge(s_v, (N_CHUNK + 1) * h + c + 1)
                    dve.wait_ge(s_ps, 2 * N_CHUNK * h + 2 * c + 1)
                    nc.vector.scalar_tensor_tensor(S[:], S[:], B["EG"][:, end:end + 1], W[2][:, 0:P],
                                                   ALU.mult, ALU.add).then_inc(s_v, 1)
                    next(convs, None)
                    if c % 2:
                        next(convs, None)
                    if c in (3, 6) and splits > EARLY:
                        split_lo(dve, 1)
                for _ in convs:
                    pass
                dve.wait_ge(o_a, h + 1)
                link(dve, nc.vector.reciprocal(rms[:], rms[:]))
                nc.vector.tensor_tensor(v3(B["osc"][:]), v3(W[3][:]), bc(rms[:], P), ALU.mult).then_inc(osc_v, 1)
                dve.wait_ge(stored, 16 * h + STORED2)
                dve.wait_ge(o_ps, h + 1)
                nc.vector.scalar_tensor_tensor(ob[0][:], W[1][:], ng[:], B["zs"][:], ALU.mult, ALU.mult)\
                    .then_inc(o_v, 1)
                dve.wait_ge(o_v, h + 2)

            def dn_pool(pool, h):
                for lv in range(NL):
                    pool.wait_ge(at_a, h + 1)
                    nc.gpsimd.tensor_tensor(v3(LT[:, lv, :]), v3(B["AT"][:]), c3b(K_LV + lv), ALU.mult)\
                        .then_inc(lt_g, 1)

            @block.sync
            def _(sp):
                sp.dma_start(sw[:], t["w_small"]).then_inc(in_small, 16)
                sp.dma_start(ab[:], t["ab"]).then_inc(in_small, 16)
                sp.dma_start(cwa[:], t["dn_conv"]).then_inc(par_in, 16)
                sp.dma_start(ng[:], t["dn_norm"]).then_inc(par_in, 16)
                for h in range(DN_H):
                    load_units(sp, (16 + 16 * min(h + 1, DN_H - 1) + 12 * (h == DN_H - 1) + AHEAD + 3) // 4)
                    sp.wait_ge(o_v, h + 2)
                    sp.dma_start(mix_d[h, :, :], ob[0][:]).then_inc(stored, 16)

            @block.gpsimd
            def _(pool):
                with pool.Fori(0, DN_H) as h:
                    dn_pool(pool, h)

            @block.tensor
            def _(pe):
                fill = filler(pe, 4, first=1)
                fill(12)
                small_pe(pe)
                fill(4)
                small_turn_pe(pe)
                fill(14)
                cumulate_pe(pe)
                fill(1000)
                with repeat(pe, DN_H - 1, (pe_q, 16, "dn_pe quarters")) as h:
                    dn_pe(pe, h, 4)
                dn_pe(pe, DN_H - 1, 3)

            @block.scalar
            def _(act):
                act.wait_ge(in_small, 32)
                nc.scalar.activation(sw_hi[:], sw[:], ACT.Copy).then_inc(sm_hi, 1)
                small_act(act)
                split_hi(act, 6)
                silu_part(act, 0)
                with repeat(act, DN_H - 1, (act_q, 16, "dn_act quarters"), (act_c, TICKS["dn_act"], "dn_act")) as h:
                    dn_act(act, h, 16, False)
                dn_act(act, DN_H - 1, 12, True)

            @block.vector
            def _(dve):
                dve.wait_ge(sm_hi, 1)
                nc.vector.tensor_tensor(sw_lo[:], sw[:], sw_hi[:].bitcast(F32), ALU.subtract).then_inc(sm_lo, 1)
                small_dve(dve)
                dve.wait_ge(par_in, 32)
                split_lo(dve, 6)
                nc.vector.memset(S[:], 0.0).then_inc(o_v, 1)
                for _ in conv_steps(dve, 0):
                    pass
                with repeat(dve, DN_H - 1, (dve_q, 16, "dn_dve quarters"), (dve_c, TICKS["dn_dve"], "dn_dve")) as h:
                    dn_dve(dve, h, 16, False)
                dn_dve(dve, DN_H - 1, 12, True)

        (att_s, att_m, att_e, att_p, att_t, att_pt, att_o) = (
            sem(f"att_{n}") for n in (
                "scores",
                "max",
                "exp",
                "probs",
                "turned",
                "probs_t",
                "out"))

        def scores(n, b, q, k):
            m = nc.tensor.matmul(W[b % 2][:, 0:(b + 1) * P], q[:, b * P:(b + 1) * P], k[:, 0:(b + 1) * P],
                                 start=True, stop=True)
            m.then_inc(att_s, 1)

        def attend_pe(pe, n, k, q, v, lg, PT, out, start, stop, fill, fills, after=None):
            for b in range(TB):
                pe.wait_ge(att_p, 4 * n + b + 1)
                for sb_ in range(b + 1):
                    m = nc.tensor.transpose(W[2 + b % 2][:, sb_ * P:(sb_ + 1) * P], lg[:, b, sb_ * P:(sb_ + 1) * P],
                                            ident)
                m.then_inc(att_t, 1)
                if b < 2:
                    pe.wait_ge(att_m, 4 * n + b + 1)
                    scores(n, b + 2, q, k)
                elif after is not None:
                    pe.wait_ge(att_m, 4 * n + b + 1)
                    scores(n + 1, b - 2, after[0], after[1])
                fill(fills[b])
                if b < 2:
                    pe.wait_ge(att_pt, 4 * n + b + 1)
            pe.wait_ge(att_pt, 4 * n + 4)
            for sb_ in range(TB):
                m = nc.tensor.matmul(out[:, sb_ * P:SEQ], v[:, sb_, :], PT[:, sb_, sb_ * P:SEQ],
                                     start=(start and sb_ == 0), stop=(stop and sb_ == TB - 1))
            m.then_inc(att_o, 1)

        def att_rows(dve, n, b, lg, nm, bias):
            dve.wait_ge(att_s, 4 * n + b + 1)
            width = (b + 1) * P
            link(dve, nc.vector.tensor_tensor(lg[:, b, 0:width], W[b % 2][:, 0:width],
                                              bias(TB * P - width, TB * P), ALU.add))
            nc.vector.tensor_reduce(nm[:, b:b + 1], lg[:, b, 0:width], AX.X, ALU.max, negate=True).then_inc(att_m, 1)

        def att_norm(dve, n, b, lg, den, gates):
            width = (b + 1) * P
            dve.wait_ge(att_e, 4 * n + b + 1)
            link(dve, nc.vector.reciprocal(den[:, b:b + 1], den[:, b:b + 1]))
            if gates is None:
                ins = nc.vector.tensor_scalar(lg[:, b, 0:width], lg[:, b, 0:width], den[:, b:b + 1], None, ALU.mult)
            else:
                ins = nc.vector.tensor_scalar(lg[:, b, 0:width], lg[:, b, 0:width], den[:, b:b + 1],
                                              gates[:, b:b + 1], ALU.mult, ALU.mult)
            ins.then_inc(att_p, 1)

        def attend_dve(dve, n, lg, nm, den, bias, gates, first, split):
            for b in range(TB):
                if not first:
                    dve.wait_ge(att_t, 4 * (n - 1) + b + 1)
                att_rows(dve, n, b, lg, nm, bias)
                if b >= 1:
                    att_norm(dve, n, b - 1, lg, den, gates)
                split(1)
            att_norm(dve, n, TB - 1, lg, den, gates)

        def attend_act(act, n, lg, nm, den, PT, first, split):
            def turn(b):
                act.wait_ge(att_t, 4 * n + b + 1)
                if b == 0 and not first:
                    act.wait_ge(att_o, n)
                nc.scalar.activation(PT[:, 0:b + 1, b * P:(b + 1) * P],
                                     W[2 + b % 2][:, 0:(b + 1) * P].rearrange("p (s n) -> p s n", n=P),
                                     ACT.Copy).then_inc(att_pt, 1)

            for b in range(TB):
                act.wait_ge(att_m, 4 * n + b + 1)
                nc.scalar.activation(lg[:, b, 0:(b + 1) * P], lg[:, b, 0:(b + 1) * P], ACT.Exp,
                                     bias=nm[:, b:b + 1], accum_out=den[:, b:b + 1]).then_inc(att_e, 1)
                split(1)
                if b >= 1:
                    turn(b - 1)
            turn(TB - 1)

        Q3 = 16 * DN_H + 12
        with ExitStack() as c3, nc.Block() as block:
            tab = sb(c3, "dil_tab", [P, DIL_H, TW_DIL])
            lg, PT = sb(c3, "dil_lg", [P, TB, SEQ]), sb(c3, "dil_PT", [P, TB, SEQ])
            qs, ks, vs = (sb(c3, f"dil_{n}", [P, SEQ]) for n in "qkv")
            vt = sb(c3, "dil_vt", [P, TB, P])
            nm, den = sb(c3, "dil_nm", [P, TB]), sb(c3, "dil_den", [P, TB])
            q_ev, kv_ev, vtr_ps, vt_ev, ob_v = (sem(f"dil_{n}") for n in ("q_ev", "kv_ev", "vtr_ps", "vt_ev", "ob_v"))

            def dil_pe(pe, n):
                fill = filler(pe, 3)
                pe.wait_ge(q_ev, n + 1)
                pe.wait_ge(kv_ev, 2 * n + 1)
                scores(n, 0, qs, ks)
                scores(n, 1, qs, ks)
                pe.wait_ge(kv_ev, 2 * n + 2)
                for b in range(TB):
                    m = nc.tensor.transpose(W[3][:, b * P:(b + 1) * P], vs[:, b * P:(b + 1) * P], ident)
                m.then_inc(vtr_ps, 1)
                fill(12)
                pe.wait_ge(vt_ev, n + 1)
                attend_pe(pe, n, ks, qs, vt, lg, PT, PB[3], True, True, fill, (9, 9, 9, 5))
                fill(1000)

            def dil_act(act, n):
                act.wait_ge(q_used, Q3 + 12 * n)
                nc.scalar.activation(ks[:], PB[1][:], ACT.Copy).then_inc(kv_ev, 1)
                nc.scalar.activation(vs[:], PB[2][:], ACT.Copy).then_inc(kv_ev, 1)
                split_hi(act, 2)
                act.wait_ge(vtr_ps, n + 1)
                nc.scalar.activation(vt[:].rearrange("p b n -> p (b n)"), W[3][:], ACT.Copy).then_inc(vt_ev, 1)
                attend_act(act, n, lg, nm, den, PT, True, lambda k: split_hi(act, 2 * k))
                split_hi(act, 2)

            def dil_dve(dve, n, hd):
                settle(dve)
                dve.wait_ge(q_used, Q3 + 12 * n)
                nc.vector.tensor_scalar(qs[:], PB[0][:], SCALE, None, ALU.mult).then_inc(q_ev, 1)
                split_lo(dve, 2)
                dve.wait_ge(table_in, 16 * len(PIECES) + 16)

                def bias(a, e):
                    if isinstance(hd, int):
                        return tab[:, hd, a:e]
                    return tab[:, bass.ds(hd, 1), a:e].rearrange("p a n -> p (a n)")

                attend_dve(dve, n, lg, nm, den, bias, None, True, lambda k: split_lo(dve, 2 * k))
                split_lo(dve, 2)
                dve.wait_ge(att_o, n + 1)
                dve.wait_ge(stored, 16 * DN_H + STORED2 + 16 * n)
                nc.vector.tensor_copy(ob[0][:], PB[3][:]).then_inc(ob_v, 1)
                dve.wait_ge(ob_v, n + 1)

            @block.sync
            def _(sp):
                sp.dma_start(tab[:], toep_d[0:DIL_H, :, 0:TW_DIL].rearrange("h p c -> p h c")).then_inc(table_in, 16)
                for n in range(DIL_H):
                    load_units(sp, (Q3 + 12 * (n + 1) + AHEAD + 3) // 4)
                    sp.wait_ge(ob_v, n + 1)
                    sp.dma_start(mix_d[DN_H + n, :, :], ob[0][:]).then_inc(stored, 16)

            @block.tensor
            def _(pe):
                with repeat(pe, DIL_H // 2, (pe_q, 24, "dil_pe quarters")) as i:
                    dil_pe(pe, 2 * i)
                    dil_pe(pe, 2 * i + 1)

            @block.scalar
            def _(act):
                with repeat(act, DIL_H // 2, (act_q, 24, "dil_act quarters")) as i:
                    dil_act(act, 2 * i)
                    dil_act(act, 2 * i + 1)

            @block.vector
            def _(dve):
                with repeat(dve, DIL_H // 2, (dve_q, 24, "dil_dve quarters"), (dve_c, TICKS["dil_dve"], "dil_dve")) as i:
                    dil_dve(dve, 2 * i, 2 * i)
                    dil_dve(dve, 2 * i + 1, 2 * i + 1)

        Q4 = Q3 + 12 * DIL_H
        N4 = DIL_H
        W1Q = 16
        NC2 = NSA_G * N_CMP
        m_in = [sem(f"mix_in{i}") for i in range(3)]
        m_hi, m_lo = sem("mix_hi"), sem("mix_lo")
        MIX_EARLY = [*range(DN_H + DIL_H)] + [DN_H + DIL_H + NSA_R * g + r for r in range(NSA_R - 1) for g in range(NSA_G)]
        MIX_LATE = [DN_H + DIL_H + NSA_R * g + NSA_R - 1 for g in range(NSA_G)]
        MIX_ORDER = MIX_EARLY + MIX_LATE

        def load_mix(sp, tiles, signal):
            a, e = tiles[0], tiles[-1] + 1
            sp.dma_start(h_lo[:, a:e, :].bitcast(F32), mix_d[a:e, :, :].rearrange("k p n -> p k n")).then_inc(signal, 16)

        def mix_hi(act, i):
            kt = MIX_ORDER[i]
            k = 0 if kt < DN_H + DIL_H else 1 if i < len(MIX_EARLY) else 2
            act.wait_ge(m_in[k], (16, 16 * NSA_G, 16 * NSA_G)[k])
            nc.scalar.activation(h_hi[:, kt, :], h_lo[:, kt, :].bitcast(F32), ACT.Copy).then_inc(m_hi, 1)

        def mix_lo(dve, i):
            kt = MIX_ORDER[i]
            dve.wait_ge(m_hi, i + 1)
            nc.vector.tensor_tensor(h_lo[:, kt, :], h_lo[:, kt, :].bitcast(F32), h_hi[:, kt, :].bitcast(F32), ALU.subtract)\
                .then_inc(m_lo, 1)

        with ExitStack() as c4, nc.Block() as block:
            tab = sb(c4, "nsa_tab", [P, NSA_H, TW_NSA])
            lg, PT = sb(c4, "nsa_lg", [P, TB, SEQ]), sb(c4, "nsa_PT", [P, TB, SEQ])
            qs = [sb(c4, f"nsa_q{g}", [P, SEQ]) for g in range(NSA_G)]
            kT = [[sb(c4, f"nsa_k{br}{g}", [P, SEQ]) for g in range(NSA_G)] for br in range(2)]
            vt = [[sb(c4, f"nsa_v{br}{g}", [P, TB, P]) for g in range(NSA_G)] for br in range(2)]
            cb_own = sb(c4, "cmp_blocks", [P, 2, CMP_LEN, NC2], F32R)
            cb_tab = tab[:].rearrange("p h n -> p (h n)")[:, 0:2 * CMP_LEN * NC2].bitcast(F32R)\
                .rearrange("p (x l c) -> p x l c", x=2, l=CMP_LEN)
            cb_hi, cb_lo = [cb_own[:, 0], cb_tab[:, 0]], [cb_own[:, 1], cb_tab[:, 1]]
            cb = PT[:].rearrange("p b n -> p (b n)")[:, 0:CMP_LEN * NC2].rearrange("p (l c) -> p l c", l=CMP_LEN)
            pos = sb(c4, "cmp_pos", [P, 2, CMP_LEN])
            w2 = sb(c4, "cmp_w2", [P, 2, 2, HD])
            hm = [sb(c4, f"cmp_mid{i}", [NC2, CMP_HID]) for i in range(2)]
            hmT = sb(c4, "cmp_midT", [P, 2, NC2])
            kc, vc = sb(c4, "k_cmp", [P, NC2]), sb(c4, "v_cmp", [N_CMP, NSA_G, HD])
            lc, PTc = sb(c4, "cmp_lg", [P, NSA_G, TB, N_CMP]), sb(c4, "cmp_PT", [N_CMP, NSA_G, SEQ])
            nm, den = sb(c4, "nsa_nm", [P, TB]), sb(c4, "nsa_den", [P, TB])
            nmc, denc = sb(c4, "cmp_nm", [P, NSA_G, TB]), sb(c4, "cmp_den", [P, NSA_G, TB])
            gs = sb(c4, "nsa_gates", [P, 3 * NSA_G, TB])
            (par4, kv_ev, kv_tr, kv_vt, cb_v, cb_a, cb_l, cm_ps, cm_a, cm_tr, cm_t, cm_k, cm_kv, q_ev, c_s, c_m, c_e,
             c_p, c_t, c_pt, c_o, o_v4) = (sem(f"nsa_{n}") for n in (
                 "par kv_ev kv_tr kv_vt cb_v cb_a cb_l cm_ps cm_a cm_tr cm_t cm_k cm_kv q_ev c_s c_m c_e c_p c_t "
                 "c_pt c_o o_v").split())
            UNITS = 12
            BLOCKS_AT = (5, 8)
            V_UNITS = (5, 7, 9, 11)
            Q_CMP = Q4 + 4 * (UNITS - 3)
            Q_HEAD = Q_CMP + 2 * W1Q + 8

            def nsa_pe(pe, r, last):
                fill = filler(pe, 0 if last else 2)
                pe.wait_ge(q_ev, 2 * r + 2)
                for g in range(NSA_G):
                    for b in range(TB):
                        m = nc.tensor.matmul(W[g][:, b * N_CMP:(b + 1) * N_CMP], qs[g][:, b * P:(b + 1) * P],
                                             kc[:, g * N_CMP:(g + 1) * N_CMP], start=True, stop=True)
                    m.then_inc(c_s, 1)
                fill(8)
                for g in range(NSA_G):
                    pe.wait_ge(c_p, 2 * r + g + 1)
                    for b in range(TB):
                        m = nc.tensor.transpose(W[2 + g][0:N_CMP, b * P:(b + 1) * P], lc[:, g, b, :], ident)
                    m.then_inc(c_t, 1)
                n0 = N4 + 4 * r
                scores(n0, 0, qs[0], kT[0][0])
                scores(n0, 1, qs[0], kT[0][0])
                for g in range(NSA_G):
                    pe.wait_ge(c_pt, 2 * r + g + 1)
                    nc.tensor.matmul(PB[2 + g][:], vc[:, g, :], PTc[:, g, :], start=True, stop=False).then_inc(c_o, 1)
                seq = [(g, br) for g in range(NSA_G) for br in range(2)]
                for i, (g, br) in enumerate(seq):
                    nxt = seq[i + 1] if i < 3 else None
                    attend_pe(pe, n0 + i, kT[br][g], qs[g], vt[br][g], lg, PT, PB[2 + g], False, br == 1, fill,
                              ((2, 1, 0, 0), (2, 2, 2, 1), (2, 2, 2, 1), (2, 2, 2, KT))[i],
                              None if nxt is None else (qs[nxt[0]], kT[nxt[1]][nxt[0]]))

            mixed = {mix_hi: 0, mix_lo: 0}

            def mix_step(split, engine):
                if mixed[split] < len(MIX_EARLY):
                    split(engine, mixed[split])
                    mixed[split] += 1

            def nsa_act(act, r, last):
                left = [0 if last else 8]

                def sp_hi(k):
                    k = min(k, left[0])
                    left[0] -= k
                    split_hi(act, k)

                for g in range(NSA_G):
                    for b in range(TB):
                        act.wait_ge(c_m, 2 * r + g + 1)
                        ins = nc.scalar.activation(lc[:, g, b, :], lc[:, g, b, :], ACT.Exp, bias=nmc[:, g, b:b + 1],
                                                   accum_out=denc[:, g, b:b + 1])
                        if b == TB - 1:
                            ins.then_inc(c_e, 1)
                        else:
                            astep(ins)
                sp_hi(1)
                for g in range(NSA_G):
                    act.wait_ge(c_t, 2 * r + g + 1)
                    nc.scalar.activation(PTc[:, g, :], W[2 + g][0:N_CMP, :], ACT.Copy).then_inc(c_pt, 1)
                for i in range(4):
                    attend_act(act, N4 + 4 * r + i, lg, nm, den, PT, i == 0,
                               (lambda k: mix_step(mix_hi, act)) if last and i else lambda k: None)
                    sp_hi(2)
                sp_hi(8)
                if last:
                    for _ in range(TB):
                        mix_step(mix_hi, act)

            def take_q(dve, r):
                for g in range(NSA_G):
                    dve.wait_ge(q_used, Q_HEAD + 8 * r - 4 * (1 - g))
                    nc.vector.tensor_scalar(qs[g][:], PB[g][:], SCALE, None, ALU.mult).then_inc(q_ev, 1)
                    c0 = 3 * (NSA_R * g + r)
                    src = gate[:, c0:c0 + 3, :] if isinstance(c0, int) else gate[:, bass.ds(c0, 3), :]
                    step(nc.vector.tensor_copy(gs[:, 3 * g:3 * g + 3, :], src))
                settle(dve)

            def nsa_dve(dve, r, last):
                left = [0 if last else 8]

                def sp_lo(k):
                    k = min(k, left[0])
                    left[0] -= k
                    split_lo(dve, k)

                def bias_of(g):
                    hd = NSA_R * g + r

                    def bias(a, e, s=1):
                        if isinstance(hd, int):
                            return tab[:, hd, a:e:s]
                        return tab[:, bass.ds(hd, 1), a:e:s].rearrange("p a n -> p (a n)")
                    return bias

                for g in range(NSA_G):
                    dve.wait_ge(c_s, 2 * r + g + 1)
                    for b in range(TB):
                        a = TW_DIL - P - P * b + CMP_LEN - 1
                        ins = nc.vector.tensor_tensor(lc[:, g, b, :], W[g][:, b * N_CMP:(b + 1) * N_CMP],
                                                      bias_of(g)(a, a + CMP_STRIDE * (N_CMP - 1) + 1, CMP_STRIDE), ALU.add)
                        step(ins)
                    settle(dve)
                    link(dve, nc.vector.tensor_reduce(nmc[:, g, :], lc[:, g], AX.X, ALU.max, negate=True))
                    nc.vector.tensor_scalar(nmc[:, g, :], nmc[:, g, :], BIG / 10, None, ALU.min).then_inc(c_m, 1)
                sp_lo(1)
                for g in range(NSA_G):
                    dve.wait_ge(c_e, 2 * r + g + 1)
                    link(dve, nc.vector.tensor_scalar(denc[:, g, :], denc[:, g, :], 1e-30, None, ALU.max))
                    link(dve, nc.vector.reciprocal(denc[:, g, :], denc[:, g, :]))
                    link(dve, nc.vector.tensor_tensor(denc[:, g, :], denc[:, g, :], gs[:, 3 * g, :], ALU.mult))
                    nc.vector.tensor_tensor(lc[:, g], lc[:, g], bc(denc[:, g, :], N_CMP), ALU.mult).then_inc(c_p, 1)
                for i in range(4):
                    g, br = i // 2, i % 2
                    attend_dve(dve, N4 + 4 * r + i, lg, nm, den, bias_of(g), gs[:, 3 * g + 1 + br, :], i == 0,
                               (lambda k: mix_step(mix_lo, dve)) if last and i else lambda k: None)
                    sp_lo(2)
                sp_lo(8)
                if last:
                    for _ in range(TB):
                        mix_step(mix_lo, dve)
                else:
                    dve.wait_ge(att_p, 4 * (N4 + 4 * (r + 1)))
                    take_q(dve, r + 1)
                dve.wait_ge(stored, 16 * (DN_H + DIL_H) + STORED2 + 32 * r)
                for g in range(NSA_G):
                    dve.wait_ge(att_o, N4 + 4 * r + 2 * g + 2)
                    nc.vector.tensor_copy(ob[g][:], PB[2 + g][:]).then_inc(o_v4, 1)
                dve.wait_ge(o_v4, 2 * r + 2)

            @block.sync
            def _(sp):
                sp.dma_start(pos[:], t["cmp_pos"]).then_inc(par4, 16)
                sp.dma_start(w2[:], t["cmp_w2"]).then_inc(par4, 16)
                load_units(sp, (Q_HEAD + AHEAD + 3) // 4)
                sp.wait_ge(q_used, Q_CMP + 2 * W1Q)
                sp.dma_start(tab[:], toep_d[DIL_H:, :, :].rearrange("h p c -> p h c")).then_inc(table_in, 16)
                for r in range(NSA_R):
                    load_units(sp, (Q_HEAD + 8 * min(r + 1, NSA_R - 1) + AHEAD + 3) // 4)
                    if r == NSA_R - 1:
                        sp.wait_ge(q_used, Q_HEAD + 8 * r)
                        sp.wait_ge(stored, 16 * (DN_H + DIL_H + NSA_G * r) + STORED2)
                        load_mix(sp, range(0, DN_H + DIL_H), m_in[0])
                        for g in range(NSA_G):
                            a = DN_H + DIL_H + NSA_R * g
                            load_mix(sp, range(a, a + NSA_R - 1), m_in[1])
                    for g in range(NSA_G):
                        sp.wait_ge(o_v4, 2 * r + g + 1)
                        sp.dma_start(mix_d[DN_H + DIL_H + NSA_R * g + r, :, :], ob[g][:]).then_inc(stored, 16)
            @block.tensor
            def _(pe):
                def turn_v(i):
                    pe.wait_ge(kv_ev, V_UNITS[i] + 1)
                    for b in range(TB):
                        m = nc.tensor.transpose(W[i][:, b * P:(b + 1) * P], qs[i % 2][:, b * P:(b + 1) * P], ident)
                    m.then_inc(kv_tr, 1)

                for u in range(3, UNITS):
                    if u > 3:
                        pe.wait_ge(kv_ev, u - 3)
                    for kt in range(KT):
                        project(pe, u % 4, kt)
                    if u - 1 in V_UNITS:
                        turn_v(V_UNITS.index(u - 1))
                for i in range(2):
                    pe.wait_ge(cb_l, i + 1)
                    pe.wait_ge(kv_ev, UNITS - 1 + i)
                    for q in range(W1Q):
                        s = pe_q.n % RING
                        pe.wait_ge(lo_done, pe_q.at(1))
                        for ll in range(2):
                            l = 2 * q + ll
                            for n, (a, b) in enumerate(((cb_hi[i], w_hi), (cb_lo[i], w_hi), (cb_hi[i], w_lo))):
                                m = nc.tensor.matmul(PB[2 + i][0:NC2, 0:CMP_HID], a[:, l, :],
                                                     b[:, s, ll * CMP_HID:(ll + 1) * CMP_HID],
                                                     start=(l == 0 and n == 0), stop=(l == CMP_LEN - 1 and n == 2))
                        m.then_inc(q_used, 1)
                        pe_q.n += 1
                    if i == 0:
                        turn_v(3)
                fill = filler(pe, 2)
                for i in range(2):
                    pe.wait_ge(cm_a, i + 1)
                    if i == 0:
                        pe.wait_ge(kv_vt, 4)
                    for hh in range(2):
                        m = nc.tensor.transpose(W[0][:, hh * NC2:(hh + 1) * NC2], hm[i][:, hh * P:(hh + 1) * P],
                                                cst[0:NC2, K_ID, 0:NC2])
                    m.then_inc(cm_tr, 1)
                    fill(8)
                    pe.wait_ge(cm_t, i + 1)
                    if i == 0:
                        for hh in range(2):
                            m = nc.tensor.matmul(W[1][:, 0:NC2], w2[:, 0, hh, :], hmT[:, hh, :],
                                                 start=(hh == 0), stop=(hh == 1))
                        m.then_inc(cm_k, 1)
                        fill(8)
                    else:
                        for g in range(NSA_G):
                            for hh in range(2):
                                m = nc.tensor.matmul(W[2 + g][0:N_CMP, 0:HD], hmT[:, hh, g * N_CMP:(g + 1) * N_CMP],
                                                     w2[:, 1, hh, :], start=(hh == 0), stop=(hh == 1))
                            m.then_inc(cm_k, 1)
                fill(1000)
                pe.wait_ge(cm_kv, 3)
                with repeat(pe, NSA_R - 1, (pe_q, 8, "nsa_pe quarters")) as r:
                    nsa_pe(pe, r, False)
                nsa_pe(pe, NSA_R - 1, True)

            KV_DST = [lg[:, 0], lg[:, 2], lg[:, 1], lg[:, 3], kT[0][0][:], qs[0][:], kT[0][1][:], qs[1][:],
                      kT[1][0][:], qs[0][:], kT[1][1][:], qs[1][:]]

            @block.scalar
            def _(act):
                for u in range(UNITS):
                    act.wait_ge(q_used, Q4 - 12 + 4 * (u + 1))
                    if u in V_UNITS[2:]:
                        act.wait_ge(kv_tr, V_UNITS.index(u) - 1)
                    nc.scalar.activation(KV_DST[u], PB[u % 4][:], ACT.Copy).then_inc(kv_ev, 1)
                    if u >= 2 and u < UNITS - 1:
                        split_hi(act, 4)
                    if u in BLOCKS_AT:
                        i = BLOCKS_AT.index(u)
                        act.wait_ge(cb_v, i + 1)
                        nc.scalar.activation(cb_hi[i], cb, ACT.Copy).then_inc(cb_a, 1)
                for i in range(2):
                    split_hi(act, W1Q)
                    act.wait_ge(q_used, Q_CMP + W1Q * (i + 1))
                    nc.scalar.activation(hm[i][:], PB[2 + i][0:NC2, 0:CMP_HID], ACT.Gelu_apprx_tanh).then_inc(cm_a, 1)
                split_hi(act, 8)
                with repeat(act, NSA_R - 1, (act_q, 8, "nsa_act quarters"), (act_c, TICKS["nsa_act"], "nsa_act")) as r:
                    nsa_act(act, r, False)
                nsa_act(act, NSA_R - 1, True)

            @block.vector
            def _(dve):
                dve.wait_ge(par4, 32)
                def take_v(i):
                    dve.wait_ge(kv_tr, i + 1)
                    nc.vector.tensor_copy(vt[i // 2][i % 2][:].rearrange("p b n -> p (b n)"), W[i][:]).then_inc(kv_vt, 1)

                def blocks(i):
                    for g in range(NSA_G):
                        for a in range(2):
                            src = lg[:, 2 * i + g, CMP_STRIDE * a:CMP_STRIDE * (a + N_CMP)]\
                                .rearrange("p (c l) -> p c l", l=CMP_STRIDE)
                            dst = cb[:, CMP_STRIDE * a:CMP_STRIDE * (a + 1), g * N_CMP:(g + 1) * N_CMP]\
                                .rearrange("p l c -> p c l")
                            pp = pos[:, i, None, CMP_STRIDE * a:CMP_STRIDE * (a + 1)].to_broadcast([P, N_CMP, CMP_STRIDE])
                            ins = nc.vector.tensor_tensor(dst, src, pp, ALU.add)
                            if g == 1 and a == 1:
                                ins.then_inc(cb_v, 1)
                            else:
                                step(ins)

                def blocks_lo(i):
                    dve.wait_ge(cb_a, i + 1)
                    nc.vector.tensor_tensor(cb_lo[i], cb, cb_hi[i].bitcast(F32), ALU.subtract).then_inc(cb_l, 1)
                    dve.wait_ge(cb_l, i + 1)

                for u in range(UNITS):
                    dve.wait_ge(kv_ev, u + 1)
                    if u >= 2 and u < UNITS - 1:
                        split_lo(dve, 4)
                    if u in BLOCKS_AT:
                        i = BLOCKS_AT.index(u)
                        settle(dve)
                        blocks(i)
                        blocks_lo(i)
                    if u in (7, 9, 11):
                        take_v((u - 7) // 2)
                split_lo(dve, W1Q)
                take_v(3)
                split_lo(dve, W1Q)

                def mid(i):
                    dve.wait_ge(cm_tr, i + 1)
                    nc.vector.tensor_copy(hmT[:].rearrange("p h c -> p (h c)"), W[0][:, 0:2 * NC2]).then_inc(cm_t, 1)

                mid(0)
                split_lo(dve, 2)
                dve.wait_ge(cm_k, 1)
                nc.vector.tensor_copy(kc[:], W[1][:, 0:NC2]).then_inc(cm_kv, 1)
                split_lo(dve, 2)
                mid(1)
                split_lo(dve, 4)
                for g in range(NSA_G):
                    dve.wait_ge(cm_k, 2 + g)
                    nc.vector.tensor_copy(vc[:, g, :], W[2 + g][0:N_CMP, 0:HD]).then_inc(cm_kv, 1)
                dve.wait_ge(table_in, 16 * len(PIECES) + 32)
                take_q(dve, 0)
                with repeat(dve, NSA_R - 1, (dve_q, 8, "nsa_dve quarters"), (dve_c, TICKS["nsa_dve"], "nsa_dve")) as r:
                    nsa_dve(dve, r, False)
                nsa_dve(dve, NSA_R - 1, True)

        CG = D_MODEL // QW
        c5 = ctx.enter_context(ExitStack())
        xs = sb(c5, "xs", [P, TB, D_MODEL])
        xr_in, bank_free, wo_ps = (sem(n) for n in ("xr_in", "bank_free", "wo_ps"))
        Q5 = Q_HEAD + 8 * (NSA_R - 1)
        N2_DONE = D_MODEL - QW
        rest = sb(c5, "n2_rest", [P, TB])
        rest_a = sem("n2_rest_a")
        g2_row, g2_in = sb(c5, "gain_row", [P, D_MODEL]), sem("n2_g_in")
        with ExitStack() as c6, nc.Block() as block:
            sq5 = sb(c6, "wo_squares", [P, N2_DONE])

            @block.sync
            def _(sp):
                sp.wait_ge(stored, 16 * KT + STORED2)
                for kt in MIX_LATE:
                    load_mix(sp, [kt], m_in[2])
                load_unit(sp)
                sp.dma_start(xs[:], t["x"].rearrange("(b p) d -> p b d", p=P)).then_inc(xr_in, 16)
                load_unit(sp)
                sp.dma_start(g2_row[:], t["g2"]).then_inc(g2_in, 16)
                load_units(sp, (Q5 + 16 * CG + AHEAD + 3) // 4)

            @block.tensor
            def _(pe):
                with repeat(pe, CG // 2, (pe_q, 32, "wo_pe quarters")) as i:
                    for c in range(2):
                        for kt in range(KT):
                            s = pe_q.n % RING
                            pe.wait_ge(lo_done, pe_q.at(1))
                            pe.wait_ge(m_lo, len(MIX_EARLY) if kt < MIX_LATE[0] else KT)
                            for b in range(TB):
                                if kt == 0:
                                    pe.wait_ge(bank_free, 8 * i + 4 * c + b + 1)
                                for n, (x, w) in enumerate(((h_hi, w_hi), (h_lo, w_hi), (h_hi, w_lo))):
                                    m = nc.tensor.matmul(bank[4 * c + b][:], x[:, kt, b * P:(b + 1) * P], w[:, s, :],
                                                         start=(kt == 0 and n == 0), stop=(kt == KT - 1 and n == 2))
                                if kt == KT - 1 and b < TB - 1:
                                    m.then_inc(wo_ps, 1)
                            m.then_inc(q_used, 1)
                            pe_q.n += 1

            @block.scalar
            def _(act):
                for i in range(len(MIX_EARLY), KT):
                    mix_hi(act, i)
                with repeat(act, CG // 2, (act_q, 32, "wo_act quarters")) as i:
                    split_hi(act, 32)
                act.wait_ge(bank_free, 8 + 4 * (CG - 1))
                for b in range(TB):
                    if b:
                        act.wait_ge(rest_a, b)
                    nc.scalar.activation(sq5[:], xs[:, b, 0:N2_DONE], ACT.Square, accum_out=rest[:, b:b + 1])\
                        .then_inc(rest_a, 1)

            @block.vector
            def _(dve):
                dve.sem_inc(bank_free, 8)
                for i in range(len(MIX_EARLY), KT):
                    mix_lo(dve, i)
                with repeat(dve, CG // 2, (dve_q, 32, "wo_dve quarters")) as i:
                    for c in range(2):
                        split_lo(dve, KT)
                        dve.wait_ge(xr_in, 16)
                        for b in range(TB):
                            if b < TB - 1:
                                dve.wait_ge(wo_ps, 6 * i + 3 * c + b + 1)
                            else:
                                dve.wait_ge(q_used, Q5 + 32 * i + 16 * (c + 1))
                            dst = xs[:, b, bass.ds(i * 2 * QW + c * QW, QW)]
                            nc.vector.tensor_tensor(dst, dst, bank[4 * c + b][:], ALU.add).then_inc(bank_free, 1)
                dve.wait_ge(rest_a, TB)
                link(dve, nc.vector.tensor_scalar(rest[:], rest[:], 1.0 / D_MODEL, EPS, ALU.mult, ALU.add))
                dve.wait_ge(bank_free, 8 + 4 * CG)

        with ExitStack() as c6, nc.Block() as block:
            n2_act, n2_dve, n2_pe, _, _ = normalize("n2", lambda e, b: None, g2_row, g2_in, xs, c6, ident, N2_DONE, rest)

            @block.scalar
            def _(act):
                n2_act(act)

            @block.vector
            def _(dve):
                n2_dve(dve)

            @block.tensor
            def _(pe):
                n2_pe(pe)

        Q7 = Q5 + 16 * CG
        GQ = 8 * GT + 4 * CG
        with ExitStack() as c7, nc.Block() as block:
            g_hi = sb(c7, "g_hi", [P, 2, GT, SEQ], F32R)
            g_lo = sb(c7, "g_lo", [P, 2, GT, SEQ], F32R)
            cg, cv, gf = (sb(c7, f"ffn_{n}", [P, SEQ]) for n in ("gate", "val", "prod"))
            fw = sb(c7, "ffn_w", [P, 2, 3, FT])
            fwg = sb(c7, "ffn_wg", [P, 2, 3, GT])
            fwd = sb(c7, "ffn_wd", [P, 2, 3, GT])
            fg, squares = g2_row, sb(c7, "fin_squares", [P, QW])
            ss, rs = sb(c7, "fin_ss", [P, TB, CG]), sb(c7, "fin_rs", [P, TB])
            (par7, up_free, tap_a, silu7, prod_v, gh_a, gl_v, dn_free, dn_ps, taps_v) = (
                sem(f"ffn_{n}") for n in "par up_free tap silu prod g_hi g_lo down_free down_ps taps".split())
            (fin_sq, fin_g, fin_sum, fin_rms, fin_rs, fin_a, fin_v, out_s) = (
                sem(f"fin_{n}") for n in "squares gain sum rms rs act dve out".split())
            FIN_A = D_MODEL // 2

            def up_pe(pe, g, slot):
                for j in range(GT):
                    for v in range(2):
                        bk = 2 * (j % 2) + v
                        pe.wait_ge(up_free, 8 * g + 2 * j + v + 1)
                        for kt in range(KT):
                            project(pe, bk, kt)

            def down_pe(pe, g, slot):
                for c in range(CG):
                    for kt in range(GT):
                        s = pe_q.n % RING
                        pe.wait_ge(lo_done, pe_q.at(1))
                        if c == 0:
                            pe.wait_ge(gl_v, 4 * g + kt + 1)
                        for b in range(TB):
                            if kt == 0:
                                pe.wait_ge(dn_free, 16 * g + 4 * c + b + 1)
                            for n, (x, w) in enumerate(((g_hi, w_hi), (g_lo, w_hi), (g_hi, w_lo))):
                                m = nc.tensor.matmul(W[b][:], x[:, slot, kt, b * P:(b + 1) * P], w[:, s, :],
                                                     start=(kt == 0 and n == 0), stop=(kt == GT - 1 and n == 2))
                            if kt == GT - 1 and b < TB - 1:
                                m.then_inc(dn_ps, 1)
                        m.then_inc(q_used, 1)
                        pe_q.n += 1

            def up_act(act, g, slot, q_start):
                for j in range(GT):
                    split_hi(act, 8)
                    for v, dst in ((0, cg), (1, cv)):
                        act.wait_ge(q_used, q_start + 8 * j + 4 * v + 4)
                        if v == 0 and j == 0:
                            act.wait_ge(taps_v, g + 1)
                        if v == 0:
                            act.wait_ge(prod_v, 4 * g + j)
                        nc.scalar.activation(dst[:], PB[2 * (j % 2) + v][:], ACT.Copy, scale=fwg[:, v, 2, j:j + 1])\
                            .then_inc(tap_a, 1)
                    act.wait_ge(up_free, 4 + 8 * g + 2 * j + 1)
                    nc.scalar.activation(cg[:], cg[:], ACT.Silu).then_inc(silu7, 1)
                    act.wait_ge(prod_v, 4 * g + j + 1)
                    nc.scalar.activation(g_hi[:, slot, j, :], gf[:], ACT.Copy).then_inc(gh_a, 1)

            def up_dve(dve, g, slot):
                g4 = g * GT
                for v in range(2):
                    for k in range(3):
                        src = fw[:, v, k, g4:g4 + GT] if isinstance(g, int) else \
                            fw[:, v, k, bass.ds(g4, GT)]
                        ins = nc.vector.tensor_copy(fwg[:, v, k, :], src)
                        if v == 1 and k == 2:
                            ins.then_inc(taps_v, 1)
                        else:
                            step(ins)
                dve.wait_ge(taps_v, g + 1)
                for j in range(GT):
                    split_lo(dve, 8)
                    for v, dst in ((0, cg), (1, cv)):
                        dve.wait_ge(tap_a, 8 * g + 2 * j + v + 1)
                        bk = PB[2 * (j % 2) + v]
                        link(dve, nc.vector.scalar_tensor_tensor(dst[:, 1:SEQ], bk[:, 0:SEQ - 1], fwg[:, v, 1, j:j + 1],
                                                                 dst[:, 1:SEQ], ALU.mult, ALU.add))
                        nc.vector.scalar_tensor_tensor(dst[:, 2:SEQ], bk[:, 0:SEQ - 2], fwg[:, v, 0, j:j + 1],
                                                       dst[:, 2:SEQ], ALU.mult, ALU.add).then_inc(up_free, 1)
                        dve.wait_ge(up_free, 4 + 8 * g + 2 * j + v + 1)
                    dve.wait_ge(silu7, 4 * g + j + 1)
                    dve.wait_ge(gl_v, 4 * g + j)
                    nc.vector.tensor_tensor(gf[:], cg[:], cv[:], ALU.mult).then_inc(prod_v, 1)
                    dve.wait_ge(gh_a, 4 * g + j + 1)
                    nc.vector.tensor_tensor(g_lo[:, slot, j, :], gf[:], g_hi[:, slot, j, :].bitcast(F32), ALU.subtract)\
                        .then_inc(gl_v, 1)

            def down_dve(dve, g, q_start, splits=4 * CG):
                for c in range(CG):
                    split_lo(dve, max(0, min(4, splits - 4 * c)))
                    for b in range(TB):
                        if b < TB - 1:
                            dve.wait_ge(dn_ps, 12 * g + 3 * c + b + 1)
                        else:
                            dve.wait_ge(q_used, q_start + 4 * (c + 1))
                        dve.wait_ge(dn_free, 4 + 16 * g + 4 * c + b)
                        dst = xs[:, b, c * QW:(c + 1) * QW]
                        nc.vector.tensor_tensor(dst, dst, W[b][:], ALU.add).then_inc(dn_free, 1)

            @block.sync
            def _(sp):
                sp.dma_start(fw[:], t["ffn_conv"]).then_inc(par7, 16)
                sp.dma_start(fg[:], t["final_g"]).then_inc(par7, 16)
                load_units(sp, (Q7 + GQ * N_GROUP) // 4)
                for b in range(TB):
                    sp.wait_ge(fin_a, b + 1)
                    sp.wait_ge(fin_v, 2 * (b + 1))
                    sp.dma_start(t["out"][b * P:(b + 1) * P, :], xs[:, b, :]).then_inc(out_s, 16)
                sp.wait_ge(out_s, 16 * TB)

            @block.tensor
            def _(pe):
                up_pe(pe, 0, 0)
                with repeat(pe, N_GROUP // 2, (pe_q, 2 * GQ, "ffn_pe quarters")) as i:
                    up_pe(pe, 2 * i + 1, 1)
                    down_pe(pe, 2 * i, 0)
                    up_pe(pe, 2 * i + 2, 0)
                    down_pe(pe, 2 * i + 1, 1)
                down_pe(pe, N_GROUP - 1, 0)

            UPQ, DNQ = 8 * GT, 4 * CG

            @block.scalar
            def _(act):
                act.wait_ge(par7, 32)
                up_act(act, 0, 0, Q7)
                with repeat(act, N_GROUP // 2, (act_q, 2 * GQ, "ffn_act quarters")) as i:
                    q0 = Q7 + UPQ + 2 * GQ * i
                    up_act(act, 2 * i + 1, 1, q0)
                    split_hi(act, DNQ)
                    up_act(act, 2 * i + 2, 0, q0 + GQ)
                    split_hi(act, DNQ)
                split_hi(act, DNQ - AHEAD)
                for c in range(CG):
                    for b in range(TB):
                        act.wait_ge(dn_free, 4 + 16 * (N_GROUP - 1) + 4 * c + b + 1)
                        if c or b:
                            act.wait_ge(fin_sq, 4 * c + b)
                        nc.scalar.activation(squares[:], xs[:, b, c * QW:(c + 1) * QW], ACT.Square,
                                             accum_out=ss[:, b, c:c + 1]).then_inc(fin_sq, 1)
                act.wait_ge(fin_sum, 1)
                nc.scalar.activation(rs[:], rs[:], ACT.Sqrt, bias=eps_t[:], scale=1.0 / D_MODEL).then_inc(fin_rms, 1)
                act.wait_ge(fin_rs, 1)
                act.wait_ge(fin_g, TB * (CG - 1))
                for b in range(TB):
                    nc.scalar.activation(xs[:, b, 0:FIN_A], xs[:, b, 0:FIN_A], ACT.Copy, scale=rs[:, b:b + 1])\
                        .then_inc(fin_a, 1)

            @block.gpsimd
            def _(pool):
                pool.wait_ge(par7, 32)
                for c in range(CG - 1):
                    for b in range(TB):
                        pool.wait_ge(fin_sq, 4 * c + b + 1)
                        cc = slice(c * QW, (c + 1) * QW)
                        nc.gpsimd.tensor_tensor(xs[:, b, cc], xs[:, b, cc], fg[:, cc], ALU.mult).then_inc(fin_g, 1)

            @block.vector
            def _(dve):
                dve.sem_inc(up_free, 4)
                dve.sem_inc(dn_free, 4)
                dve.wait_ge(par7, 32)
                up_dve(dve, 0, 0)
                with repeat(dve, N_GROUP // 2, (dve_q, 2 * GQ, "ffn_dve quarters"),
                            (dve_c, TICKS["ffn_dve"], "ffn_dve")) as i:
                    q0 = Q7 + UPQ + 2 * GQ * i
                    up_dve(dve, 2 * i + 1, 1)
                    down_dve(dve, 2 * i, q0 + UPQ)
                    up_dve(dve, 2 * i + 2, 0)
                    down_dve(dve, 2 * i + 1, q0 + GQ + UPQ)
                down_dve(dve, N_GROUP - 1, Q7 + GQ * N_GROUP - DNQ, DNQ - AHEAD)
                dve.wait_ge(fin_sq, TB * CG)
                nc.vector.tensor_reduce(rs[:], ss[:], AX.X, ALU.add).then_inc(fin_sum, 1)
                dve.wait_ge(fin_rms, 1)
                nc.vector.reciprocal(rs[:], rs[:]).then_inc(fin_rs, 1)
                dve.wait_ge(fin_rs, 1)
                dve.wait_ge(fin_g, TB * (CG - 1))
                for b in range(TB):
                    c2, c3 = slice(FIN_A, D_MODEL - QW), slice(D_MODEL - QW, D_MODEL)
                    nc.vector.tensor_scalar(xs[:, b, c2], xs[:, b, c2], rs[:, b:b + 1], None, ALU.mult).then_inc(fin_v, 1)
                    nc.vector.scalar_tensor_tensor(xs[:, b, c3], xs[:, b, c3], rs[:, b:b + 1], fg[:, c3],
                                                   ALU.mult, ALU.mult).then_inc(fin_v, 1)


def rel_bucket(dist):
    exact = BUCKETS // 2
    n = np.maximum(dist, 0)
    nf = np.maximum(n, 1).astype(np.float32)
    large = exact + (np.log(nf / np.float32(exact)) / np.float32(math.log(REL_MAX / exact))
                     * np.float32(BUCKETS - exact)).astype(np.int32)
    return np.where(n < exact, n, np.minimum(large, BUCKETS - 1))


def constant_tiles():
    i, j = np.arange(P)[:, None], np.arange(P)[None, :]
    same = i // CHUNK == j // CHUNK

    def level(b):
        return (i // (2 * b) == j // (2 * b)) & ((i // b) % 2 == 1) & ((j // b) % 2 == 0)

    out = np.zeros((P, N_CST, P), np.float32)
    out[:, K_ID] = i == j
    out[:, K_ONE] = 1
    out[:, K_TRI] = same & (i <= j)
    out[:, K_BLK] = same
    out[:, K_ML] = np.where(same & (i > j), 0, BIG)
    out[:, K_MU] = np.where(same & (i <= j), 0, -BIG)
    out[:, K_M1] = level(1)
    out[:, K_REV] = i + j == P - 1
    out[:, K_M1T] = level(1).T
    for n, b in enumerate(LEVELS):
        out[:, K_LV + n] = level(b).T
    return out


def bias_columns():
    d = TW_DIL - 1 - np.arange(YLEN)
    out = np.zeros((BUCKETS + 2, YLEN), np.float32)
    out[rel_bucket(d), np.arange(YLEN)] = d >= 0
    count = (d <= 128).astype(int) + (d % 4 == 0) + (d % 16 == 0)
    ok = (d >= 0) & (count > 0)
    out[BUCKETS] = np.where(ok, np.log(np.where(ok, count, 1)), -BIG)
    out[BUCKETS + 1] = np.where(d >= 0, 0, -BIG)
    return out


def stream(w_in, cmp_w1, w_out, ffn_up, ffn_down):
    units = []

    def columns(w, c):
        units.append(w[:, c:c + P].reshape(KT, P, P).transpose(1, 0, 2).reshape(P, -1))

    def rows(w, r, c):
        units.append(w[r:r + 4 * P, c:c + QW].reshape(4, P, QW).transpose(1, 0, 2).reshape(P, -1))

    dn_w, dil_w = DN_H * HD, DIL_H * HD
    dil0 = 4 * dn_w + 2 * DN_H
    q0 = dil0 + 3 * dil_w
    kv0 = q0 + NSA_H * HD
    for h in range(DN_H):
        for part in range(4):
            columns(w_in, part * dn_w + h * HD)
    for h in range(DIL_H):
        for part in range(3):
            columns(w_in, dil0 + part * dil_w + h * HD)

    def kv(br, which, g):
        columns(w_in, kv0 + ((br * 2 + which) * NSA_G + g) * HD)

    for br in range(3):
        for g in range(NSA_G):
            for which in range(2):
                kv(br, which, g)
    for i in range(2):
        w = cmp_w1[i].reshape(CMP_LEN, P, CMP_HID)
        for l in range(0, CMP_LEN, 8):
            units.append(w[l:l + 8].transpose(1, 0, 2).reshape(P, -1))
    for r in range(NSA_R):
        for g in range(NSA_G):
            columns(w_in, q0 + (g * NSA_R + r) * HD)
    for c in range(0, D_MODEL, QW):
        for r in range(0, D_MODEL, 4 * P):
            rows(w_out, r, c)

    def up(g):
        for j in range(GT):
            for v in range(2):
                columns(ffn_up, v * D_FF + (g * GT + j) * P)

    def down(g):
        for c in range(0, D_MODEL, QW):
            rows(ffn_down, g * GT * P, c)

    up(0)
    for g in range(1, N_GROUP):
        up(g)
        down(g - 1)
    down(N_GROUP - 1)
    return np.stack(units)


def kernel(x, norm1_g, w_in, dn_conv, dn_a_log, dn_dt_bias, dn_norm_g, cmp_pos, cmp_w1, cmp_w2,
           w_out, norm2_g, ffn_up, ffn_conv, ffn_down, rel_bias, final_g):
    import concourse.bacc as bacc
    from concourse.bass_utils import run_bass_kernel_spmd

    x, w = np.asarray(x)[0], np.asarray(w_in)[0]
    small = np.concatenate([w[:, 4 * DN_H * HD:4 * DN_H * HD + 2 * DN_H], w[:, -3 * NSA_H:]], axis=1)
    extra = np.zeros((2, DIL_H + NSA_H), np.float32)
    extra[0, :DIL_H] = 1
    extra[1, DIL_H:] = 1
    arrays = {
        "x": x,
        "weights": stream(w, np.asarray(cmp_w1)[0], np.asarray(w_out)[0], np.asarray(ffn_up)[0],
                          np.asarray(ffn_down)[0]),
        "w_small": small.reshape(KT, P, N_SMALL).transpose(1, 0, 2),
        "ab": np.broadcast_to(np.stack([np.asarray(dn_a_log)[0], np.asarray(dn_dt_bias)[0]])[None], (P, 2, DN_H)),
        "g1": np.broadcast_to(np.asarray(norm1_g), (P, D_MODEL)),
        "g2": np.broadcast_to(np.asarray(norm2_g), (P, D_MODEL)),
        "final_g": np.broadcast_to(np.asarray(final_g)[None], (P, D_MODEL)),
        "dn_conv": np.asarray(dn_conv)[0].reshape(4, 3, DN_H, P).transpose(3, 2, 1, 0),
        "dn_norm": np.asarray(dn_norm_g)[0].reshape(P, 1),
        "cmp_pos": np.asarray(cmp_pos)[0].transpose(2, 0, 1),
        "cmp_w2": np.asarray(cmp_w2)[0].reshape(2, 2, P, HD).transpose(2, 0, 1, 3),
        "ffn_conv": np.asarray(ffn_conv)[0].reshape(3, 2, FT, P).transpose(3, 1, 0, 2),
        "bias_lhs": np.concatenate([np.asarray(rel_bias).T, extra]),
        "cst": constant_tiles(),
        "onehot": bias_columns(),
    }
    arrays = {k: np.ascontiguousarray(a) for k, a in arrays.items()}
    nc = bacc.Bacc("TRN2", target_bir_lowering=False, num_devices=1)
    t = {k: nc.dram_tensor(f"in_{k}", a.shape, mybir.dt.from_np(a.dtype), kind="ExternalInput").ap()
         for k, a in arrays.items()}
    t["out"] = nc.dram_tensor("out", (SEQ, D_MODEL), F32, kind="ExternalOutput").ap()
    program(nc, t)
    r = run_bass_kernel_spmd(nc, [{f"in_{k}": a for k, a in arrays.items()}], core_ids=[0])
    return r.results[0]["out"].reshape(1, SEQ, D_MODEL)
```
